# Optimizing a Trainium2 kernel written in Bass

```python
import jax, jax.numpy as jnp
from jax import lax
import numpy as np

D_MODEL = 1024
BATCH = 1
SEQ = 256
DEPTH = 2

A_HEADS = 16
A_KV_HEADS = 4
A_HEAD_DIM = 64
A_REP = A_HEADS // A_KV_HEADS
IDX_HEADS = 8
IDX_DIM = 64
IDX_TOPK_MAX = 256
Q_BLOCK = 128
A_Q = A_HEADS * A_HEAD_DIM
A_KV = A_KV_HEADS * A_HEAD_DIM
A_IN = A_Q + 2 * A_KV + IDX_HEADS * IDX_DIM + IDX_DIM + IDX_HEADS
A_SPLITS = (A_Q, A_Q + A_KV, A_Q + 2 * A_KV, A_Q + 2 * A_KV + IDX_HEADS * IDX_DIM,
            A_Q + 2 * A_KV + IDX_HEADS * IDX_DIM + IDX_DIM)

B_HEADS = 4
B_DK = D_MODEL // 2 // B_HEADS
B_DV = D_MODEL // B_HEADS
B_GATE_RANK = 16
B_GATE_TAU = 16.0
B_CHUNK = 64
B_QK = B_HEADS * B_DK
B_V = B_HEADS * B_DV
B_IN = 2 * B_QK + 2 * B_V + B_GATE_RANK
B_SPLITS = (B_QK, 2 * B_QK, 2 * B_QK + B_V, 2 * B_QK + 2 * B_V)

D_FF = 4 * D_MODEL

ROPE_THETA = 500000.0
ROT_DIM = A_HEAD_DIM // 4
LN_EPS = 1e-5
RMS_EPS = 1e-6
DN_ALPHA = (2 * DEPTH) ** 0.25
DN_BETA = (8 * DEPTH) ** -0.25
N_A_LAYERS = (DEPTH + 1) // 2
N_B_LAYERS = DEPTH // 2


def layer_norm(x, g, b):
    xf = x.astype(jnp.float32)
    mu = jnp.mean(xf, axis=-1, keepdims=True)
    var = jnp.mean(jnp.square(xf - mu), axis=-1, keepdims=True)
    return ((xf - mu) * lax.rsqrt(var + LN_EPS) * g + b).astype(x.dtype)

def rotary_tables(positions):
    inv = ROPE_THETA ** (-jnp.arange(0, ROT_DIM, 2, dtype=jnp.float32) / ROT_DIM)
    ang = positions.astype(jnp.float32)[..., None] * inv
    return jnp.cos(ang), jnp.sin(ang)

def partial_rotary(t, cos, sin):
    half = cos.shape[-1]
    shape = cos.shape[:2] + (1,) * (t.ndim - 3) + (half,)
    c = cos.reshape(shape)
    s = sin.reshape(shape)
    t1 = t[..., :half].astype(jnp.float32)
    t2 = t[..., half:2 * half].astype(jnp.float32)
    return jnp.concatenate([(t1 * c - t2 * s).astype(t.dtype),
                            (t2 * c + t1 * s).astype(t.dtype),
                            t[..., 2 * half:]], axis=-1)

def dsa_mixer(x, cos, sin, w_in, w_o):
    bsz, L, _ = x.shape
    top_k = min(IDX_TOPK_MAX, L // 4)
    proj = x @ w_in
    q, k, v, iq, ik, iw = jnp.split(proj, A_SPLITS, axis=-1)
    q = partial_rotary(q.reshape(bsz, L, A_HEADS, A_HEAD_DIM), cos, sin)
    k = partial_rotary(k.reshape(bsz, L, A_KV_HEADS, A_HEAD_DIM), cos, sin)
    v = v.reshape(bsz, L, A_KV_HEADS, A_HEAD_DIM)
    iq = partial_rotary(iq.reshape(bsz, L, IDX_HEADS, IDX_DIM), cos, sin)
    ik = partial_rotary(ik, cos, sin)
    iw = iw.astype(jnp.float32) * IDX_HEADS ** -0.5
    key_idx = jnp.arange(L)

    def block(i):
        start = i * Q_BLOCK
        q_idx = start + jnp.arange(Q_BLOCK)
        iq_b = lax.dynamic_slice_in_dim(iq, start, Q_BLOCK, axis=1)
        iw_b = lax.dynamic_slice_in_dim(iw, start, Q_BLOCK, axis=1)
        s = jnp.einsum('bqhd,bsd->bqhs', iq_b, ik, preferred_element_type=jnp.float32) * IDX_DIM ** -0.5
        score = jnp.einsum('bqh,bqhs->bqs', iw_b, jax.nn.relu(s))
        causal = key_idx[None, :] <= q_idx[:, None]
        score = jnp.where(causal[None], score, -jnp.inf)
        _, sel = lax.top_k(score, top_k)
        valid = sel <= q_idx[None, :, None]
        k_sel = jax.vmap(lambda kk, ii: kk[ii])(k, sel)
        v_sel = jax.vmap(lambda vv, ii: vv[ii])(v, sel)
        q_b = lax.dynamic_slice_in_dim(q, start, Q_BLOCK, axis=1).reshape(bsz, Q_BLOCK, A_KV_HEADS, A_REP, A_HEAD_DIM)
        logits = jnp.einsum('bqgrd,bqkgd->bqgrk', q_b, k_sel, preferred_element_type=jnp.float32) * A_HEAD_DIM ** -0.5
        logits = jnp.where(valid[:, :, None, None, :], logits, -jnp.inf)
        p = jax.nn.softmax(logits, axis=-1)
        o = jnp.einsum('bqgrk,bqkgd->bqgrd', p.astype(v.dtype), v_sel)
        return o.reshape(bsz, Q_BLOCK, A_Q)

    out = lax.map(block, jnp.arange(L // Q_BLOCK))
    out = out.transpose(1, 0, 2, 3).reshape(bsz, L, A_Q)
    return out @ w_o

def gla_mixer(x, w_in, w_a2, b_a, g_norm, w_o):
    bsz, L, _ = x.shape
    n_c = L // B_CHUNK
    proj = x @ w_in
    q, k, v, r, a_low = jnp.split(proj, B_SPLITS, axis=-1)
    log_a = jax.nn.log_sigmoid((a_low @ w_a2 + b_a).astype(jnp.float32)) / B_GATE_TAU

    def to_chunks(t, d):
        return t.astype(jnp.float32).reshape(bsz, n_c, B_CHUNK, B_HEADS, d).transpose(1, 0, 3, 2, 4)

    qc = to_chunks(q, B_DK) * B_DK ** -0.5
    kc = to_chunks(k, B_DK)
    vc = to_chunks(v, B_DV)
    gc = to_chunks(log_a, B_DK)
    mask = jnp.tril(jnp.ones((B_CHUNK, B_CHUNK), dtype=bool))

    def step(state, inp):
        qi, ki, vi, gi = inp
        b = jnp.cumsum(gi, axis=2)
        b_last = b[:, :, -1:, :]
        diff = jnp.where(mask[None, None, :, :, None], b[:, :, :, None, :] - b[:, :, None, :, :], -jnp.inf)
        attn = jnp.einsum('bhid,bhjd,bhijd->bhij', qi, ki, jnp.exp(diff))
        intra = jnp.einsum('bhij,bhje->bhie', attn, vi)
        inter = jnp.einsum('bhid,bhde->bhie', qi * jnp.exp(b), state)
        new_state = jnp.exp(b_last)[:, :, 0, :, None] * state + jnp.einsum('bhjd,bhje->bhde', ki * jnp.exp(b_last - b), vi)
        return new_state, intra + inter

    state0 = jnp.zeros((bsz, B_HEADS, B_DK, B_DV), jnp.float32)
    _, outs = lax.scan(step, state0, (qc, kc, vc, gc))
    o = outs.transpose(1, 0, 3, 2, 4).reshape(bsz, L, B_HEADS, B_DV)
    o = o * lax.rsqrt(jnp.mean(jnp.square(o), axis=-1, keepdims=True) + RMS_EPS) * g_norm
    gate = jax.nn.silu(r.astype(jnp.float32).reshape(bsz, L, B_HEADS, B_DV))
    y = (o * gate).reshape(bsz, L, B_V).astype(x.dtype)
    return y @ w_o

def squared_relu_mlp(x, w_up, w_down):
    return jnp.square(jax.nn.relu(x @ w_up)) @ w_down

def first_inputs(seed: int = 0) -> dict:
    key = jax.random.key(seed)
    ks = jax.random.split(key, 16)
    f32 = jnp.float32

    def nrm(k, shape, fan_in, scale=1.0):
        return jax.random.normal(k, shape, f32) * (scale * fan_in ** -0.5)

    x = jax.random.normal(ks[0], (BATCH, SEQ, D_MODEL), f32)
    positions = jnp.broadcast_to(jnp.arange(SEQ, dtype=jnp.int32), (BATCH, SEQ))
    a_w_in = nrm(ks[1], (N_A_LAYERS, D_MODEL, A_IN), D_MODEL)
    a_w_o = nrm(ks[2], (N_A_LAYERS, A_Q, D_MODEL), A_Q, DN_BETA)
    b_w_in = nrm(ks[3], (N_B_LAYERS, D_MODEL, B_IN), D_MODEL)
    b_w_a2 = nrm(ks[4], (N_B_LAYERS, B_GATE_RANK, B_QK), B_GATE_RANK)
    b_b_a = 0.1 * jax.random.normal(ks[5], (N_B_LAYERS, B_QK), f32)
    b_g_norm = 1.0 + 0.02 * jax.random.normal(ks[6], (N_B_LAYERS, B_DV), f32)
    b_w_o = nrm(ks[7], (N_B_LAYERS, B_V, D_MODEL), B_V, DN_BETA)
    ln_mix_g = 1.0 + 0.02 * jax.random.normal(ks[8], (DEPTH, D_MODEL), f32)
    ln_mix_b = 0.02 * jax.random.normal(ks[9], (DEPTH, D_MODEL), f32)
    mlp_w_up = nrm(ks[10], (DEPTH, D_MODEL, D_FF), D_MODEL)
    mlp_w_down = nrm(ks[11], (DEPTH, D_FF, D_MODEL), D_FF, DN_BETA)
    ln_mlp_g = 1.0 + 0.02 * jax.random.normal(ks[12], (DEPTH, D_MODEL), f32)
    ln_mlp_b = 0.02 * jax.random.normal(ks[13], (DEPTH, D_MODEL), f32)
    return {'x': x, 'positions': positions, 'a_w_in': a_w_in, 'a_w_o': a_w_o,
            'b_w_in': b_w_in, 'b_w_a2': b_w_a2, 'b_b_a': b_b_a, 'b_g_norm': b_g_norm, 'b_w_o': b_w_o,
            'ln_mix_g': ln_mix_g, 'ln_mix_b': ln_mix_b, 'mlp_w_up': mlp_w_up, 'mlp_w_down': mlp_w_down,
            'ln_mlp_g': ln_mlp_g, 'ln_mlp_b': ln_mlp_b}

def first_block(x, positions, a_w_in, a_w_o, b_w_in, b_w_a2, b_b_a, b_g_norm, b_w_o,
              ln_mix_g, ln_mix_b, mlp_w_up, mlp_w_down, ln_mlp_g, ln_mlp_b):
    cos, sin = rotary_tables(positions)
    h = x
    for i in range(DEPTH):
        j = i // 2
        if i % 2 == 0:
            mix = dsa_mixer(h, cos, sin, a_w_in[j], a_w_o[j])
        else:
            mix = gla_mixer(h, b_w_in[j], b_w_a2[j], b_b_a[j], b_g_norm[j], b_w_o[j])
        h = layer_norm(DN_ALPHA * h + mix, ln_mix_g[i], ln_mix_b[i])
        h = layer_norm(DN_ALPHA * h + squared_relu_mlp(h, mlp_w_up[i], mlp_w_down[i]), ln_mlp_g[i], ln_mlp_b[i])
    return h


N_MIXERS = 2
MLA_HEADS = 8
MLA_Q_LORA = 256
MLA_KV_LORA = 256
MLA_NOPE = 128
MLA_ROPE = 64
MLA_V = 128
ROPE_THETA_2 = 10000.0
HGRN_HEADS = 8
HGRN_DK = D_MODEL // HGRN_HEADS
HGRN_DV = D_MODEL // HGRN_HEADS
HGRN_CHUNK = 64
D_FF_2 = ((8 * D_MODEL // 3 + 255) // 256) * 256
D_PLE = 256
DEEPNORM_ALPHA = (2 * DEPTH) ** 0.25
DEEPNORM_BETA = (8 * DEPTH) ** -0.25
N_MLA_LAYERS = (DEPTH + N_MIXERS - 1) // N_MIXERS
N_HGRN_LAYERS = DEPTH // N_MIXERS


def layer_norm_2(x, g, b):
    xf = x.astype(jnp.float32)
    mu = jnp.mean(xf, axis=-1, keepdims=True)
    var = jnp.mean(jnp.square(xf - mu), axis=-1, keepdims=True)
    y = (xf - mu) * lax.rsqrt(var + LN_EPS) * g.astype(jnp.float32) + b.astype(jnp.float32)
    return y.astype(x.dtype)

def rms_norm(x, g):
    xf = x.astype(jnp.float32)
    y = xf * lax.rsqrt(jnp.mean(jnp.square(xf), axis=-1, keepdims=True) + RMS_EPS) * g.astype(jnp.float32)
    return y.astype(x.dtype)

def rope_tables(positions):
    inv_freq = ROPE_THETA_2 ** (-jnp.arange(0, MLA_ROPE, 2, dtype=jnp.float32) / MLA_ROPE)
    ang = positions.astype(jnp.float32)[..., None] * inv_freq
    return jnp.cos(ang), jnp.sin(ang)

def apply_rope(t, cos, sin):
    half = t.shape[-1] // 2
    t1, t2 = t[..., :half], t[..., half:]
    out = jnp.concatenate([t1 * cos - t2 * sin, t2 * cos + t1 * sin], axis=-1)
    return out.astype(t.dtype)

def mla_mixer(x, cos, sin, w_dqkv, q_norm, kv_norm, w_uq, w_ukv, w_o):
    B, S, _ = x.shape
    H = MLA_HEADS
    down = x @ w_dqkv
    c_q = rms_norm(down[..., :MLA_Q_LORA], q_norm)
    c_kv = rms_norm(down[..., MLA_Q_LORA:MLA_Q_LORA + MLA_KV_LORA], kv_norm)
    k_rope = apply_rope(down[..., MLA_Q_LORA + MLA_KV_LORA:], cos, sin)
    q = (c_q @ w_uq).reshape(B, S, H, MLA_NOPE + MLA_ROPE)
    q_nope = q[..., :MLA_NOPE]
    q_rope = apply_rope(q[..., MLA_NOPE:], cos[:, :, None, :], sin[:, :, None, :])
    kv = (c_kv @ w_ukv).reshape(B, S, H, MLA_NOPE + MLA_V)
    k_nope, v = kv[..., :MLA_NOPE], kv[..., MLA_NOPE:]

    nblk = S // Q_BLOCK
    scale = (MLA_NOPE + MLA_ROPE) ** -0.5
    kpos = jnp.arange(S, dtype=jnp.int32)
    qpos = kpos.reshape(nblk, Q_BLOCK)

    def to_blocks(t):
        return jnp.moveaxis(t.reshape((B, nblk, Q_BLOCK) + t.shape[2:]), 1, 0)

    def attend(blk):
        qn, qr, qp = blk
        s = (jnp.einsum('bqhd,bkhd->bhqk', qn, k_nope)
             + jnp.einsum('bqhr,bkr->bhqk', qr, k_rope)).astype(jnp.float32) * scale
        s = jnp.where(kpos[None, None, None, :] <= qp[None, None, :, None], s, -jnp.inf)
        w = jax.nn.softmax(s, axis=-1).astype(v.dtype)
        return jnp.einsum('bhqk,bkhd->bqhd', w, v)

    o = lax.map(attend, (to_blocks(q_nope), to_blocks(q_rope), qpos))
    o = jnp.moveaxis(o, 0, 1).reshape(B, S, H * MLA_V)
    return o @ w_o

def hgrn2_mixer(x, lb, w_in, out_norm, w_o):
    B, S, _ = x.shape
    H, DK, DV, C = HGRN_HEADS, HGRN_DK, HGRN_DV, HGRN_CHUNK
    proj = x @ w_in
    q = jax.nn.silu(proj[..., :H * DK].astype(jnp.float32)).reshape(B, S, H, DK)
    f = proj[..., H * DK:2 * H * DK].astype(jnp.float32).reshape(B, S, H, DK)
    v = proj[..., 2 * H * DK:2 * H * DK + H * DV].astype(jnp.float32).reshape(B, S, H, DV)
    gate = proj[..., 2 * H * DK + H * DV:]
    lb = lb.reshape(H, DK)
    log_f = jnp.logaddexp(jnp.log(lb), jnp.log1p(-lb) + jax.nn.log_sigmoid(f))
    k = (1.0 - lb) * jax.nn.sigmoid(-f)

    n = S // C

    def to_chunks(t):
        return t.reshape(B, n, C, H, t.shape[-1]).transpose(1, 0, 3, 2, 4)

    causal = jnp.tril(jnp.ones((C, C), dtype=bool))

    def step(state, chunk):
        qc, kc, gc, vc = chunk
        G = jnp.cumsum(gc, axis=2)
        inter = jnp.einsum('bhtd,bhde->bhte', qc * jnp.exp(G), state)
        diff = G[:, :, :, None, :] - G[:, :, None, :, :]
        decay = jnp.exp(jnp.where(causal[:, :, None], diff, -jnp.inf))
        A = jnp.einsum('bhtd,bhsd,bhtsd->bhts', qc, kc, decay)
        intra = jnp.einsum('bhts,bhse->bhte', A, vc)
        G_last = G[:, :, -1:, :]
        new_state = (jnp.exp(G_last[:, :, 0, :])[..., None] * state
                     + jnp.einsum('bhsd,bhse->bhde', kc * jnp.exp(G_last - G), vc))
        return new_state, inter + intra

    s0 = jnp.zeros((B, H, DK, DV), jnp.float32)
    _, o = lax.scan(step, s0, (to_chunks(q), to_chunks(k), to_chunks(log_f), to_chunks(v)))
    o = o.transpose(1, 0, 3, 2, 4).reshape(B, S, H, DV)
    o = rms_norm(o, out_norm.reshape(H, DV))
    o = o * jax.nn.silu(gate.astype(jnp.float32)).reshape(B, S, H, DV)
    return o.reshape(B, S, H * DV).astype(x.dtype) @ w_o

def swiglu_ffn(x, w_in, w_down):
    h = x @ w_in
    g, u = h[..., :D_FF_2], h[..., D_FF_2:]
    return (jax.nn.silu(g) * u) @ w_down

def second_inputs(seed: int = 0) -> dict:
    key = jax.random.key(seed)
    ks = jax.random.split(key, 24)

    def w(k, shape, fan_in, scale=1.0):
        return jax.random.normal(k, shape, jnp.float32) * (fan_in ** -0.5) * scale

    def gain(k, shape):
        return 1.0 + 0.05 * jax.random.normal(k, shape, jnp.float32)

    def bias(k, shape):
        return 0.02 * jax.random.normal(k, shape, jnp.float32)

    NM, NH = N_MLA_LAYERS, N_HGRN_LAYERS
    return {
        'x': jax.random.normal(ks[0], (BATCH, SEQ, D_MODEL), jnp.float32),
        'p': jax.random.normal(ks[1], (DEPTH, BATCH, SEQ, D_PLE), jnp.float32),
        'positions': jnp.tile(jnp.arange(SEQ, dtype=jnp.int32)[None, :], (BATCH, 1)),
        'mla_w_dqkv': w(ks[2], (NM, D_MODEL, MLA_Q_LORA + MLA_KV_LORA + MLA_ROPE), D_MODEL),
        'mla_q_norm': gain(ks[3], (NM, MLA_Q_LORA)),
        'mla_kv_norm': gain(ks[4], (NM, MLA_KV_LORA)),
        'mla_w_uq': w(ks[5], (NM, MLA_Q_LORA, MLA_HEADS * (MLA_NOPE + MLA_ROPE)), MLA_Q_LORA),
        'mla_w_ukv': w(ks[6], (NM, MLA_KV_LORA, MLA_HEADS * (MLA_NOPE + MLA_V)), MLA_KV_LORA),
        'mla_w_o': w(ks[7], (NM, MLA_HEADS * MLA_V, D_MODEL), MLA_HEADS * MLA_V, DEEPNORM_BETA),
        'hgrn_w_in': w(ks[8], (NH, D_MODEL, 2 * HGRN_HEADS * HGRN_DK + 2 * HGRN_HEADS * HGRN_DV), D_MODEL),
        'hgrn_lb_logits': 0.1 * jax.random.normal(ks[9], (DEPTH, HGRN_HEADS * HGRN_DK), jnp.float32),
        'hgrn_out_norm': gain(ks[10], (NH, HGRN_HEADS * HGRN_DV)),
        'hgrn_w_o': w(ks[11], (NH, HGRN_HEADS * HGRN_DV, D_MODEL), HGRN_HEADS * HGRN_DV, DEEPNORM_BETA),
        'ffn_w_in': w(ks[12], (DEPTH, D_MODEL, 2 * D_FF_2), D_MODEL),
        'ffn_w_down': w(ks[13], (DEPTH, D_FF_2, D_MODEL), D_FF_2, DEEPNORM_BETA),
        'ln_mix_g': gain(ks[14], (DEPTH, D_MODEL)),
        'ln_mix_b': bias(ks[15], (DEPTH, D_MODEL)),
        'ln_ffn_g': gain(ks[16], (DEPTH, D_MODEL)),
        'ln_ffn_b': bias(ks[17], (DEPTH, D_MODEL)),
        'ple_w_proj': w(ks[18], (DEPTH, D_PLE, D_MODEL), D_PLE),
        'ple_w_gate': w(ks[19], (DEPTH, D_MODEL, D_MODEL), D_MODEL),
    }

def second_block(x, p, positions, mla_w_dqkv, mla_q_norm, mla_kv_norm, mla_w_uq, mla_w_ukv, mla_w_o,
              hgrn_w_in, hgrn_lb_logits, hgrn_out_norm, hgrn_w_o, ffn_w_in, ffn_w_down,
              ln_mix_g, ln_mix_b, ln_ffn_g, ln_ffn_b, ple_w_proj, ple_w_gate):
    cos, sin = rope_tables(positions)
    lb_soft = jax.nn.softmax(hgrn_lb_logits.astype(jnp.float32), axis=0)
    lower_bounds = jnp.cumsum(lb_soft, axis=0) - lb_soft[0:1]

    for i in range(DEPTH):
        j = i // N_MIXERS
        if i % N_MIXERS == 0:
            h = mla_mixer(x, cos, sin, mla_w_dqkv[j], mla_q_norm[j], mla_kv_norm[j],
                          mla_w_uq[j], mla_w_ukv[j], mla_w_o[j])
        else:
            h = hgrn2_mixer(x, lower_bounds[i], hgrn_w_in[j], hgrn_out_norm[j], hgrn_w_o[j])
        x = layer_norm_2(DEEPNORM_ALPHA * x + h, ln_mix_g[i], ln_mix_b[i])
        x = layer_norm_2(DEEPNORM_ALPHA * x + swiglu_ffn(x, ffn_w_in[i], ffn_w_down[i]), ln_ffn_g[i], ln_ffn_b[i])
        x = x + jax.nn.sigmoid(x @ ple_w_gate[i]) * (p[i] @ ple_w_proj[i])
    return x


def setup_inputs(seed=0):
    out = dict(first_inputs(seed))
    for name, value in second_inputs(seed + 1).items():
        if name != "x":
            out[name + "_2"] = value
    return out


def reference(
    x, positions, a_w_in, a_w_o, b_w_in, b_w_a2, b_b_a, b_g_norm, b_w_o, ln_mix_g, ln_mix_b,
    mlp_w_up, mlp_w_down, ln_mlp_g, ln_mlp_b, p_2, positions_2, mla_w_dqkv_2, mla_q_norm_2,
    mla_kv_norm_2, mla_w_uq_2, mla_w_ukv_2, mla_w_o_2, hgrn_w_in_2, hgrn_lb_logits_2,
    hgrn_out_norm_2, hgrn_w_o_2, ffn_w_in_2, ffn_w_down_2, ln_mix_g_2, ln_mix_b_2, ln_ffn_g_2,
    ln_ffn_b_2, ple_w_proj_2, ple_w_gate_2,
):
    x = first_block(
        x, positions, a_w_in, a_w_o, b_w_in, b_w_a2, b_b_a, b_g_norm, b_w_o, ln_mix_g, ln_mix_b,
        mlp_w_up, mlp_w_down, ln_mlp_g, ln_mlp_b,
    )
    return second_block(
        x, p_2, positions_2, mla_w_dqkv_2, mla_q_norm_2, mla_kv_norm_2, mla_w_uq_2, mla_w_ukv_2,
        mla_w_o_2, hgrn_w_in_2, hgrn_lb_logits_2, hgrn_out_norm_2, hgrn_w_o_2, ffn_w_in_2,
        ffn_w_down_2, ln_mix_g_2, ln_mix_b_2, ln_ffn_g_2, ln_ffn_b_2, ple_w_proj_2,
        ple_w_gate_2,
    )


_drawn_inputs = setup_inputs


def setup_inputs(seed=0):
    import zlib

    import numpy as np

    out = dict(_drawn_inputs(seed))
    spreads = {}
    factors = {'b_b_a': 7.078,
     'b_g_norm': 8.0,
     'mla_q_norm_2': 8.0,
     'mla_kv_norm_2': 8.0,
     'hgrn_lb_logits_2': 8.0,
     'hgrn_out_norm_2': 5.923}
    for name, (base, spread) in spreads.items():
        noise = np.random.default_rng([zlib.crc32(name.encode()), seed]).standard_normal(out[name].shape)
        drawn = base * np.exp(spread * noise) if base else spread * noise
        out[name] = __import__('jax').numpy.asarray(drawn.astype(out[name].dtype))
    for name, factor in factors.items():
        out[name] = (out[name] * factor).astype(out[name].dtype)
    return out
```

```python
from contextlib import ExitStack

import numpy as np

import concourse.bass as bass
from concourse import mybir
from concourse.alu_op_type import AluOpType as ALU

F32 = mybir.dt.float32
F32R = mybir.dt.float32r
I32 = mybir.dt.int32
ACT = mybir.ActivationFunctionType
AX_X = mybir.AxisListType.X

P = 128
SEQ = 256
TT = SEQ // P
D = 1024
KD = D // P
DEPTH = 2
ALPHA = float((2 * DEPTH) ** 0.25)
LN_EPS = 1e-5
RMS_EPS = 1e-6
DFF = 4 * D
DFF2 = ((8 * D // 3 + 255) // 256) * 256
D_PLE = 256

A_HEADS, A_KV, A_HD = 16, 4, 64
IDX_HEADS = 8
TOPK = min(256, SEQ // 4)
A_Q, A_K, A_V, A_IQ, A_IK = 0, 1024, 1280, 1536, 2048
A_IN = 2120
A_SMALL = A_IN - A_IK
ROT = A_HD // 4 // 2
B_LOW = 3072
B_RANK = 16
M_HEADS, M_NOPE, M_ROPE = 8, 128, 64
M_HALF = M_ROPE // 2
M_SCALE = float((M_NOPE + M_ROPE) ** -0.5)

RING = 3
CH = 2048
FG = 256
MLP_GROUPS = DFF // FG
FFN_GROUPS = DFF2 // FG

MASKED = -1.0e30
NOT_CAUSAL = -3.0e38
TAKEN = -3.4e38
MAGIC = 12582912.0
TWO_PI = 2.0 * np.pi
PI_A = 6.28125
PI_B = float(np.float32(np.round((TWO_PI - PI_A) * 2.0**21) / 2.0**21))
PI_C = float(np.float32(TWO_PI - PI_A - PI_B))
PI_MAX = 3.1415925
LN_FLOOR = float(2.0**-64)
RSQRT_SEED = float(0x5F3759DF)

V_BA, V_QN, V_KVN, V_LB, V_ROWS = 0, 4, 6, 8, 24

LEVELS = [128, 64, 32, 16, 8, 4, 2, 1]


def inverse_frequencies():
    a = [float(np.float32(500000.0) ** np.float32(-i / 16.0)) for i in range(0, 16, 2)]
    m = [float(np.float32(10000.0) ** np.float32(-i / 64.0)) for i in range(0, 64, 2)]
    return a, m


def build(nc, t, out):
    with ExitStack() as ctx:

        def sb(name, shape, dt=F32):
            return ctx.enter_context(nc.sbuf_tensor(name, shape, dt))

        class Semaphores(dict):
            def __missing__(self, name):
                self[name] = ctx.enter_context(nc.semaphore(name))
                return self[name]

        s = Semaphores()

        ps = ctx.enter_context(nc.psum_tensor("ps", [P, 8, 512], F32))
        x = sb("x", [P, TT, D])
        y = sb("y", [P, TT, D])
        xh = sb("xh", [P, KD, SEQ], F32R)
        xl = sb("xl", [P, KD, SEQ], F32R)
        raw = sb("raw", [P, RING, CH])
        whi = sb("whi", [P, RING, CH], F32R)
        wlo = sb("wlo", [P, RING, CH], F32R)
        lnw = sb("lnw", [P, 2, D])
        hh = sb("hh", [P, 3, 512], F32R)
        hl = sb("hl", [P, 3, 512], F32R)
        buf = [sb(f"buf{i}", [P, 2048]) for i in range(8)]
        ident = sb("ident", [P, P])
        stats = sb("stats", [P, TT, 2, 6])
        mv = sb("mv", [P, TT, 2])
        small = sb("small", [P, 64])
        inv = sb("inv", [P, 40])
        posi = sb("posi", [P, 2, TT], I32)
        posf = sb("posf", [P, 2, TT])
        sinA = sb("sinA", [P, TT, ROT])
        cosA = sb("cosA", [P, TT, ROT])
        sinM = sb("sinM", [P, TT, M_HALF])
        cosM = sb("cosM", [P, TT, M_HALF])
        vrow = sb("vrow", [V_ROWS, P])
        vcol = sb("vcol", [P, V_ROWS])
        lbv = sb("lbv", [P, 8, 8])
        masks = sb("masks", [P, 8, P])
        alow = sb("alow", [P, TT, B_RANK])
        alowT = sb("alowT", [B_RANK, SEQ])

        def bank(b, n=512):
            return ps[:, b, 0:n]

        def banks(b, n):
            return ps[:, b : b + n, :].rearrange("p b c -> p (b c)")

        width = []
        source = []
        first = {}

        def chunk(name, src, k, cols):
            first.setdefault(name, len(width))
            width.append(k * cols)
            source.append((src, k, cols))

        def rows_of(w, k0, kn, c0, cn):
            return w.rearrange("(k p) c -> p k c", p=P)[:, k0 : k0 + kn, c0 : c0 + cn]

        def square_chunks(name, w, c0=0):
            for q in range(4):
                chunk(name, rows_of(w, 2 * q, 2, c0, D), 2, D)

        def column_chunks(name, w, c0, count):
            for q in range(count):
                chunk(name, rows_of(w, 0, KD, c0 + FG * q, FG), KD, FG)

        a_in, b_in = t["a_w_in"][0], t["b_w_in"][0]
        square_chunks("dsa_kvi", a_in, A_K)
        chunk("dsa_small", rows_of(a_in, 0, KD, A_IK, A_SMALL), KD, A_SMALL)
        square_chunks("dsa_q", a_in, A_Q)
        square_chunks("dsa_o", t["a_w_o"][0])

        def mlp_chunks(layer):
            up, down = t["mlp_w_up"][layer], t["mlp_w_down"][layer]
            for q in range(MLP_GROUPS + 1):
                if q < MLP_GROUPS:
                    chunk(f"mlp{layer}", rows_of(up, 0, KD, FG * q, FG), KD, FG)
                if q:
                    chunk(f"mlp{layer}", rows_of(down, 2 * q - 2, 2, 0, D), 2, D)

        def ffn_chunks(layer):
            w_in, down = t["ffn_w_in_2"][layer], t["ffn_w_down_2"][layer]
            for q in range(FFN_GROUPS + 1):
                if q < FFN_GROUPS:
                    chunk(f"ffn{layer}", rows_of(w_in, 0, KD, FG * q, FG), KD, FG)
                    chunk(f"ffn{layer}", rows_of(w_in, 0, KD, DFF2 + FG * q, FG), KD, FG)
                if q:
                    chunk(f"ffn{layer}", rows_of(down, 2 * q - 2, 2, 0, D), 2, D)

        def ple_chunks(layer):
            square_chunks(f"ple{layer}", t["ple_w_gate_2"][layer])
            chunk(f"ple{layer}", rows_of(t["ple_w_proj_2"][layer], 0, 2, 0, D), 2, D)

        mlp_chunks(0)
        column_chunks("gla_qk", b_in, 0, 4)
        chunk("gla_low", rows_of(b_in, 0, KD, B_LOW, B_RANK), KD, B_RANK)
        square_chunks("gla_v", b_in, 1024)
        square_chunks("gla_r", b_in, 2048)
        square_chunks("gla_o", t["b_w_o"][0])
        mlp_chunks(1)
        w_down = t["mla_w_dqkv_2"][0]
        chunk("mla_down", rows_of(w_down, 0, 4, 0, 512), 4, 512)
        chunk("mla_down", rows_of(w_down, 4, 4, 0, 512), 4, 512)
        chunk("mla_down", rows_of(w_down, 0, KD, 512, M_ROPE), KD, M_ROPE)
        for q in range(2):
            chunk("mla_q", rows_of(t["mla_w_uq_2"][0], 0, 2, 768 * q, 768), 2, 768)
        for q in range(2):
            chunk("mla_kv", rows_of(t["mla_w_ukv_2"][0], 0, 2, D * q, D), 2, D)
        square_chunks("mla_o", t["mla_w_o_2"][0])
        ffn_chunks(0)
        ple_chunks(0)
        column_chunks("hgrn_f", t["hgrn_w_in_2"][0], 1024, 4)
        column_chunks("hgrn_q", t["hgrn_w_in_2"][0], 0, 4)
        square_chunks("hgrn_v", t["hgrn_w_in_2"][0], 2048)
        square_chunks("hgrn_gate", t["hgrn_w_in_2"][0], 3072)
        square_chunks("hgrn_o", t["hgrn_w_o_2"][0])
        ffn_chunks(1)
        ple_chunks(1)
        N_CHUNKS = len(width)

        (T_X0, T_DSA, T_X1, T_X2, T_GLA, T_X3, T_X4, T_MLA, T_X5, T_X6, T_X7, T_HGRN, T_X8, T_X9) = range(14)

        NORM_TURN = [T_X1, T_X2, T_X3, T_X4, T_X5, T_X6, T_X8, T_X9]

        block = ctx.enter_context(nc.Block())

        @block.sync
        def _(sp):
            sp.dma_start(x[:, :, :], t["x"][0].rearrange("(t p) d -> p t d", p=P)).then_inc(s["x_landed"], 16)

            def load(n):
                src, k, cols = source[n]
                if n >= RING:
                    sp.wait_ge(s["lo_done"], n - RING + 1)
                dst = raw[:, n % RING, 0 : k * cols].rearrange("p (k c) -> p k c", k=k)
                sp.dma_start(dst, src).then_inc(s[f"raw_landed{n % RING}"], 16)

            def load_in_loop(n, per, i, src, k, cols):
                sp.wait_ge(s["lo_done"], i * per + (n - RING + 1))
                dst = raw[:, n % RING, :].rearrange("p (k c) -> p k c", k=k)
                sp.dma_start(dst, src).then_inc(s[f"raw_landed{n % RING}"], 16)

            def load_mlp(layer):
                n0 = first[f"mlp{layer}"]
                up = t["mlp_w_up"][layer].rearrange("(k p) f -> p k f", p=P)
                down = t["mlp_w_down"][layer].rearrange("(c p) d -> p c d", p=P)
                load(n0)
                with sp.Fori(0, (MLP_GROUPS - 1) // 3) as i:
                    for j in range(3):
                        load_in_loop(n0 + 1 + 2 * j, 6, i, up[:, :, bass.ds(i * (3 * FG) + (j + 1) * FG, FG)], KD, FG)
                        load_in_loop(n0 + 2 + 2 * j, 6, i, down[:, bass.ds(i * 6 + 2 * j, 2), :], 2, D)
                load(n0 + 2 * MLP_GROUPS - 1)

            def load_ffn(layer):
                n0 = first[f"ffn{layer}"]
                w_in = t["ffn_w_in_2"][layer].rearrange("(k p) f -> p k f", p=P)
                down = t["ffn_w_down_2"][layer].rearrange("(c p) d -> p c d", p=P)
                load(n0)
                load(n0 + 1)
                with sp.Fori(0, (FFN_GROUPS - 1) // 2) as i:
                    for j in range(2):
                        g0 = (j + 1) * FG
                        load_in_loop(n0 + 2 + 3 * j, 6, i, w_in[:, :, bass.ds(i * (2 * FG) + g0, FG)], KD, FG)
                        load_in_loop(n0 + 3 + 3 * j, 6, i, w_in[:, :, bass.ds(i * (2 * FG) + (DFF2 + g0), FG)], KD, FG)
                        load_in_loop(n0 + 4 + 3 * j, 6, i, down[:, bass.ds(i * 4 + 2 * j, 2), :], 2, D)
                load(n0 + 3 * FFN_GROUPS - 1)

            def load_from(n, end):
                for m in range(n, end):
                    load(m)

            load_from(0, first["mlp0"])
            load_mlp(0)
            load_from(first["gla_qk"], first["mlp1"])
            load_mlp(1)
            load_from(first["mla_down"], first["ffn0"])
            load_ffn(0)
            load_from(first["ple0"], first["ffn1"])
            load_ffn(1)
            load_from(first["ple1"], N_CHUNKS)
            for tt in range(TT):
                sp.wait_ge(s["out_ready"], tt + 1)
                sp.dma_start(out[0, tt * P : (tt + 1) * P, :], x[:, tt, :]).then_inc(s["out_landed"], 16)
            sp.wait_ge(s["out_landed"], 16 * TT)

        half = lambda b, h: buf[b][:, 1024 * h : 1024 * h + 1024]
        kvi = buf[0][:, :].rearrange("p (t c) -> p t c", t=TT)
        qtok = buf[1][:, :].rearrange("p (t c) -> p t c", t=TT)
        ikw = sb("ikw", [P, TT, A_SMALL])
        kdup = half(2, 0).rearrange("p (t g e d) -> p t g e d", t=TT, g=A_KV, e=2)
        iqT = half(2, 1).rearrange("p (c n) -> p c n", c=4)
        qT = buf[3][:, :].rearrange("p (c n) -> p c n", c=KD)
        kT = buf[4][:, :].rearrange("p (g e n) -> p g e n", g=A_KV, e=2)
        ikT = half(7, 0)[:, 0:512].rearrange("p (e n) -> p e n", e=2)
        ikdup = half(7, 0)[:, 512:768].rearrange("p (t e d) -> p t e d", t=TT, e=2)
        score = half(7, 1)[:, 0:512].rearrange("p (b n) -> p b n", b=TT)
        relu_s = buf[5][:, :].rearrange("p (u n) -> p u n", u=4)
        work = sb("work", [P, TT, 2, SEQ])
        top8 = sb("top8", [P, TT, 8])
        bias = work[:, :, 0, :]
        logit = buf[6][:, :].rearrange("p (e n) -> p e n", e=2)
        probT = buf[7][:, :].rearrange("p (e n) -> p e n", e=2)
        negmax = sb("negmax", [P, 2, 4])
        rowsum = sb("rowsum", [P, TT, A_HEADS])
        rinv = sb("rinv", [P, TT, A_HEADS])
        lat = half(1, 0).rearrange("p (t c) -> p t c", t=TT)
        latn = half(1, 1).rearrange("p (t c) -> p t c", t=TT)
        vM = buf[0][:, :].rearrange("p (t c) -> p t c", t=TT)
        qnT = buf[3][:, :].rearrange("p (h n) -> p h n", h=M_HEADS)
        knT = buf[2][:, :].rearrange("p (h n) -> p h n", h=M_HEADS)
        qrT = half(4, 0).rearrange("p (c n) -> p c n", c=4)
        krT = half(4, 1)[:, 0:512].rearrange("p (e n) -> p e n", e=2)
        krdup = half(4, 1)[:, 512:768].rearrange("p (t e d) -> p t e d", t=TT, e=2)
        krtok = half(4, 1)[:, 768:896].rearrange("p (t d) -> p t d", t=TT)
        qrtok = half(5, 0).rearrange("p (t c) -> p t c", t=TT)
        causal = half(5, 1)[:, 0:512].rearrange("p (b n) -> p b n", b=TT)
        rot4 = sb("rot4", [P, 4, 256])
        q4 = [half(0, 0).rearrange("p (h n) -> p h n", h=4), half(0, 1).rearrange("p (h n) -> p h n", h=4)]
        k4 = [half(1, 0).rearrange("p (h n) -> p h n", h=4), half(1, 1).rearrange("p (h n) -> p h n", h=4)]
        g4 = [half(2, 0).rearrange("p (h n) -> p h n", h=4), half(2, 1).rearrange("p (h n) -> p h n", h=4)]
        expo = [half(3, 0), half(3, 1)]
        zed = [half(7, 0), half(7, 1)]
        wa2 = buf[4][0:B_RANK, 1536:2048]
        att = buf[4][:, 0:1536].rearrange("p (h e n) -> p h e n", h=4, e=3)
        vtok = buf[5][:, :].rearrange("p (t c) -> p t c", t=TT)
        gate = buf[6][:, :].rearrange("p (t c) -> p t c", t=TT)
        gn = y[:, 0, :]
        ss = sb("ss", [P, TT, 8])
        ptok = buf[0][:, 0:512].rearrange("p (t c) -> p t c", t=TT)

        def decay_out(c, tt, h, hd):
            if hd == 256:
                return ps[:, 2 * tt + h // 2, 256 * (h % 2) : 256 * (h % 2) + 256]
            return ps[:, 2 * (c == 2) + tt, P * h : P * h + P]

        @block.gpsimd
        def _(pool):
            n_step = [0]

            def step(ins):
                ins.then_inc(s["pool_step"], 1)
                n_step[0] += 1
                pool.wait_ge(s["pool_step"], n_step[0])

            g = nc.gpsimd
            for w, name in enumerate(("positions", "positions_2")):
                pool.dma_start(posi[:, w, :], t[name][0].rearrange("(t p) -> p t", p=P), allow_slow_non_contiguous=True).then_inc(s["pos_landed"], 16)
            pool.dma_start(vrow[V_BA : V_BA + 4, :], t["b_b_a"][0].rearrange("(r p) -> r p", p=P)).then_inc(s["vrow_landed"], 16)
            pool.dma_start(vrow[V_QN : V_QN + 2, :], t["mla_q_norm_2"][0].rearrange("(r p) -> r p", p=P)).then_inc(s["vrow_landed"], 16)
            pool.dma_start(vrow[V_KVN : V_KVN + 2, :], t["mla_kv_norm_2"][0].rearrange("(r p) -> r p", p=P)).then_inc(s["vrow_landed"], 16)
            pool.dma_start(vrow[V_LB : V_LB + 16, :], t["hgrn_lb_logits_2"].rearrange("l (h p) -> (l h) p", p=P)).then_inc(s["vrow_landed"], 16)

            def load_ln(i):
                layer = (i // 2) % 2
                if i < 4:
                    gb = ("ln_mix_g", "ln_mix_b") if i % 2 == 0 else ("ln_mlp_g", "ln_mlp_b")
                else:
                    gb = ("ln_mix_g_2", "ln_mix_b_2") if i % 2 == 0 else ("ln_ffn_g_2", "ln_ffn_b_2")
                if i >= 1:
                    pool.wait_ge(s["src_ready"], ready(NORM_TURN[i - 1], 1))
                for w, name in enumerate(gb):
                    pool.dma_start(lnw[:, w, :], t[name][layer].partition_broadcast(P)).then_inc(s["ln_landed"], 16)

            load_ln(0)
            freq_a, freq_m = inverse_frequencies()
            for c, f in enumerate(freq_a + freq_m):
                last = g.memset(inv[:, c : c + 1], f)
            last.then_inc(s["inv_done"], 1)
            step(g.memset(ident[:, :], 0.0))
            g.affine_select(out=ident[:, :], in_=ident[:, :], compare_op=ALU.not_equal, fill=1.0, base=0,
                            pattern=[[-1, P]], channel_multiplier=1).then_inc(s["ident_done"], 1)

            def note(ins):
                ins.then_inc(s["pool_step"], 1)
                n_step[0] += 1

            def rotate(v, n_heads, cos, sin, hd, tt, scratch, signal=None):
                c = cos[:, tt, :].unsqueeze(1).broadcast_to([P, n_heads, hd])
                sn = sin[:, tt, :].unsqueeze(1).broadcast_to([P, n_heads, hd])
                a, b, e, f = (scratch[:, q, 0 : n_heads * hd].rearrange("p (h d) -> p h d", h=n_heads) for q in range(4))
                t1, t2 = v[:, :, 0:hd], v[:, :, hd : 2 * hd]
                note(g.tensor_tensor(a, t1, c, ALU.mult))
                note(g.tensor_tensor(b, t2, sn, ALU.mult))
                note(g.tensor_tensor(e, t2, c, ALU.mult))
                step(g.tensor_tensor(f, t1, sn, ALU.mult))
                step(g.tensor_tensor(t1, a, b, ALU.subtract))
                last = g.tensor_tensor(t2, e, f, ALU.add)
                if signal is None:
                    step(last)
                else:
                    last.then_inc(s[signal], 1)
                    pool.wait_ge(s[signal], tt + 1)

            note(g.memset(ikT[:, :, :], 0.0))
            step(g.memset(kT[:, :, :, :], 0.0))
            pool.wait_ge(s["tables_done"], 1)
            pool.wait_ge(s["kvi_act"], 2)
            pool.wait_ge(s["kvi_dve"], 2)
            pool.wait_ge(s["small_out"], 2)
            for tt in range(TT):
                rotate(kvi[:, tt, 512:1024].rearrange("p (h d) -> p h d", d=A_HD), IDX_HEADS, cosA, sinA, ROT, tt, rot4)
                rotate(ikw[:, tt, 0:A_HD].unsqueeze(1), 1, cosA, sinA, ROT, tt, rot4)
                step(g.tensor_copy(ikdup[:, tt, :, :], ikw[:, tt, 0:A_HD].unsqueeze(1).broadcast_to([P, 2, A_HD])))
                g.tensor_scalar(ikw[:, tt, A_HD:A_SMALL], ikw[:, tt, A_HD:A_SMALL], float(IDX_HEADS**-0.5), None,
                                ALU.mult).then_inc(s["index_rotated"], 1)
            for tt in range(TT):
                rotate(kvi[:, tt, 0:256].rearrange("p (h d) -> p h d", d=A_HD), A_KV, cosA, sinA, ROT, tt, rot4)
                g.tensor_copy(kdup[:, tt, :, :, :], kvi[:, tt, 0:256].rearrange("p (h d) -> p h d", d=A_HD).unsqueeze(2)
                              .broadcast_to([P, A_KV, 2, A_HD])).then_inc(s["k_rotated"], 1)
            for b in range(TT):
                pool.wait_ge(s["index_added"], (2, 6)[b])
                g.affine_select(out=work[:, b, 0, :], in_=score[:, b, :], compare_op=ALU.is_ge, fill=NOT_CAUSAL,
                                base=b * P, pattern=[[-1, SEQ]], channel_multiplier=1).then_inc(s["score_masked"], 1)
            pool.wait_ge(s["q_out"], 4)
            for tt in range(TT):
                rotate(qtok[:, tt, :].rearrange("p (h d) -> p h d", d=A_HD), A_HEADS, cosA, sinA, ROT, tt, rot4, "q_rotated")
            for b in range(TT):
                pool.wait_ge(s["chosen"], b + 1)
                g.affine_select(out=bias[:, b, :], in_=work[:, b, 1, :], compare_op=ALU.is_ge, fill=MASKED,
                                base=b * P, pattern=[[-1, SEQ]], channel_multiplier=1).then_inc(s["bias_done"], 1)

            for m in range(1, 8):
                lv = LEVELS[m]
                v = masks[:, m - 1, :].rearrange("p (b e c) -> p b e c", e=2, c=lv)
                step(g.memset(masks[:, m - 1, :], 0.0))
                step(g.memset(v[:, :, 1, :], 1.0))
                step(g.affine_select(out=v[:, :, 1, :], in_=v[:, :, 1, :], compare_op=ALU.is_ge, fill=0.0, base=0,
                                     pattern=[[-2 * lv, P // (2 * lv)], [0, lv]], channel_multiplier=1))
                step(g.affine_select(out=v[:, :, 1, :], in_=v[:, :, 1, :], compare_op=ALU.is_ge, fill=0.0, base=lv - 1,
                                     pattern=[[2 * lv, P // (2 * lv)], [0, lv]], channel_multiplier=-1))
            g.tensor_copy(masks[:, 7, :], ident[:, :]).then_inc(s["masks_done"], 1)
            pool.wait_ge(s["src_ready"], ready(T_DSA, 1))
            pool.dma_start(wa2, t["b_w_a2"][0]).then_inc(s["wa2_landed"], 16)
            load_ln(1)
            load_ln(2)
            for h in range(4):
                pool.dma_start(gn[:, 256 * h : 256 * h + 256], t["b_g_norm"][0].partition_broadcast(P)).then_inc(s["gn_landed"], 16)
            load_ln(3)
            pool.wait_ge(s["src_ready"], ready(T_GLA, 1))
            step(g.memset(causal[:, :, :], 0.0))
            for b in range(TT):
                ins = g.affine_select(out=causal[:, b, :], in_=causal[:, b, :], compare_op=ALU.is_ge, fill=MASKED,
                                      base=b * P, pattern=[[-1, SEQ]], channel_multiplier=1)
            ins.then_inc(s["causal_done"], 1)
            step(g.memset(krT[:, :, :], 0.0))
            pool.wait_ge(s["kr_out"], TT)
            for tt in range(TT):
                rotate(krtok[:, tt, :].unsqueeze(1), 1, cosM, sinM, M_HALF, tt, rot4)
                g.tensor_copy(krdup[:, tt, :, :], krtok[:, tt, :].unsqueeze(1).broadcast_to([P, 2, M_ROPE])).then_inc(s["kr_rotated"], 1)
            pool.wait_ge(s["qr_out"], 4)
            for tt in range(TT):
                rotate(qrtok[:, tt, :].rearrange("p (h d) -> p h d", d=M_ROPE), M_HEADS, cosM, sinM, M_HALF, tt, rot4, "qr_rotated")
            load_ln(4)
            pool.wait_ge(s["src_ready"], ready(T_MLA, 1))
            pool.dma_start(ptok, t["p_2"][0, 0].rearrange("(t p) d -> p t d", p=P)).then_inc(s["p_landed"], 16)
            load_ln(5)
            load_ln(6)
            pool.wait_ge(s["src_ready"], ready(T_X7, 1))
            pool.dma_start(gn, t["hgrn_out_norm_2"][0].partition_broadcast(P)).then_inc(s["gn_landed"], 16)
            pool.wait_ge(s["src_ready"], ready(T_HGRN, 1))
            pool.dma_start(ptok, t["p_2"][1, 0].rearrange("(t p) d -> p t d", p=P)).then_inc(s["p_landed"], 16)
            load_ln(7)

        @block.tensor
        def _(pe):
            mm = nc.tensor.matmul

            def three(o, a, b, start, stop):
                mm(o, a[0], b[0], start=start, stop=False)
                mm(o, a[1], b[0], start=False, stop=False)
                return mm(o, a[0], b[1], start=False, stop=stop)

            def weights(n, k, cols):
                slot = n % RING
                return [w[:, slot, 0 : k * cols].rearrange("p (k c) -> p k c", k=k) for w in (whi, wlo)]

            def take(n):
                pe.wait_ge(s["lo_done"], n + 1)

            def by_rows(n, k, cols, k0, total_k, outs, src=(xh, xl)):
                take(n)
                w = weights(n, k, cols)
                for kk in range(k):
                    for tt, cs, o in outs:
                        a = [v[:, k0 + kk, tt * P : (tt + 1) * P] for v in src]
                        last = three(o, a, [v[:, kk, cs] for v in w], k0 + kk == 0, k0 + kk == total_k - 1)
                last.then_inc(s["w_done"], 1)

            def wide(base):
                return [(tt, slice(512 * c, 512 * c + 512), bank(base + 2 * tt + c)) for tt in range(TT) for c in range(2)]

            def square(n0, base):
                for q in range(4):
                    by_rows(n0 + q, 2, D, 2 * q, KD, wide(base))

            def columns(w, o, src=(xh, xl)):
                for f in range(2):
                    for kk in range(KD):
                        last = three(o[:, 256 * f : 256 * f + 256], [v[:, kk, P * f : P * f + P] for v in w],
                                     [v[:, kk, :] for v in src], kk == 0, kk == KD - 1)
                return last

            def turn(j, src):
                for tt in range(TT):
                    if j == 0:
                        pe.wait_ge(s["x_landed"], 16)
                        pe.wait_ge(s["ident_done"], 1)
                    else:
                        pe.wait_ge(s["src_ready"], ready(j, tt))
                    for hf in range(2):
                        for q in range(4):
                            last = nc.tensor.transpose(ps[:, 4 + 2 * tt + hf, P * q : P * q + P],
                                                       src[:, tt, P * (4 * hf + q) : P * (4 * hf + q) + P], ident[:, :])
                        last.then_inc(s["turned"], 1)
                pe.wait_ge(s["turn_lo"], 4 * j + 4)

            def mlp(layer):
                n0 = first[f"mlp{layer}"]

                take(n0)
                columns(weights(n0, KD, FG), bank(4)).then_inc(s["w_done"], 1)

                def down(n, slot, start, stop):
                    w = weights(n, 2, D)
                    for f in range(2):
                        for tt, cs, o in wide(0):
                            a = [v[:, slot, 256 * f + P * tt : 256 * f + P * tt + P] for v in (hh, hl)]
                            last = three(o, a, [v[:, f, cs] for v in w], start and f == 0, stop and f == 1)
                    last.then_inc(s["w_done"], 1)

                def body(it, j, start):
                    n = n0 + 1 + 2 * j
                    up_ready, h_ready, down_ready = n + 1, hcount(layer, 0, j) + 1, n + 2
                    if it is not None:
                        up_ready = pe.snap(it * 6 + up_ready)
                        h_ready = pe.snap(it * 3 + h_ready)
                        down_ready = pe.snap(it * 6 + down_ready)
                    pe.wait_ge(s["lo_done"], up_ready)
                    columns(weights(n, KD, FG), bank(4 + (j + 1) % 3)).then_inc(s["w_done"], 1)
                    pe.wait_ge(s["h_lo"], h_ready)
                    pe.wait_ge(s["lo_done"], down_ready)
                    down(n + 1, j % 3, start, False)

                for j in range(3):
                    body(None, j, j == 0)
                with pe.Fori(1, (MLP_GROUPS - 1) // 3) as it:
                    for j in range(3):
                        body(it, j, False)
                n = n0 + 2 * MLP_GROUPS - 1
                take(n)
                pe.wait_ge(s["h_lo"], hcount(layer, 0, MLP_GROUPS - 1) + 1)
                down(n, (MLP_GROUPS - 1) % 3, False, True)

            def ffn(layer):
                n0 = first[f"ffn{layer}"]
                for w in range(2):
                    take(n0 + w)
                    columns(weights(n0 + w, KD, FG), bank(4 + w)).then_inc(s["w_done"], 1)

                def down(n, slot, start, stop):
                    w = weights(n, 2, D)
                    for f in range(2):
                        for tt, cs, o in wide(0):
                            a = [v[:, slot, 256 * f + P * tt : 256 * f + P * tt + P] for v in (hh, hl)]
                            last = three(o, a, [v[:, f, cs] for v in w], start and f == 0, stop and f == 1)
                    last.then_inc(s["w_done"], 1)

                def body(it, j, start):
                    n = n0 + 2 + 3 * j
                    for w in range(2):
                        ready = n + w + 1
                        if it is not None:
                            ready = pe.snap(it * 6 + ready)
                        pe.wait_ge(s["lo_done"], ready)
                        columns(weights(n + w, KD, FG), bank(4 + 2 * ((j + 1) % 2) + w)).then_inc(s["w_done"], 1)
                    h_ready, down_ready = hcount(layer, 1, j) + 1, n + 3
                    if it is not None:
                        h_ready = pe.snap(it * 2 + h_ready)
                        down_ready = pe.snap(it * 6 + down_ready)
                    pe.wait_ge(s["h_lo"], h_ready)
                    pe.wait_ge(s["lo_done"], down_ready)
                    down(n + 2, j % 2, start, False)

                body(None, 0, True)
                body(None, 1, False)
                with pe.Fori(1, (FFN_GROUPS - 1) // 2) as it:
                    for j in range(2):
                        body(it, j, False)
                n = n0 + 3 * FFN_GROUPS - 1
                take(n)
                pe.wait_ge(s["h_lo"], hcount(layer, 1, FFN_GROUPS - 1) + 1)
                down(n, (FFN_GROUPS - 1) % 2, False, True)

            def attention(kind, units, score_mm, value, hd, per_bank):
                n_units = len(units)
                base = kind * ATT_BASE

                def logits(u):
                    b, g = units[u]
                    if u >= 2:
                        pe.wait_ge(s["logit_read"], base + u - 1)
                    for h in range(4):
                        n = P * (b + 1)
                        o = ps[:, 2 * (u % 2), P * h : P * h + P] if b == 0 else ps[:, 2 * (u % 2) + h // 2, 256 * (h % 2) : 256 * (h % 2) + 256]
                        last = score_mm(o, b, 4 * g + h, n)
                    last.then_inc(s["logits"], 1)

                def rest(u):
                    b, g = units[u]
                    pe.wait_ge(s["exp_done"], base + u + 1)
                    if u >= 1:
                        pe.wait_ge(s["probT_act"], base + u)
                        pe.wait_ge(s["probT_dve"], base + u)
                    nk = b + 1
                    for kt in range(nk):
                        for h in range(4):
                            src = logit[:, u % 2, P * nk * h + P * kt : P * nk * h + P * kt + P]
                            last = nc.tensor.transpose(ps[:, 4 + kt, P * h : P * h + P], src, ident[:, :])
                    last.then_inc(s["probs_turned"], 1)
                    pe.wait_ge(s["probT_act"], base + u + 1)
                    pe.wait_ge(s["probT_dve"], base + u + 1)
                    if u == n_units // 2:
                        pe.wait_ge(s["src_ready"], ready((T_DSA, T_MLA)[kind], 0))
                    for h in range(4):
                        hd0 = (4 * g + h) * hd
                        o = ps[:, 6 + hd0 // 512, hd0 % 512 : hd0 % 512 + hd]
                        for kt in range(nk):
                            lhs = probT[:, u % 2, 512 * kt + P * h : 512 * kt + P * h + P]
                            last = mm(o, lhs, value(kt, 4 * g + h), start=(kt == 0), stop=(kt == nk - 1))
                    last.then_inc(s["att_pv"], 1)

                logits(0)
                for u in range(n_units):
                    if u + 1 < n_units:
                        logits(u + 1)
                    rest(u)

            def decay(c, hd):
                for lv in range(9):
                    b0 = 4 + 2 * (lv % 2)
                    if lv < 8:
                        pe.wait_ge(s["zed_done"], 8 * c + lv + 1)
                    if lv >= 2 or c > 0:
                        pe.wait_ge(s["level_read"], 9 * c + max(lv - 1, 0))
                    if lv == 0:
                        for h in range(4):
                            z = zed[0][:, 256 * h : 256 * h + 256]
                            last = mm(ps[:, 4, P * h : P * h + P], z[:, 0:P], z[:, P:SEQ], start=True, stop=True)
                    else:
                        for h in range(4):
                            for tt in range(TT):
                                sl = slice(256 * h + P * tt, 256 * h + P * tt + P)
                                if lv < 8:
                                    a = b = zed[lv % 2][:, sl]
                                else:
                                    a = k4[int(c == 2)][:, h, P * tt : P * tt + P]
                                    b = q4[int(c == 2)][:, h, P * tt : P * tt + P]
                                o = ps[:, b0 + h // 2, 256 * (h % 2) + P * tt : 256 * (h % 2) + P * tt + P]
                                last = mm(o, a, b, start=True, stop=True)
                    last.then_inc(s["level_done"], 1)
                pe.wait_ge(s["level_read"], 9 * c + 9)
                for tt in range(TT):
                    for h in range(4):
                        o = decay_out(c, tt, h, hd)
                        hv = slice(vcol0(c) + hd * h, vcol0(c) + hd * h + hd)
                        if tt == 0:
                            last = mm(o, att[:, h, 0, :], vtok[:, 0, hv], start=True, stop=True)
                        else:
                            mm(o, att[:, h, 2, :], vtok[:, 0, hv], start=True, stop=False)
                            last = mm(o, att[:, h, 1, :], vtok[:, 1, hv], start=False, stop=True)
                    last.then_inc(s["decay_pv"], 1)

            def ple(layer, j):
                turn(j, x)
                n0 = first[f"ple{layer}"]
                square(n0, 0)
                pe.wait_ge(s["p_landed"], 16 * (layer + 1))
                for tt in range(TT):
                    for q in range(2):
                        last = nc.tensor.transpose(ps[:, 4, 256 * q + P * tt : 256 * q + P * tt + P], ptok[:, tt, P * q : P * q + P], ident[:, :])
                last.then_inc(s["p_turned"], 1)
                pe.wait_ge(s["p_lo"], layer + 1)
                by_rows(n0 + 4, 2, D, 0, 2, wide(4), src=(hh[:, 0, :].rearrange("p (k n) -> p k n", k=2), hl[:, 0, :].rearrange("p (k n) -> p k n", k=2)))

            turn(T_X0, x)
            pe.wait_ge(s["vrow_landed"], 64)
            nc.tensor.transpose(ps[:, 4, 0:V_ROWS], vrow[:, :], ident[0:V_ROWS, 0:V_ROWS]).then_inc(s["vrow_turned"], 1)

            square(first["dsa_kvi"], 0)
            pe.wait_ge(s["vcol_done"], 1)
            by_rows(first["dsa_small"], KD, A_SMALL, 0, KD,
                    [(tt, slice(0, A_SMALL), bank(4 + tt, A_SMALL)) for tt in range(TT)])
            pe.wait_ge(s["kvi_act"], 2)
            pe.wait_ge(s["kvi_dve"], 2)
            for q in range(2):
                by_rows(first["dsa_q"] + q, 2, D, 2 * q, KD, wide(0))
            for tt in range(TT):
                pe.wait_ge(s["index_rotated"], tt + 1)
                for q in range(4):
                    nc.tensor.transpose(ps[:, 6 + tt, P * q : P * q + P], kvi[:, tt, 512 + P * q : 512 + P * q + P], ident[:, :])
                last = nc.tensor.transpose(ps[:, 4 + tt, 0:P], ikdup[:, tt, :, :].rearrange("p e d -> p (e d)"), ident[:, :])
                last.then_inc(s["index_turned"], 1)
            pe.wait_ge(s["indexT_done"], 2 * TT)
            for u, (b, hs) in enumerate(INDEX_UNITS):
                if u >= 4:
                    pe.wait_ge(s["index_relu"], u - 3)
                n = P * (b + 1)
                for i, h in enumerate(hs):
                    last = mm(ps[:, 4 + u % 4, n * i : n * i + n], iqT[:, h // 2, b * P : b * P + P], ikT[:, h % 2, 0:n], start=True, stop=True)
                last.then_inc(s["index_scores"], 1)
            for q in range(2, 4):
                by_rows(first["dsa_q"] + q, 2, D, 2 * q, KD, wide(0))
            pe.wait_ge(s["index_relu"], len(INDEX_UNITS))
            for tt in range(TT):
                pe.wait_ge(s["k_rotated"], tt + 1)
                for g in range(A_KV):
                    last = nc.tensor.transpose(ps[:, 4 + tt, P * g : P * g + P], kdup[:, tt, g, :, :].rearrange("p e d -> p (e d)"), ident[:, :])
                last.then_inc(s["k_turned"], 1)
            for tt in range(TT):
                pe.wait_ge(s["q_rotated"], tt + 1)
                for hf in range(2):
                    b = 6 + hf if tt == 0 else 4 + hf
                    if tt == 1:
                        pe.wait_ge(s["kT_done"], hf + 1)
                    for q in range(4):
                        last = nc.tensor.transpose(ps[:, b, P * q : P * q + P], qtok[:, tt, P * (4 * hf + q) : P * (4 * hf + q) + P], ident[:, :])
                    last.then_inc(s["q_turned"], 1)
            pe.wait_ge(s["qT_done"], 4)

            def dsa_scores(o, b, h, n):
                return mm(o, qT[:, h // 2, b * P : b * P + P], kT[:, h // 4, h % 2, 0:n], start=True, stop=True)

            attention(0, ATT_UNITS[0], dsa_scores, lambda kt, h: kvi[:, kt, 256 + 64 * (h // 4) : 320 + 64 * (h // 4)], A_HD, 8)
            turn(T_DSA, y)
            square(first["dsa_o"], 0)
            turn(T_X1, x)
            mlp(0)
            turn(T_X2, x)

            for q in range(4):
                n = first["gla_qk"] + q
                take(n)
                columns(weights(n, KD, FG), bank(q)).then_inc(s["w_done"], 1)
            by_rows(first["gla_low"], KD, B_RANK, 0, KD, [(tt, slice(0, B_RANK), bank(4 + tt, B_RANK)) for tt in range(TT)])
            pe.wait_ge(s["low_out"], 1)
            for tt in range(TT):
                last = nc.tensor.transpose(ps[0:B_RANK, 6, P * tt : P * tt + P], alow[:, tt, :], ident[:, :])
            last.then_inc(s["low_turned"], 1)
            pe.wait_ge(s["lowT_done"], 1)
            pe.wait_ge(s["wa2_landed"], 16)
            for h in range(4):
                last = mm(ps[:, 6 + h // 2, 256 * (h % 2) : 256 * (h % 2) + 256], wa2[:, P * h : P * h + P], alowT[:, :], start=True, stop=True)
            last.then_inc(s["gates"], 1)
            pe.wait_ge(s["qk_out"], 4)
            square(first["gla_v"], 0)
            pe.wait_ge(s["v_out"], 4)
            square(first["gla_r"], 0)
            pe.wait_ge(s["r_out"], 4)
            decay(0, 256)
            turn(T_GLA, y)
            square(first["gla_o"], 0)
            turn(T_X3, x)
            mlp(1)
            turn(T_X4, x)

            for q in range(2):
                by_rows(first["mla_down"] + q, 4, 512, 4 * q, KD, [(tt, slice(0, 512), bank(tt)) for tt in range(TT)])
            by_rows(first["mla_down"] + 2, KD, M_ROPE, 0, KD, [(tt, slice(0, M_ROPE), bank(2 + tt, M_ROPE)) for tt in range(TT)])
            for tt in range(TT):
                pe.wait_ge(s["lat_done"], tt + 1)
                for q in range(4):
                    last = nc.tensor.transpose(ps[:, 4 + tt, P * q : P * q + P], latn[:, tt, P * q : P * q + P], ident[:, :])
                last.then_inc(s["lat_turned"], 1)
            for tt in range(TT):
                pe.wait_ge(s["kr_rotated"], tt + 1)
                last = nc.tensor.transpose(ps[:, 6, P * tt : P * tt + P], krdup[:, tt, :, :].rearrange("p e d -> p (e d)"), ident[:, :])
            last.then_inc(s["kr_turned"], 1)
            pe.wait_ge(s["latT_lo"], TT)
            lat_h, lat_l = xh, xl
            for c in range(2):
                n = first["mla_q"] + c
                take(n)
                w = [v.rearrange("p k (h d) -> p k h d", h=4) for v in weights(n, 2, 768)]
                if c == 1:
                    pe.wait_ge(s["qn_out"], 2)
                    pe.wait_ge(s["qr_out"], 2)
                for h in range(4):
                    for kk in range(2):
                        last = three(ps[:, h // 2, 256 * (h % 2) : 256 * (h % 2) + 256], [v[:, kk, h, 0:P] for v in w],
                                     (lat_h[:, kk, :], lat_l[:, kk, :]), kk == 0, kk == 1)
                for tt in range(TT):
                    for kk in range(2):
                        last = three(ps[:, 2 + tt, 0:256], (lat_h[:, kk, P * tt : P * tt + P], lat_l[:, kk, P * tt : P * tt + P]),
                                     [v[:, kk, :, P : P + M_ROPE] for v in w], kk == 0, kk == 1)
                last.then_inc(s["w_done"], 1)
            for c in range(2):
                n = first["mla_kv"] + c
                take(n)
                w = [v.rearrange("p k (h d) -> p k h d", h=4) for v in weights(n, 2, D)]
                pe.wait_ge(s["qn_out"], 4)
                pe.wait_ge(s["qr_out"], 4)
                if c == 1:
                    pe.wait_ge(s["kn_out"], 2)
                    pe.wait_ge(s["vM_out"], 2)
                for h in range(4):
                    for kk in range(2):
                        last = three(ps[:, h // 2, 256 * (h % 2) : 256 * (h % 2) + 256], [v[:, kk, h, 0:P] for v in w],
                                     (lat_h[:, 2 + kk, :], lat_l[:, 2 + kk, :]), kk == 0, kk == 1)
                for tt in range(TT):
                    for kk in range(2):
                        last = three(ps[:, 2 + tt, :], (lat_h[:, 2 + kk, P * tt : P * tt + P], lat_l[:, 2 + kk, P * tt : P * tt + P]),
                                     [v[:, kk, :, P:256] for v in w], kk == 0, kk == 1)
                last.then_inc(s["w_done"], 1)
            pe.wait_ge(s["latT_lo"], TT)
            for tt in range(TT):
                pe.wait_ge(s["qr_rotated"], tt + 1)
                for q in range(4):
                    last = nc.tensor.transpose(ps[:, 4 + tt, P * q : P * q + P], qrtok[:, tt, P * q : P * q + P], ident[:, :])
                last.then_inc(s["qr_turned"], 1)
            pe.wait_ge(s["qrT_done"], TT)
            pe.wait_ge(s["krT_done"], 1)
            pe.wait_ge(s["kn_out"], 4)
            pe.wait_ge(s["vM_out"], 4)

            def mla_scores(o, b, h, n):
                mm(o, qnT[:, h, b * P : b * P + P], knT[:, h, 0:n], start=True, stop=False)
                return mm(o, qrT[:, h // 2, b * P : b * P + P], krT[:, h % 2, 0:n], start=False, stop=True)

            attention(1, ATT_UNITS[1], mla_scores, lambda kt, h: vM[:, kt, P * h : P * h + P], P, 4)
            turn(T_MLA, y)
            square(first["mla_o"], 0)
            turn(T_X5, x)
            ffn(0)
            ple(0, T_X6)

            turn(T_X7, x)
            for q in range(4):
                n = first["hgrn_f"] + q
                take(n)
                columns(weights(n, KD, FG), bank(q)).then_inc(s["w_done"], 1)
            for q in range(4):
                n = first["hgrn_q"] + q
                take(n)
                columns(weights(n, KD, FG), bank(4 + q)).then_inc(s["w_done"], 1)
            pe.wait_ge(s["f_out"], 4)
            square(first["hgrn_v"], 0)
            pe.wait_ge(s["v_out"], 8)
            square(first["hgrn_gate"], 0)
            pe.wait_ge(s["r_out"], 8)
            decay(1, P)
            decay(2, P)
            turn(T_HGRN, y)
            square(first["hgrn_o"], 0)
            turn(T_X8, x)
            ffn(1)
            ple(1, T_X9)

        @block.scalar
        def _(act):
            n_step = [0]
            n_hi = [0]
            a = nc.scalar

            def step(ins):
                ins.then_inc(s["act_step"], 1)
                n_step[0] += 1
                act.wait_ge(s["act_step"], n_step[0])

            def hi_part(n):
                slot, w = n % RING, width[n]
                act.wait_ge(s[f"raw_landed{slot}"], 16 * (n // RING + 1))
                if n >= RING:
                    act.wait_ge(s["w_done"], n - RING + 1)
                a.activation(whi[:, slot, 0:w], raw[:, slot, 0:w], ACT.Copy).then_inc(s["hi_done"], 1)

            def ahead(n):
                while n_hi[0] <= min(n + 2, N_CHUNKS - 1):
                    hi_part(n_hi[0])
                    n_hi[0] += 1

            def turned(j):
                for u in range(4):
                    tt, hf = u // 2, u % 2
                    act.wait_ge(s["turned"], 4 * j + u + 1)
                    a.activation(xh[:, 4 * hf : 4 * hf + 4, P * tt : P * tt + P],
                                 bank(4 + u).rearrange("p (k n) -> p k n", k=4), ACT.Copy).then_inc(s["turn_hi"], 1)

            def mlp(layer):
                n0 = first[f"mlp{layer}"]

                def hidden(b, slot):
                    r = buf[slot // 2][:, 512 * (slot % 2) : 512 * (slot % 2) + 512]
                    a.activation(r, bank(b), ACT.Relu).then_inc(s["h_act"], 1)

                def high(slot):
                    r = buf[slot // 2][:, 512 * (slot % 2) : 512 * (slot % 2) + 512]
                    a.activation(hh[:, slot, :], r, ACT.Square).then_inc(s["h_hi"], 1)

                ahead(n0)
                act.wait_ge(s["w_done"], n0 + 1)
                hidden(4, 0)
                act.wait_ge(s["h_act"], hcount(layer, 0, 0) + 1)
                high(0)
                base = n_hi[0]
                assert base == n0 + 3
                with act.Fori(0, (MLP_GROUPS - 1) // 3) as it:
                    for j in range(3):
                        nu = n0 + 1 + 2 * j
                        for w in range(2):
                            n = nu + 2 + w
                            slot = n % RING
                            landed = act.snap(it * 32 + 16 * (n // RING + 1))
                            done = act.snap(it * 6 + (n - RING + 1))
                            act.wait_ge(s[f"raw_landed{slot}"], landed)
                            act.wait_ge(s["w_done"], done)
                            a.activation(whi[:, slot, :], raw[:, slot, :], ACT.Copy).then_inc(s["hi_done"], 1)
                            if w == 0:
                                ready = act.snap(it * 6 + (nu + 1))
                                act.wait_ge(s["w_done"], ready)
                                hidden(4 + (j + 1) % 3, (j + 1) % 3)
                                own = act.snap(it * 3 + (hcount(layer, 0, j + 1) + 1))
                                act.wait_ge(s["h_act"], own)
                                high((j + 1) % 3)
                n_hi[0] = base + 2 * (MLP_GROUPS - 1)

            def ffn(layer):
                n0 = first[f"ffn{layer}"]
                sig = lambda slot: buf[1][:, 512 * slot : 512 * slot + 512]
                prod = lambda slot: buf[1][:, 1024 + 512 * slot : 1536 + 512 * slot]

                ahead(n0)
                act.wait_ge(s["w_done"], n0 + 1)
                a.activation(sig(0), bank(4), ACT.Silu).then_inc(s["h_act"], 1)
                ahead(n0 + 1)
                act.wait_ge(s["h_prod"], FFN_GROUPS * layer + 1)
                a.activation(hh[:, 0, :], prod(0), ACT.Copy).then_inc(s["h_hi"], 1)
                base = n_hi[0]
                assert base == n0 + 4
                with act.Fori(0, (FFN_GROUPS - 1) // 2) as it:
                    for j in range(2):
                        nu = n0 + 2 + 3 * j
                        sl = (j + 1) % 2
                        for w in range(3):
                            n = nu + 2 + w
                            slot = n % RING
                            landed = act.snap(it * 32 + 16 * (n // RING + 1))
                            done = act.snap(it * 6 + (n - RING + 1))
                            act.wait_ge(s[f"raw_landed{slot}"], landed)
                            act.wait_ge(s["w_done"], done)
                            a.activation(whi[:, slot, :], raw[:, slot, :], ACT.Copy).then_inc(s["hi_done"], 1)
                            if w == 0:
                                ready = act.snap(it * 6 + (nu + 1))
                                act.wait_ge(s["w_done"], ready)
                                a.activation(sig(sl), bank(4 + 2 * sl), ACT.Silu).then_inc(s["h_act"], 1)
                            if w == 1:
                                ready = act.snap(it * 2 + (FFN_GROUPS * layer + j + 2))
                                act.wait_ge(s["h_prod"], ready)
                                a.activation(hh[:, sl, :], prod(sl), ACT.Copy).then_inc(s["h_hi"], 1)
                n_hi[0] = base + 3 * (FFN_GROUPS - 1)

            def attention(kind, units):
                n_units = len(units)
                base = kind * ATT_BASE

                def exps(u):
                    b, g = units[u]
                    n = P * (b + 1)
                    act.wait_ge(s["negmax"], base + u + 1)
                    for h in range(4):
                        v = logit[:, u % 2, n * h : n * h + n]
                        last = a.activation(v, v, ACT.Exp, bias=negmax[:, u % 2, h : h + 1], accum_out=rowsum[:, b, 4 * g + h : 4 * g + h + 1])
                    last.then_inc(s["exp_done"], 1)

                def copies(u):
                    b, g = units[u]
                    act.wait_ge(s["probs_turned"], base + u + 1)
                    if b == 0:
                        a.activation(probT[:, u % 2, 0:256], ps[:, 4, 0:256], ACT.Copy).then_inc(s["probT_act"], 1)
                    else:
                        a.activation(probT[:, u % 2, 0:512], bank(4), ACT.Copy).then_inc(s["probT_act"], 1)

                exps(0)
                for u in range(n_units):
                    if u + 1 < n_units:
                        exps(u + 1)
                    copies(u)

            def decay(c, scale):
                for lv in range(8):
                    act.wait_ge(s["diff_done"], 8 * c + lv + 1)
                    a.activation(expo[lv % 2], expo[lv % 2], ACT.Exp, scale=scale).then_inc(s["expo_done"], 1)

            def decay_squares(c, hd):
                for tt in range(TT):
                    act.wait_ge(s["decay_pv"], TT * c + tt + 1)
                    if c or tt:
                        act.wait_ge(s["ss_done"], TT * c + tt)
                    for h in range(4):
                        last = a.activation(rot4[:, h, 0:hd], decay_out(c, tt, h, hd), ACT.Square,
                                            accum_out=ss[:, tt, 4 * (c == 2) + h : 4 * (c == 2) + h + 1])
                    last.then_inc(s["ss_done"], 1)

            def log_sigmoid_tail(v, tmp):
                step(a.activation(tmp, v, ACT.Abs))
                step(a.activation(tmp, tmp, ACT.Exp, scale=-1.0))
                return a.activation(tmp, tmp, ACT.Ln, bias=1.0)

            def ple(layer, j):
                turned(j)
                n0 = first[f"ple{layer}"]
                for q in range(4):
                    ahead(n0 + q)
                act.wait_ge(s["p_turned"], layer + 1)
                a.activation(hh[:, 0, :], bank(4), ACT.Copy).then_inc(s["p_hi"], 1)
                act.wait_ge(s["w_done"], n0 + 4)
                for u in range(4):
                    a.activation(y[:, u // 2, 512 * (u % 2) : 512 * (u % 2) + 512], bank(u), ACT.Sigmoid).then_inc(s["sig_done"], 1)

            for w, (sn, cs) in enumerate(((sinA, cosA), (sinM, cosM))):
                act.wait_ge(s["angle_done"], w + 1)
                a.activation(sn[:, :, :], cs[:, :, :], ACT.Sin)
                a.activation(cs[:, :, :], cs[:, :, :], ACT.Sin, scale=0.5).then_inc(s["sines_done"], 1)
            ahead(0)
            turned(T_X0)

            for q in range(4):
                ahead(first["dsa_kvi"] + q)
            act.wait_ge(s["w_done"], first["dsa_kvi"] + 4)
            for c in range(2):
                a.activation(kvi[:, 0, 512 * c : 512 * c + 512], bank(c), ACT.Copy).then_inc(s["kvi_act"], 1)
            ahead(first["dsa_small"])
            act.wait_ge(s["w_done"], first["dsa_small"] + 1)
            for tt in range(TT):
                a.activation(ikw[:, tt, :], bank(4 + tt, A_SMALL), ACT.Copy).then_inc(s["small_out"], 1)
            ahead(first["dsa_q"] + 1)
            for tt in range(TT):
                act.wait_ge(s["index_turned"], tt + 1)
                a.activation(iqT[:, :, P * tt : P * tt + P], bank(6 + tt).rearrange("p (k n) -> p k n", k=4), ACT.Copy).then_inc(s["indexT_done"], 1)
                for e in range(2):
                    r = slice(64 * e, 64 * e + 64)
                    last = a.activation(ikT[r, e, P * tt : P * tt + P], ps[r, 4 + tt, 0:P], ACT.Copy)
                last.then_inc(s["indexT_done"], 1)
            for u, (b, hs) in enumerate(INDEX_UNITS):
                act.wait_ge(s["index_scores"], u + 1)
                if u >= 4:
                    act.wait_ge(s["index_added"], u - 3)
                a.activation(relu_s[:, u % 4, :], bank(4 + u % 4), ACT.Relu, scale=float(A_HD**-0.5)).then_inc(s["index_relu"], 1)
            ahead(first["dsa_q"] + 2)
            ahead(first["dsa_q"] + 3)
            act.wait_ge(s["w_done"], first["dsa_q"] + 4)
            for u in range(4):
                a.activation(qtok[:, u // 2, 512 * (u % 2) : 512 * (u % 2) + 512], bank(u), ACT.Copy).then_inc(s["q_out"], 1)
            for tt in range(TT):
                act.wait_ge(s["k_turned"], tt + 1)
                for e in range(2):
                    r = slice(64 * e, 64 * e + 64)
                    last = a.activation(kT[r, :, e, P * tt : P * tt + P], ps[r, 4 + tt, :].rearrange("p (k n) -> p k n", k=4), ACT.Copy)
                last.then_inc(s["kT_done"], 1)
            for u in range(4):
                tt, hf = u // 2, u % 2
                act.wait_ge(s["q_turned"], u + 1)
                a.activation(qT[:, 4 * hf : 4 * hf + 4, P * tt : P * tt + P], bank((6 if tt == 0 else 4) + hf).rearrange("p (k n) -> p k n", k=4),
                             ACT.Copy).then_inc(s["qT_done"], 1)
            attention(0, ATT_UNITS[0])
            turned(T_DSA)
            for q in range(4):
                ahead(first["dsa_o"] + q)
            turned(T_X1)
            mlp(0)
            ahead(first["gla_qk"] - 1)
            turned(T_X2)

            for q in range(4):
                n = first["gla_qk"] + q
                ahead(n)
                act.wait_ge(s["w_done"], n + 1)
                dst = (q4[0] if q < 2 else k4[0])[:, 2 * (q % 2) : 2 * (q % 2) + 2, :].rearrange("p h n -> p (h n)")
                a.activation(dst, bank(q), ACT.Copy, scale=float(P**-0.5) if q < 2 else 1.0).then_inc(s["qk_out"], 1)
            ahead(first["gla_low"])
            act.wait_ge(s["w_done"], first["gla_low"] + 1)
            a.activation(alow[:, :, :], ps[:, 4:6, 0:B_RANK], ACT.Copy).then_inc(s["low_out"], 1)
            act.wait_ge(s["low_turned"], 1)
            a.activation(alowT[:, :], ps[0:B_RANK, 6, 0:SEQ], ACT.Copy).then_inc(s["lowT_done"], 1)
            act.wait_ge(s["gates"], 1)
            for h in range(4):
                last = a.activation(expo[0][:, 256 * h : 256 * h + 256], ps[:, 6 + h // 2, 256 * (h % 2) : 256 * (h % 2) + 256],
                                    ACT.Identity, bias=vcol[:, V_BA + h : V_BA + h + 1])
            step(last)
            ahead(first["gla_v"])
            log_sigmoid_tail(expo[0], expo[1]).then_inc(s["tail_done"], 1)
            for q in range(4):
                ahead(first["gla_v"] + q)
            act.wait_ge(s["w_done"], first["gla_v"] + 4)
            for u in range(4):
                a.activation(vtok[:, u // 2, 512 * (u % 2) : 512 * (u % 2) + 512], bank(u), ACT.Copy).then_inc(s["v_out"], 1)
            for q in range(4):
                ahead(first["gla_r"] + q)
            act.wait_ge(s["w_done"], first["gla_r"] + 4)
            for u in range(4):
                a.activation(gate[:, u // 2, 512 * (u % 2) : 512 * (u % 2) + 512], bank(u), ACT.Silu).then_inc(s["r_out"], 1)
            decay(0, 1.0 / 16.0)
            decay_squares(0, 256)
            turned(T_GLA)
            for q in range(4):
                ahead(first["gla_o"] + q)
            turned(T_X3)
            mlp(1)
            ahead(first["mla_down"] - 1)
            turned(T_X4)

            for q in range(3):
                ahead(first["mla_down"] + q)
            act.wait_ge(s["w_done"], first["mla_down"] + 3)
            for tt in range(TT):
                for w in range(2):
                    last = a.activation(rot4[:, 2 * tt + w, :], ps[:, tt, 256 * w : 256 * w + 256], ACT.Square, accum_out=ss[:, tt, w : w + 1])
                last.then_inc(s["lat_squares"], 1)
                a.activation(krtok[:, tt, :], bank(2 + tt, M_ROPE), ACT.Copy).then_inc(s["kr_out"], 1)
            for tt in range(TT):
                act.wait_ge(s["latT_full"], tt + 1)
                a.activation(xh[:, 0:4, P * tt : P * tt + P], lat[:, tt, :].rearrange("p (k n) -> p k n", k=4), ACT.Copy).then_inc(s["latT_hi"], 1)
            act.wait_ge(s["kr_turned"], 1)
            for e in range(2):
                r = slice(64 * e, 64 * e + 64)
                last = a.activation(krT[r, e, :], ps[r, 6, 0:SEQ], ACT.Copy)
            last.then_inc(s["krT_done"], 1)
            for c in range(2):
                n = first["mla_q"] + c
                ahead(n)
                act.wait_ge(s["w_done"], n + 1)
                for u in range(2):
                    a.activation(qnT[:, 4 * c + 2 * u : 4 * c + 2 * u + 2, :].rearrange("p h n -> p (h n)"), bank(u), ACT.Copy).then_inc(s["qn_out"], 1)
            for c in range(2):
                n = first["mla_kv"] + c
                ahead(n)
                act.wait_ge(s["w_done"], n + 1)
                for u in range(2):
                    a.activation(knT[:, 4 * c + 2 * u : 4 * c + 2 * u + 2, :].rearrange("p h n -> p (h n)"), bank(u), ACT.Copy).then_inc(s["kn_out"], 1)
            for tt in range(TT):
                act.wait_ge(s["qr_turned"], tt + 1)
                a.activation(qrT[:, :, P * tt : P * tt + P], bank(4 + tt).rearrange("p (k n) -> p k n", k=4), ACT.Copy).then_inc(s["qrT_done"], 1)
            attention(1, ATT_UNITS[1])
            turned(T_MLA)
            for q in range(4):
                ahead(first["mla_o"] + q)
            turned(T_X5)
            ffn(0)
            ahead(first["ple0"] - 1)
            ple(0, T_X6)

            act.wait_ge(s["lb_diff"], 1)
            a.activation(lbv[:, 1:3, :], lbv[:, 1:3, :], ACT.Exp).then_inc(s["lb_exp"], 1)
            act.wait_ge(s["lb_done"], 1)
            a.activation(lbv[:, 4:6, :], lbv[:, 4:6, :], ACT.Ln).then_inc(s["lb_ln"], 1)
            ahead(first["hgrn_f"] - 1)
            turned(T_X7)
            for q in range(4):
                n = first["hgrn_f"] + q
                ahead(n)
                act.wait_ge(s["w_done"], n + 1)
                a.activation(expo[q // 2][:, 512 * (q % 2) : 512 * (q % 2) + 512], bank(q), ACT.Copy).then_inc(s["f_out"], 1)
            act.wait_ge(s["f_out"], 4)
            for w in range(2):
                log_sigmoid_tail(expo[w], zed[w]).then_inc(s["tail_done"], 1)
            for q in range(4):
                n = first["hgrn_q"] + q
                ahead(n)
                act.wait_ge(s["w_done"], n + 1)
                a.activation(q4[q // 2][:, 2 * (q % 2) : 2 * (q % 2) + 2, :].rearrange("p h n -> p (h n)"), bank(4 + q), ACT.Silu).then_inc(s["qk_out"], 1)
            for w in range(2):
                act.wait_ge(s["nf_done"], w + 1)
                k = k4[w].rearrange("p h n -> p (h n)")
                a.activation(k, k, ACT.Exp).then_inc(s["k_exp"], 1)
                act.wait_ge(s["gap_done"], w + 1)
                log_sigmoid_tail(g4[w].rearrange("p h n -> p (h n)"), zed[w]).then_inc(s["tail_done"], 1)
            for q in range(4):
                ahead(first["hgrn_v"] + q)
            act.wait_ge(s["w_done"], first["hgrn_v"] + 4)
            for u in range(4):
                a.activation(vtok[:, u // 2, 512 * (u % 2) : 512 * (u % 2) + 512], bank(u), ACT.Copy).then_inc(s["v_out"], 1)
            for q in range(4):
                ahead(first["hgrn_gate"] + q)
            act.wait_ge(s["w_done"], first["hgrn_gate"] + 4)
            for u in range(4):
                a.activation(gate[:, u // 2, 512 * (u % 2) : 512 * (u % 2) + 512], bank(u), ACT.Silu).then_inc(s["r_out"], 1)
            decay(1, 1.0)
            decay_squares(1, P)
            decay(2, 1.0)
            decay_squares(2, P)
            turned(T_HGRN)
            for q in range(4):
                ahead(first["hgrn_o"] + q)
            turned(T_X8)
            ffn(1)
            ahead(first["ple1"] - 1)
            ple(1, T_X9)

        @block.vector
        def _(dve):
            n_step = [0]
            n_lo = [0]
            v = nc.vector

            def step(ins):
                ins.then_inc(s["dve_step"], 1)
                n_step[0] += 1
                dve.wait_ge(s["dve_step"], n_step[0])

            def lo_part(n):
                slot, w = n % RING, width[n]
                dve.wait_ge(s["hi_done"], n + 1)
                v.tensor_tensor(wlo[:, slot, 0:w], raw[:, slot, 0:w], whi[:, slot, 0:w].bitcast(F32), ALU.subtract).then_inc(s["lo_done"], 1)

            def ahead(n):
                while n_lo[0] <= min(n + 2, N_CHUNKS - 1):
                    lo_part(n_lo[0])
                    n_lo[0] += 1

            def turned(j):
                for u in range(4):
                    tt, hf = u // 2, u % 2
                    dve.wait_ge(s["turn_hi"], 4 * j + u + 1)
                    hi = xh[:, 4 * hf : 4 * hf + 4, P * tt : P * tt + P]
                    lo = xl[:, 4 * hf : 4 * hf + 4, P * tt : P * tt + P]
                    v.tensor_tensor(lo, bank(4 + u).rearrange("p (k n) -> p k n", k=4), hi.bitcast(F32), ALU.subtract).then_inc(s["turn_lo"], 1)

            def rsqrt(o, val, tmp):
                step(v.tensor_scalar(o.bitcast(I32), val.bitcast(I32), 1, None, ALU.logical_shift_right))
                step(v.tensor_scalar(o.bitcast(I32), o.bitcast(I32), -1.0, RSQRT_SEED, ALU.mult, ALU.add))
                for _ in range(3):
                    step(v.tensor_tensor(tmp, o, o, ALU.mult))
                    step(v.tensor_tensor(tmp, tmp, val, ALU.mult))
                    step(v.tensor_scalar(tmp, tmp, -0.5, 1.5, ALU.mult, ALU.add))
                    step(v.tensor_tensor(o, o, tmp, ALU.mult))

            def layer_norm(i, n_last, j):
                dve.wait_ge(s["w_done"], n_last + 1)
                dve.wait_ge(s["ln_landed"], 32 * (i + 1))
                for u in range(4):
                    tt, cs = u // 2, slice(512 * (u % 2), 512 * (u % 2) + 512)
                    v.scalar_tensor_tensor(y[:, tt, cs], x[:, tt, cs], ALPHA, bank(u), ALU.mult, ALU.add).then_inc(s["resid"], 1)
                for u in range(4):
                    tt, cs = u // 2, slice(512 * (u % 2), 512 * (u % 2) + 512)
                    dve.wait_ge(s["resid"], 4 * i + u + 1)
                    last = v.bn_stats(stats[:, tt, u % 2, :], y[:, tt, cs])
                step(last)
                for tt in range(TT):
                    last = v.bn_aggr(mv[:, tt, :], stats[:, tt, :, :].rearrange("p a b -> p (a b)"))
                step(last)
                step(v.tensor_scalar(small[:, 0:2], mv[:, :, 1], LN_EPS, None, ALU.add))
                rsqrt(small[:, 2:4], small[:, 0:2], small[:, 4:6])
                for tt in range(TT):
                    step(v.scalar_tensor_tensor(y[:, tt, :], y[:, tt, :], mv[:, tt, 0:1], lnw[:, 0, :], ALU.subtract, ALU.mult))
                    v.scalar_tensor_tensor(x[:, tt, :], y[:, tt, :], small[:, 2 + tt : 3 + tt], lnw[:, 1, :],
                                           ALU.mult, ALU.add).then_inc(s["src_ready"], 1)

            def mlp(layer):
                n0 = first[f"mlp{layer}"]

                def full(slot):
                    r = buf[slot // 2][:, 512 * (slot % 2) : 512 * (slot % 2) + 512]
                    return v.tensor_tensor(buf[2][:, 512 * slot : 512 * slot + 512], r, r, ALU.mult).then_inc(s["h_full"], 1)

                def low(slot):
                    v.tensor_tensor(hl[:, slot, :], buf[2][:, 512 * slot : 512 * slot + 512], hh[:, slot, :].bitcast(F32), ALU.subtract).then_inc(s["h_lo"], 1)

                ahead(n0)
                dve.wait_ge(s["h_act"], hcount(layer, 0, 0) + 1)
                full(0)
                dve.wait_ge(s["h_hi"], hcount(layer, 0, 0) + 1)
                dve.wait_ge(s["h_full"], MLP_GROUPS * layer + 1)
                low(0)
                base = n_lo[0]
                with dve.Fori(0, (MLP_GROUPS - 1) // 3) as it:
                    for j in range(3):
                        nu = n0 + 1 + 2 * j
                        for w in range(2):
                            n = nu + 2 + w
                            slot = n % RING
                            ready = dve.snap(it * 6 + (n + 1))
                            dve.wait_ge(s["hi_done"], ready)
                            v.tensor_tensor(wlo[:, slot, :], raw[:, slot, :], whi[:, slot, :].bitcast(F32), ALU.subtract).then_inc(s["lo_done"], 1)
                            if w == 0:
                                sl = (j + 1) % 3
                                ready = dve.snap(it * 3 + (hcount(layer, 0, j + 1) + 1))
                                dve.wait_ge(s["h_act"], ready)
                                full(sl)
                                ready = dve.snap(it * 3 + (hcount(layer, 0, j + 1) + 1))
                                own = dve.snap(it * 3 + (MLP_GROUPS * layer + j + 2))
                                dve.wait_ge(s["h_hi"], ready)
                                dve.wait_ge(s["h_full"], own)
                                low(sl)
                n_lo[0] = base + 2 * (MLP_GROUPS - 1)

            def ffn(layer):
                n0 = first[f"ffn{layer}"]
                sig = lambda slot: buf[1][:, 512 * slot : 512 * slot + 512]
                prod = lambda slot: buf[1][:, 1024 + 512 * slot : 1536 + 512 * slot]

                ahead(n0)
                ahead(n0 + 1)
                dve.wait_ge(s["h_act"], hcount(layer, 1, 0) + 1)
                dve.wait_ge(s["w_done"], n0 + 2)
                v.tensor_tensor(prod(0), sig(0), bank(5), ALU.mult).then_inc(s["h_prod"], 1)
                dve.wait_ge(s["h_hi"], hcount(layer, 1, 0) + 1)
                v.tensor_tensor(hl[:, 0, :], prod(0), hh[:, 0, :].bitcast(F32), ALU.subtract).then_inc(s["h_lo"], 1)
                base = n_lo[0]
                with dve.Fori(0, (FFN_GROUPS - 1) // 2) as it:
                    for j in range(2):
                        nu = n0 + 2 + 3 * j
                        sl = (j + 1) % 2
                        for w in range(3):
                            n = nu + 2 + w
                            slot = n % RING
                            ready = dve.snap(it * 6 + (n + 1))
                            dve.wait_ge(s["hi_done"], ready)
                            v.tensor_tensor(wlo[:, slot, :], raw[:, slot, :], whi[:, slot, :].bitcast(F32), ALU.subtract).then_inc(s["lo_done"], 1)
                            if w == 1:
                                a_ready = dve.snap(it * 2 + (hcount(layer, 1, j + 1) + 1))
                                w_ready = dve.snap(it * 6 + (nu + 2))
                                dve.wait_ge(s["h_act"], a_ready)
                                dve.wait_ge(s["w_done"], w_ready)
                                v.tensor_tensor(prod(sl), sig(sl), bank(5 + 2 * sl), ALU.mult).then_inc(s["h_prod"], 1)
                                ready = dve.snap(it * 2 + (hcount(layer, 1, j + 1) + 1))
                                dve.wait_ge(s["h_hi"], ready)
                                v.tensor_tensor(hl[:, sl, :], prod(sl), hh[:, sl, :].bitcast(F32), ALU.subtract).then_inc(s["h_lo"], 1)
                n_lo[0] = base + 3 * (FFN_GROUPS - 1)

            def attention(kind, units, bias_of, scale, heads):
                n_units = len(units)
                base = kind * ATT_BASE
                hd = D // heads

                def prepare(u):
                    b, g = units[u]
                    n = P * (b + 1)
                    dve.wait_ge(s["logits"], base + u + 1)
                    if u >= 2:
                        dve.wait_ge(s["probs_turned"], base + u - 1)
                    src = banks(2 * (u % 2), 2)[:, 0 : 4 * n].rearrange("p (h n) -> p h n", h=4)
                    dst = logit[:, u % 2, 0 : 4 * n].rearrange("p (h n) -> p h n", h=4)
                    bb = bias_of(b)[:, 0:n].unsqueeze(1).broadcast_to([P, 4, n])
                    v.scalar_tensor_tensor(dst, src, scale, bb, ALU.mult, ALU.add).then_inc(s["logit_read"], 1)
                    dve.wait_ge(s["logit_read"], base + u + 1)
                    v.tensor_reduce(negmax[:, u % 2, :], dst, AX_X, ALU.max, negate=True).then_inc(s["negmax"], 1)

                def copies(u):
                    b, g = units[u]
                    dve.wait_ge(s["probT_act"], base + u + 1)
                    if b == 0:
                        v.tensor_copy(probT[:, u % 2, 256:512], ps[:, 4, 256:512]).then_inc(s["probT_dve"], 1)
                    else:
                        v.tensor_copy(probT[:, u % 2, 512:1024], bank(5)).then_inc(s["probT_dve"], 1)

                def output(b, j):
                    step(v.reciprocal(rinv[:, b, 0:heads], rowsum[:, b, 0:heads]))
                    dve.wait_ge(s["att_pv"], base + n_units // 2 * (b + 1))
                    v.tensor_tensor(y[:, b, :].rearrange("p (h d) -> p h d", h=heads), banks(6, 2).rearrange("p (h d) -> p h d", h=heads),
                                    rinv[:, b, 0:heads].unsqueeze(2).broadcast_to([P, heads, hd]), ALU.mult).then_inc(s["src_ready"], 1)

                prepare(0)
                for u in range(n_units):
                    if u + 1 < n_units:
                        prepare(u + 1)
                    copies(u)
                    if u == n_units // 2 - 1:
                        output(0, 0)
                output(1, 0)

            def decay(c, w):
                def blocks(ap, lv):
                    return ap.rearrange("p (b e n) -> p b e n", e=2, n=LEVELS[lv])

                G = g4[w].rearrange("p h n -> p (h n)")
                Q = q4[w].rearrange("p h n -> p (h n)")
                K = k4[w].rearrange("p h n -> p (h n)")

                def diff(lv):
                    m = LEVELS[lv]
                    nb = 1024 // (2 * m)
                    gb, eb = blocks(G, lv), blocks(expo[lv % 2], lv)
                    ref = gb[:, :, 0, m - 1 : m].broadcast_to([P, nb, m])
                    v.tensor_tensor(eb[:, :, 0, :], ref, gb[:, :, 0, :], ALU.subtract)
                    v.tensor_tensor(eb[:, :, 1, :], gb[:, :, 1, :], ref, ALU.subtract).then_inc(s["diff_done"], 1)

                def operand(lv):
                    dve.wait_ge(s["expo_done"], 8 * c + lv + 1)
                    if lv >= 2:
                        dve.wait_ge(s["level_done"], 9 * c + lv - 1)
                    eb, zb = blocks(expo[lv % 2], lv), blocks(zed[lv % 2], lv)
                    v.tensor_tensor(zb[:, :, 0, :], blocks(K, lv)[:, :, 0, :], eb[:, :, 0, :], ALU.mult)
                    v.tensor_tensor(zb[:, :, 1, :], blocks(Q, lv)[:, :, 1, :], eb[:, :, 1, :], ALU.mult).then_inc(s["zed_done"], 1)

                def pick(lv):
                    dve.wait_ge(s["level_done"], 9 * c + lv + 1)
                    if lv >= 2:
                        dve.wait_ge(s["level_read"], 9 * c + lv)
                    if lv == 0:
                        v.tensor_copy(att[:, :, 2, :], bank(4).rearrange("p (h n) -> p h n", h=4)).then_inc(s["level_read"], 1)
                        return
                    b0 = 4 + 2 * (lv % 2)
                    for hp in range(2):
                        src = ps[:, b0 + hp, :].rearrange("p (h t n) -> p h t n", h=2, t=2)
                        for h in range(2):
                            mk = masks[:, lv - 1, :].bitcast(I32).unsqueeze(1).broadcast_to([P, 2, P])
                            last = v.copy_predicated(att[:, 2 * hp + h, 0:2, :], mk, src[:, h, :, :])
                    last.then_inc(s["level_read"], 1)

                diff(0)
                diff(1)
                step(v.memset(att[:, :, 0:2, :], 0.0))
                for lv in range(8):
                    operand(lv)
                    if lv + 2 < 8:
                        dve.wait_ge(s["zed_done"], 8 * c + lv + 1)
                        diff(lv + 2)
                    if lv >= 1:
                        pick(lv - 1)
                pick(7)
                pick(8)

            def decay_output(c, hd, j, last_set):
                h0 = 4 * (c == 2)
                for tt in range(TT):
                    dve.wait_ge(s["ss_done"], TT * c + tt + 1)
                step(v.tensor_scalar(small[:, 16:24].rearrange("p (t h) -> p t h", t=TT), ss[:, :, h0 : h0 + 4], 1.0 / hd, RMS_EPS, ALU.mult, ALU.add))
                rsqrt(small[:, 24:32], small[:, 16:24], small[:, 32:40])
                for tt in range(TT):
                    for h in range(4):
                        cs = slice(vcol0(c) + hd * h, vcol0(c) + hd * h + hd)
                        col = 24 + 4 * tt + h
                        last = v.scalar_tensor_tensor(y[:, tt, cs], decay_out(c, tt, h, hd), small[:, col : col + 1], gate[:, tt, cs], ALU.mult, ALU.mult)
                    if last_set:
                        last.then_inc(s["src_ready"], 1)

            def gated(n_gate, n_landed):
                dve.wait_ge(s["r_out"], n_gate)
                dve.wait_ge(s["gn_landed"], n_landed)
                for tt in range(TT):
                    last = v.tensor_tensor(gate[:, tt, :], gate[:, tt, :], gn, ALU.mult)
                step(last)

            def ple(layer, j):
                turned(j)
                n0 = first[f"ple{layer}"]
                for q in range(4):
                    ahead(n0 + q)
                dve.wait_ge(s["p_hi"], layer + 1)
                v.tensor_tensor(hl[:, 0, :], bank(4), hh[:, 0, :].bitcast(F32), ALU.subtract).then_inc(s["p_lo"], 1)
                dve.wait_ge(s["w_done"], n0 + 5)
                dve.wait_ge(s["sig_done"], 4 * layer + 4)
                for u in range(4):
                    tt, cs = u // 2, slice(512 * (u % 2), 512 * (u % 2) + 512)
                    step(v.tensor_tensor(y[:, tt, cs], y[:, tt, cs], bank(4 + u), ALU.mult))
                    last = v.tensor_tensor(x[:, tt, cs], x[:, tt, cs], y[:, tt, cs], ALU.add)
                    if u % 2:
                        last.then_inc(s["src_ready" if layer == 0 else "out_ready"], 1)

            dve.wait_ge(s["pos_landed"], 32)
            dve.wait_ge(s["inv_done"], 1)
            step(v.tensor_copy(posf[:, :, :], posi[:, :, :]))
            for w, (sn, cs, c0, n) in enumerate(((sinA, cosA, 0, ROT), (sinM, cosM, ROT, M_HALF))):
                for tt in range(TT):
                    last = v.tensor_scalar(cs[:, tt, :], inv[:, c0 : c0 + n], posf[:, w, tt : tt + 1], None, ALU.mult)
                step(last)
                step(v.tensor_scalar(sn[:, :, :], cs[:, :, :], 1.0 / TWO_PI, MAGIC, ALU.mult, ALU.add))
                step(v.tensor_scalar(sn[:, :, :], sn[:, :, :], -MAGIC, None, ALU.add))
                for part in (PI_A, PI_B, PI_C):
                    step(v.scalar_tensor_tensor(cs[:, :, :], sn[:, :, :], -part, cs[:, :, :], ALU.mult, ALU.add))
                v.tensor_scalar(cs[:, :, :], cs[:, :, :], PI_MAX, -PI_MAX, ALU.min, ALU.max).then_inc(s["angle_done"], 1)
            for w, cs in enumerate((cosA, cosM)):
                dve.wait_ge(s["sines_done"], w + 1)
                step(v.tensor_tensor(cs[:, :, :], cs[:, :, :], cs[:, :, :], ALU.mult))
                last = v.tensor_scalar(cs[:, :, :], cs[:, :, :], -2.0, 1.0, ALU.mult, ALU.add)
            last.then_inc(s["tables_done"], 1)
            ahead(0)
            turned(T_X0)
            dve.wait_ge(s["vrow_turned"], 1)
            v.tensor_copy(vcol[:, :], ps[:, 4, 0:V_ROWS]).then_inc(s["vcol_done"], 1)
            dve.wait_ge(s["vcol_done"], 1)

            for q in range(4):
                ahead(first["dsa_kvi"] + q)
            dve.wait_ge(s["w_done"], first["dsa_kvi"] + 4)
            for c in range(2):
                v.tensor_copy(kvi[:, 1, 512 * c : 512 * c + 512], bank(2 + c)).then_inc(s["kvi_dve"], 1)
            ahead(first["dsa_small"])
            ahead(first["dsa_q"] + 1)
            dve.wait_ge(s["index_rotated"], TT)
            for u, (b, hs) in enumerate(INDEX_UNITS):
                dve.wait_ge(s["index_relu"], u + 1)
                n = P * (b + 1)
                for i, h in enumerate(hs):
                    w = ikw[:, b, A_HD + h : A_HD + h + 1]
                    rs = relu_s[:, u % 4, n * i : n * i + n]
                    if h == 0:
                        if b == 0:
                            step(v.memset(score[:, 0, P:SEQ], 0.0))
                        ins = v.tensor_scalar(score[:, b, 0:n], rs, w, None, ALU.mult)
                    else:
                        ins = v.scalar_tensor_tensor(score[:, b, 0:n], rs, w, score[:, b, 0:n], ALU.mult, ALU.add)
                    if i == len(hs) - 1:
                        ins.then_inc(s["index_added"], 1)
                        dve.wait_ge(s["index_added"], u + 1)
                    else:
                        step(ins)
            ahead(first["dsa_q"] + 2)
            ahead(first["dsa_q"] + 3)
            dve.wait_ge(s["score_masked"], TT)
            for r in range(TOPK // 8):
                for b in range(TT):
                    ins = v.max(top8[:, b, :], work[:, b, r % 2, :])
                step(ins)
                for b in range(TT):
                    ins = v.match_replace(work[:, b, 1 - r % 2, :], top8[:, b, :], work[:, b, r % 2, :], TAKEN)
                step(ins)
            for b in range(TT):
                v.tensor_scalar(work[:, b, 1, :], work[:, b, 0, :], 1.05 * NOT_CAUSAL, MASKED, ALU.is_gt, ALU.mult).then_inc(s["chosen"], 1)
            dve.wait_ge(s["bias_done"], TT)
            attention(0, ATT_UNITS[0], lambda b: bias[:, b, :], float(A_HD**-0.5), A_HEADS)
            turned(T_DSA)
            for q in range(4):
                ahead(first["dsa_o"] + q)
            layer_norm(0, first["dsa_o"] + 3, T_X1)
            turned(T_X1)
            mlp(0)
            ahead(first["gla_qk"] - 1)
            layer_norm(1, first["gla_qk"] - 1, T_X2)
            turned(T_X2)

            for q in range(4):
                ahead(first["gla_qk"] + q)
            ahead(first["gla_low"])
            ahead(first["gla_v"])
            dve.wait_ge(s["tail_done"], 1)
            step(v.scalar_tensor_tensor(expo[1], expo[0], 0.0, expo[1], ALU.min, ALU.subtract))
            step(v.memset(zed[0][:, 0:SEQ], 1.0))
            for h in range(4):
                last = v.tensor_tensor_scan(g4[0][:, h, :], zed[0][:, 0:SEQ], expo[1][:, 256 * h : 256 * h + 256], 0.0, ALU.mult, ALU.add)
            step(last)
            for q in range(4):
                ahead(first["gla_v"] + q)
            for q in range(4):
                ahead(first["gla_r"] + q)
            dve.wait_ge(s["masks_done"], 1)
            dve.wait_ge(s["qk_out"], 4)
            decay(0, 0)
            gated(4, 64)
            decay_output(0, 256, T_GLA, True)
            turned(T_GLA)
            for q in range(4):
                ahead(first["gla_o"] + q)
            layer_norm(2, first["gla_o"] + 3, T_X3)
            turned(T_X3)
            mlp(1)
            ahead(first["mla_down"] - 1)
            layer_norm(3, first["mla_down"] - 1, T_X4)
            turned(T_X4)

            for q in range(3):
                ahead(first["mla_down"] + q)
            dve.wait_ge(s["lat_squares"], TT)
            step(v.tensor_scalar(small[:, 16:20].rearrange("p (t w) -> p t w", t=TT), ss[:, :, 0:2], 1.0 / 256.0, RMS_EPS, ALU.mult, ALU.add))
            rsqrt(small[:, 24:28], small[:, 16:20], small[:, 32:36])
            for tt in range(TT):
                for w in range(2):
                    last = v.tensor_scalar(latn[:, tt, 256 * w : 256 * w + 256], ps[:, tt, 256 * w : 256 * w + 256],
                                           small[:, 24 + 2 * tt + w : 25 + 2 * tt + w], None, ALU.mult)
                last.then_inc(s["lat_done"], 1)
            for tt in range(TT):
                dve.wait_ge(s["lat_turned"], tt + 1)
                v.tensor_tensor(lat[:, tt, :].rearrange("p (k n) -> p k n", k=4), bank(4 + tt).rearrange("p (k n) -> p k n", k=4),
                                vcol[:, V_QN : V_QN + 4].unsqueeze(2).broadcast_to([P, 4, P]), ALU.mult).then_inc(s["latT_full"], 1)
            for tt in range(TT):
                dve.wait_ge(s["latT_hi"], tt + 1)
                dve.wait_ge(s["latT_full"], tt + 1)
                v.tensor_tensor(xl[:, 0:4, P * tt : P * tt + P], lat[:, tt, :].rearrange("p (k n) -> p k n", k=4),
                                xh[:, 0:4, P * tt : P * tt + P].bitcast(F32), ALU.subtract).then_inc(s["latT_lo"], 1)
            for c in range(2):
                n = first["mla_q"] + c
                ahead(n)
                dve.wait_ge(s["w_done"], n + 1)
                for tt in range(TT):
                    v.tensor_copy(qrtok[:, tt, 256 * c : 256 * c + 256], ps[:, 2 + tt, 0:256]).then_inc(s["qr_out"], 1)
            for c in range(2):
                n = first["mla_kv"] + c
                ahead(n)
                dve.wait_ge(s["w_done"], n + 1)
                for tt in range(TT):
                    v.tensor_copy(vM[:, tt, 512 * c : 512 * c + 512], bank(2 + tt)).then_inc(s["vM_out"], 1)
            dve.wait_ge(s["causal_done"], 1)
            attention(1, ATT_UNITS[1], lambda b: causal[:, b, :], M_SCALE, M_HEADS)
            turned(T_MLA)
            for q in range(4):
                ahead(first["mla_o"] + q)
            layer_norm(4, first["mla_o"] + 3, T_X5)
            turned(T_X5)
            ffn(0)
            ahead(first["ple0"] - 1)
            layer_norm(5, first["ple0"] - 1, T_X6)
            ple(0, T_X6)

            l0, l1 = vcol[:, V_LB : V_LB + 8], vcol[:, V_LB + 8 : V_LB + 16]
            mx, e0, e1, sm, c1, a1, ga, one = (lbv[:, i, :] for i in range(8))
            step(v.tensor_tensor(mx, l0, l1, ALU.max))
            v.tensor_tensor(e0, l0, mx, ALU.subtract)
            v.tensor_tensor(e1, l1, mx, ALU.subtract).then_inc(s["lb_diff"], 1)
            dve.wait_ge(s["lb_exp"], 1)
            step(v.tensor_tensor(sm, e0, e1, ALU.add))
            step(v.reciprocal(sm, sm))
            v.tensor_tensor(e0, e0, sm, ALU.mult)
            step(v.tensor_tensor(e1, e1, sm, ALU.mult))
            step(v.tensor_tensor(e1, e0, e1, ALU.add))
            step(v.tensor_tensor(e1, e1, e0, ALU.subtract))
            step(v.tensor_scalar(one, e1, -1.0, 1.0, ALU.mult, ALU.add))
            v.tensor_scalar(c1, one, LN_FLOOR, None, ALU.max)
            v.tensor_scalar(a1, e1, LN_FLOOR, None, ALU.max).then_inc(s["lb_done"], 1)
            dve.wait_ge(s["lb_ln"], 1)
            step(v.tensor_tensor(ga, c1, a1, ALU.subtract))
            ahead(first["hgrn_f"] - 1)
            turned(T_X7)
            for q in range(4):
                ahead(first["hgrn_f"] + q)

            def per_head(col, w):
                return col[:, 4 * w : 4 * w + 4].unsqueeze(2).broadcast_to([P, 4, SEQ])

            heads4 = lambda ap: ap.rearrange("p (h n) -> p h n", h=4)
            for w in range(2):
                dve.wait_ge(s["tail_done"], 2 + w)
                step(v.scalar_tensor_tensor(zed[w], expo[w], 0.0, zed[w], ALU.min, ALU.subtract))
                v.tensor_tensor(k4[w], heads4(zed[w]), heads4(expo[w]), ALU.subtract).then_inc(s["nf_done"], 1)
                v.tensor_tensor(g4[w], heads4(zed[w]), per_head(ga, w), ALU.add).then_inc(s["gap_done"], 1)
            for q in range(4):
                ahead(first["hgrn_q"] + q)
            for w in range(2):
                dve.wait_ge(s["k_exp"], w + 1)
                v.tensor_tensor(k4[w], k4[w], per_head(one, w), ALU.mult)
                dve.wait_ge(s["tail_done"], 4 + w)
                step(v.scalar_tensor_tensor(zed[w], g4[w].rearrange("p h n -> p (h n)"), 0.0, zed[w], ALU.max, ALU.add))
                step(v.tensor_tensor(heads4(zed[w]), heads4(zed[w]), per_head(a1, w), ALU.add))
            step(v.memset(expo[0][:, 0:SEQ], 1.0))
            for w in range(2):
                for h in range(4):
                    last = v.tensor_tensor_scan(g4[w][:, h, :], expo[0][:, 0:SEQ], zed[w][:, 256 * h : 256 * h + 256], 0.0, ALU.mult, ALU.add)
            step(last)
            for q in range(4):
                ahead(first["hgrn_v"] + q)
            for q in range(4):
                ahead(first["hgrn_gate"] + q)
            dve.wait_ge(s["qk_out"], 8)
            decay(1, 0)
            gated(8, 80)
            decay_output(1, P, T_HGRN, False)
            decay(2, 1)
            decay_output(2, P, T_HGRN, True)
            turned(T_HGRN)
            for q in range(4):
                ahead(first["hgrn_o"] + q)
            layer_norm(6, first["hgrn_o"] + 3, T_X8)
            turned(T_X8)
            ffn(1)
            ahead(first["ple1"] - 1)
            layer_norm(7, first["ple1"] - 1, T_X9)
            ple(1, T_X9)


INDEX_UNITS = [(0, [0, 1, 2, 3]), (0, [4, 5, 6, 7])] + [(1, [2 * i, 2 * i + 1]) for i in range(4)]
ATT_UNITS = [[(b, g) for b in range(TT) for g in range(n // 4)] for n in (A_HEADS, M_HEADS)]
ATT_BASE = len(ATT_UNITS[0])


def hcount(layer, kind, group):
    return (MLP_GROUPS * layer if kind == 0 else 2 * MLP_GROUPS + FFN_GROUPS * layer) + group


def ready(j, tt):
    return TT * (j - 1) + tt + 1


def vcol0(c):
    return 512 if c == 2 else 0


INS = ["x", "positions", "a_w_in", "a_w_o", "b_w_in", "b_w_a2", "b_b_a", "b_g_norm", "b_w_o", "ln_mix_g", "ln_mix_b",
       "mlp_w_up", "mlp_w_down", "ln_mlp_g", "ln_mlp_b", "p_2", "positions_2", "mla_w_dqkv_2", "mla_q_norm_2",
       "mla_kv_norm_2", "mla_w_uq_2", "mla_w_ukv_2", "mla_w_o_2", "hgrn_w_in_2", "hgrn_lb_logits_2",
       "hgrn_out_norm_2", "hgrn_w_o_2", "ffn_w_in_2", "ffn_w_down_2", "ln_mix_g_2", "ln_mix_b_2", "ln_ffn_g_2",
       "ln_ffn_b_2", "ple_w_proj_2", "ple_w_gate_2"]


def kernel(**inputs):
    import concourse.bacc as bacc
    from concourse.bass_utils import run_bass_kernel_spmd as run

    nc = bacc.Bacc("TRN2", target_bir_lowering=False, num_devices=1)
    arrays, t = {}, {}
    for name in INS:
        a = np.ascontiguousarray(inputs[name])
        arrays[f"in_{name}"] = a
        t[name] = nc.dram_tensor(f"in_{name}", a.shape, mybir.dt.from_np(a.dtype), kind="ExternalInput").ap()
    out = nc.dram_tensor("out", (1, SEQ, D), F32, kind="ExternalOutput").ap()
    build(nc, t, out)
    r = run(nc, [arrays], core_ids=[0])
    return r.results[0]["out"]
```

```python
from contextlib import ExitStack

import numpy as np

import concourse.bass as bass
from concourse import mybir
from concourse.alu_op_type import AluOpType as ALU

F32 = mybir.dt.float32
F32R = mybir.dt.float32r
I32 = mybir.dt.int32
ACT = mybir.ActivationFunctionType
AX_X = mybir.AxisListType.X

P = 128
SEQ = 256
TT = SEQ // P
D = 1024
KD = D // P
DEPTH = 2
ALPHA = float((2 * DEPTH) ** 0.25)
LN_EPS = 1e-5
RMS_EPS = 1e-6
DFF = 4 * D
DFF2 = ((8 * D // 3 + 255) // 256) * 256
D_PLE = 256

A_HEADS, A_KV, A_HD = 16, 4, 64
IDX_HEADS = 8
TOPK = min(256, SEQ // 4)
A_Q, A_K, A_V, A_IQ, A_IK = 0, 1024, 1280, 1536, 2048
A_IN = 2120
A_SMALL = A_IN - A_IK
ROT = A_HD // 4 // 2
B_LOW = 3072
B_RANK = 16
M_HEADS, M_NOPE, M_ROPE = 8, 128, 64
M_HALF = M_ROPE // 2
M_SCALE = float((M_NOPE + M_ROPE) ** -0.5)

RING = 3
CH = 2048
FG = 256
MLP_GROUPS = DFF // FG
FFN_GROUPS = DFF2 // FG

MASKED = -1.0e30
NOT_CAUSAL = -3.0e38
TAKEN = -3.4e38
MAGIC = 12582912.0
TWO_PI = 2.0 * np.pi
PI_A = 6.28125
PI_B = float(np.float32(np.round((TWO_PI - PI_A) * 2.0**21) / 2.0**21))
PI_C = float(np.float32(TWO_PI - PI_A - PI_B))
PI_MAX = 3.1415925
LN_FLOOR = float(2.0**-64)
RSQRT_SEED_8 = float(0x5F3759DF - (3 << 23) - (1 << 31))

V_BA, V_QN, V_KVN, V_LB, V_ROWS = 0, 4, 6, 8, 24

LEVELS = [128, 64, 32, 16, 8, 4, 2, 1]


def inverse_frequencies():
    a = [float(np.float32(500000.0) ** np.float32(-i / 16.0)) for i in range(0, 16, 2)]
    m = [float(np.float32(10000.0) ** np.float32(-i / 64.0)) for i in range(0, 64, 2)]
    return a, m


def build(nc, t, out):
    with ExitStack() as ctx:

        def sb(name, shape, dt=F32):
            return ctx.enter_context(nc.sbuf_tensor(name, shape, dt))

        class Semaphores(dict):
            def __missing__(self, name):
                self[name] = ctx.enter_context(nc.semaphore(name))
                return self[name]

        s = Semaphores()

        ps = ctx.enter_context(nc.psum_tensor("ps", [P, 8, 512], F32))
        x = sb("x", [P, TT, D])
        y = sb("y", [P, TT, D])
        xh = sb("xh", [P, KD, SEQ], F32R)
        xl = sb("xl", [P, KD, SEQ], F32R)
        raw = sb("raw", [P, RING, CH])
        whi = sb("whi", [P, RING, CH], F32R)
        wlo = sb("wlo", [P, RING, CH], F32R)
        lnw = sb("lnw", [P, 2, D])
        hh = sb("hh", [P, 3, 512], F32R)
        hl = sb("hl", [P, 3, 512], F32R)
        buf = [sb(f"buf{i}", [P, 2048]) for i in range(8)]
        ident = sb("ident", [P, P])
        stats = sb("stats", [P, TT, 2, 6])
        mv = sb("mv", [P, TT, 2])
        small = sb("small", [P, 64])
        inv = sb("inv", [P, 40])
        posi = sb("posi", [P, 2, TT], I32)
        posf = sb("posf", [P, 2, TT])
        sinA = sb("sinA", [P, TT, ROT])
        cosA = sb("cosA", [P, TT, ROT])
        sinM = sb("sinM", [P, TT, M_HALF])
        cosM = sb("cosM", [P, TT, M_HALF])
        vrow = sb("vrow", [V_ROWS, P])
        vcol = sb("vcol", [P, V_ROWS])
        lbv = sb("lbv", [P, 8, 8])
        masks = sb("masks", [P, 8, P])
        alow = sb("alow", [P, TT, B_RANK])
        alowT = sb("alowT", [B_RANK, SEQ])

        def bank(b, n=512):
            return ps[:, b, 0:n]

        def banks(b, n):
            return ps[:, b : b + n, :].rearrange("p b c -> p (b c)")

        width = []
        source = []
        first = {}

        def chunk(name, src, k, cols):
            first.setdefault(name, len(width))
            width.append(k * cols)
            source.append((src, k, cols))

        def rows_of(w, k0, kn, c0, cn):
            return w.rearrange("(k p) c -> p k c", p=P)[:, k0 : k0 + kn, c0 : c0 + cn]

        def square_chunks(name, w, c0=0):
            for q in range(4):
                chunk(name, rows_of(w, 2 * q, 2, c0, D), 2, D)

        def column_chunks(name, w, c0, count):
            for q in range(count):
                chunk(name, rows_of(w, 0, KD, c0 + FG * q, FG), KD, FG)

        a_in, b_in = t["a_w_in"][0], t["b_w_in"][0]
        square_chunks("dsa_kvi", a_in, A_K)
        chunk("dsa_small", rows_of(a_in, 0, KD, A_IK, A_SMALL), KD, A_SMALL)
        square_chunks("dsa_q", a_in, A_Q)
        square_chunks("dsa_o", t["a_w_o"][0])

        def mlp_chunks(layer):
            up, down = t["mlp_w_up"][layer], t["mlp_w_down"][layer]
            for q in range(MLP_GROUPS + 1):
                if q < MLP_GROUPS:
                    chunk(f"mlp{layer}", rows_of(up, 0, KD, FG * q, FG), KD, FG)
                if q:
                    chunk(f"mlp{layer}", rows_of(down, 2 * q - 2, 2, 0, D), 2, D)

        def ffn_chunks(layer):
            w_in, down = t["ffn_w_in_2"][layer], t["ffn_w_down_2"][layer]
            for q in range(FFN_GROUPS + 1):
                if q < FFN_GROUPS:
                    chunk(f"ffn{layer}", rows_of(w_in, 0, KD, FG * q, FG), KD, FG)
                    chunk(f"ffn{layer}", rows_of(w_in, 0, KD, DFF2 + FG * q, FG), KD, FG)
                if q:
                    chunk(f"ffn{layer}", rows_of(down, 2 * q - 2, 2, 0, D), 2, D)

        def ple_chunks(layer):
            chunk(f"ple{layer}", rows_of(t["ple_w_proj_2"][layer], 0, 2, 0, D), 2, D)
            square_chunks(f"ple{layer}", t["ple_w_gate_2"][layer])

        mlp_chunks(0)
        chunk("gla_low", rows_of(b_in, 0, KD, B_LOW, B_RANK), KD, B_RANK)
        column_chunks("gla_qk", b_in, 0, 4)
        square_chunks("gla_v", b_in, 1024)
        square_chunks("gla_r", b_in, 2048)
        square_chunks("gla_o", t["b_w_o"][0])
        mlp_chunks(1)
        w_down = t["mla_w_dqkv_2"][0]
        chunk("mla_down", rows_of(w_down, 0, 4, 0, 512), 4, 512)
        chunk("mla_down", rows_of(w_down, 4, 4, 0, 512), 4, 512)
        chunk("mla_down", rows_of(w_down, 0, KD, 512, M_ROPE), KD, M_ROPE)
        for q in range(2):
            chunk("mla_q", rows_of(t["mla_w_uq_2"][0], 0, 2, 768 * q, 768), 2, 768)
        for q in range(2):
            chunk("mla_kv", rows_of(t["mla_w_ukv_2"][0], 0, 2, D * q, D), 2, D)
        square_chunks("mla_o", t["mla_w_o_2"][0])
        ffn_chunks(0)
        ple_chunks(0)
        column_chunks("hgrn_f", t["hgrn_w_in_2"][0], 1024, 4)
        column_chunks("hgrn_q", t["hgrn_w_in_2"][0], 0, 4)
        square_chunks("hgrn_v", t["hgrn_w_in_2"][0], 2048)
        square_chunks("hgrn_gate", t["hgrn_w_in_2"][0], 3072)
        square_chunks("hgrn_o", t["hgrn_w_o_2"][0])
        ffn_chunks(1)
        ple_chunks(1)
        N_CHUNKS = len(width)

        (T_X0, T_DSA, T_X1, T_X2, T_GLA, T_X3, T_X4, T_MLA, T_X5, T_X6, T_X7, T_HGRN, T_X8, T_X9) = range(14)

        NORM_TURN = [T_X1, T_X2, T_X3, T_X4, T_X5, T_X6, T_X8, T_X9]

        block = ctx.enter_context(nc.Block())

        @block.sync
        def _(sp):
            for tt in range(TT):
                sp.dma_start(x[:, tt, :], t["x"][0, tt * P : (tt + 1) * P, :]).then_inc(s[f"x_landed{tt}"], 16)

            def load(n):
                src, k, cols = source[n]
                if n >= RING:
                    sp.wait_ge(s["lo_done"], n - RING + 1)
                dst = raw[:, n % RING, 0 : k * cols].rearrange("p (k c) -> p k c", k=k)
                sp.dma_start(dst, src).then_inc(s[f"raw_landed{n % RING}"], 16)

            def load_in_loop(n, per, i, src, k, cols):
                sp.wait_ge(s["lo_done"], i * per + (n - RING + 1))
                dst = raw[:, n % RING, :].rearrange("p (k c) -> p k c", k=k)
                sp.dma_start(dst, src).then_inc(s[f"raw_landed{n % RING}"], 16)

            def load_mlp(layer):
                n0 = first[f"mlp{layer}"]
                up = t["mlp_w_up"][layer].rearrange("(k p) f -> p k f", p=P)
                down = t["mlp_w_down"][layer].rearrange("(c p) d -> p c d", p=P)
                load(n0)
                with sp.Fori(0, (MLP_GROUPS - 1) // 3) as i:
                    for j in range(3):
                        load_in_loop(n0 + 1 + 2 * j, 6, i, up[:, :, bass.ds(i * (3 * FG) + (j + 1) * FG, FG)], KD, FG)
                        load_in_loop(n0 + 2 + 2 * j, 6, i, down[:, bass.ds(i * 6 + 2 * j, 2), :], 2, D)
                load(n0 + 2 * MLP_GROUPS - 1)

            def load_ffn(layer):
                n0 = first[f"ffn{layer}"]
                w_in = t["ffn_w_in_2"][layer].rearrange("(k p) f -> p k f", p=P)
                down = t["ffn_w_down_2"][layer].rearrange("(c p) d -> p c d", p=P)
                load(n0)
                load(n0 + 1)
                with sp.Fori(0, (FFN_GROUPS - 1) // 2) as i:
                    for j in range(2):
                        g0 = (j + 1) * FG
                        load_in_loop(n0 + 2 + 3 * j, 6, i, w_in[:, :, bass.ds(i * (2 * FG) + g0, FG)], KD, FG)
                        load_in_loop(n0 + 3 + 3 * j, 6, i, w_in[:, :, bass.ds(i * (2 * FG) + (DFF2 + g0), FG)], KD, FG)
                        load_in_loop(n0 + 4 + 3 * j, 6, i, down[:, bass.ds(i * 4 + 2 * j, 2), :], 2, D)
                load(n0 + 3 * FFN_GROUPS - 1)

            def load_from(n, end):
                for m in range(n, end):
                    load(m)

            load_from(0, first["mlp0"])
            load_mlp(0)
            load_from(first["gla_low"], first["mlp1"])
            load_mlp(1)
            load_from(first["mla_down"], first["ffn0"])
            load_ffn(0)
            load_from(first["ple0"], first["ffn1"])
            load_ffn(1)
            load_from(first["ple1"], N_CHUNKS)
            for tt in range(TT):
                sp.wait_ge(s["out_ready"], tt + 1)
                sp.dma_start(out[0, tt * P : (tt + 1) * P, :], x[:, tt, :]).then_inc(s["out_landed"], 16)
            sp.wait_ge(s["out_landed"], 16 * TT)

        half = lambda b, h: buf[b][:, 1024 * h : 1024 * h + 1024]
        kvi = buf[0][:, :].rearrange("p (t c) -> p t c", t=TT)
        qtok = buf[1][:, :].rearrange("p (t c) -> p t c", t=TT)
        ikw = sb("ikw", [P, TT, A_SMALL])
        kdup = half(2, 0).rearrange("p (t g e d) -> p t g e d", t=TT, g=A_KV, e=2)
        iqT = half(2, 1).rearrange("p (c n) -> p c n", c=4)
        qT = buf[3][:, :].rearrange("p (c n) -> p c n", c=KD)
        kT = buf[4][:, :].rearrange("p (g e n) -> p g e n", g=A_KV, e=2)
        ikT = half(7, 0)[:, 0:512].rearrange("p (e n) -> p e n", e=2)
        ikdup = half(7, 0)[:, 512:768].rearrange("p (t e d) -> p t e d", t=TT, e=2)
        score = half(7, 1)[:, 0:512].rearrange("p (b n) -> p b n", b=TT)
        relu_s = buf[5][:, :].rearrange("p (u n) -> p u n", u=4)
        work = sb("work", [P, TT, 2, SEQ])
        top8 = sb("top8", [P, TT, 8])
        bias = work[:, :, 0, :]
        logit = buf[6][:, :].rearrange("p (e n) -> p e n", e=2)
        probT = buf[7][:, :].rearrange("p (e n) -> p e n", e=2)
        negmax = sb("negmax", [P, 2, 4])
        rowsum = sb("rowsum", [P, TT, A_HEADS])
        rinv = sb("rinv", [P, TT, A_HEADS])
        lat = half(1, 0).rearrange("p (t c) -> p t c", t=TT)
        latn = half(1, 1).rearrange("p (t c) -> p t c", t=TT)
        vM = buf[0][:, :].rearrange("p (t c) -> p t c", t=TT)
        qnT = buf[3][:, :].rearrange("p (h n) -> p h n", h=M_HEADS)
        knT = buf[2][:, :].rearrange("p (h n) -> p h n", h=M_HEADS)
        qrT = half(4, 0).rearrange("p (c n) -> p c n", c=4)
        krT = half(4, 1)[:, 0:512].rearrange("p (e n) -> p e n", e=2)
        krdup = half(4, 1)[:, 512:768].rearrange("p (t e d) -> p t e d", t=TT, e=2)
        krtok = half(4, 1)[:, 768:896].rearrange("p (t d) -> p t d", t=TT)
        qrtok = half(5, 0).rearrange("p (t c) -> p t c", t=TT)
        causal = half(5, 1)[:, 0:512].rearrange("p (b n) -> p b n", b=TT)
        rot4 = sb("rot4", [P, 4, 256])
        q4 = [half(0, 0).rearrange("p (h n) -> p h n", h=4), half(0, 1).rearrange("p (h n) -> p h n", h=4)]
        k4 = [half(1, 0).rearrange("p (h n) -> p h n", h=4), half(1, 1).rearrange("p (h n) -> p h n", h=4)]
        g4 = [half(2, 0).rearrange("p (h n) -> p h n", h=4), half(2, 1).rearrange("p (h n) -> p h n", h=4)]
        expo = [half(3, 0), half(3, 1)]
        zed = [half(7, 0), half(7, 1)]
        wa2 = buf[4][0:B_RANK, 1536:2048]
        att_own = [half(4, 0).rearrange("p (h e n) -> p h e n", h=4, e=2),
                   work.rearrange("p b e n -> p (b e n)").rearrange("p (h e n) -> p h e n", h=4, e=2)]
        att_past = [half(4, 1)[:, 0:512].rearrange("p (h n) -> p h n", h=4), half(4, 1)[:, 512:1024].rearrange("p (h n) -> p h n", h=4)]
        vtok = buf[5][:, :].rearrange("p (t c) -> p t c", t=TT)
        gate = buf[6][:, :].rearrange("p (t c) -> p t c", t=TT)
        gn = y[:, 0, :]
        negref = sb("negref", [P, 2, 4, 3])
        ss = sb("ss", [P, TT, 8])
        ptok = buf[0][:, 0:512].rearrange("p (t c) -> p t c", t=TT)
        side = buf[2][:, :].rearrange("p (t c) -> p t c", t=TT)
        P_SLOT = 2

        def decay_out(c, tt, h, hd):
            if hd == 256:
                return ps[:, 2 * tt + h // 2, 256 * (h % 2) : 256 * (h % 2) + 256]
            return ps[:, 2 * tt + (c == 2), P * h : P * h + P]

        @block.gpsimd
        def _(pool):
            n_step = [0]

            def step(ins):
                ins.then_inc(s["pool_step"], 1)
                n_step[0] += 1
                pool.wait_ge(s["pool_step"], n_step[0])

            g = nc.gpsimd
            step(g.memset(ident[:, :], 0.0))
            g.affine_select(out=ident[:, :], in_=ident[:, :], compare_op=ALU.not_equal, fill=1.0, base=0,
                            pattern=[[-1, P]], channel_multiplier=1).then_inc(s["ident_done"], 1)
            for w, name in enumerate(("positions", "positions_2")):
                pool.dma_start(posi[:, w, :], t[name][0].rearrange("(t p) -> p t", p=P), allow_slow_non_contiguous=True).then_inc(s["pos_landed"], 16)
            pool.dma_start(vrow[V_BA : V_BA + 4, :], t["b_b_a"][0].rearrange("(r p) -> r p", p=P)).then_inc(s["vrow_landed"], 16)
            pool.dma_start(vrow[V_QN : V_QN + 2, :], t["mla_q_norm_2"][0].rearrange("(r p) -> r p", p=P)).then_inc(s["vrow_landed"], 16)
            pool.dma_start(vrow[V_KVN : V_KVN + 2, :], t["mla_kv_norm_2"][0].rearrange("(r p) -> r p", p=P)).then_inc(s["vrow_landed"], 16)
            pool.dma_start(vrow[V_LB : V_LB + 16, :], t["hgrn_lb_logits_2"].rearrange("l (h p) -> (l h) p", p=P)).then_inc(s["vrow_landed"], 16)

            def load_ln(i):
                layer = (i // 2) % 2
                if i < 4:
                    gb = ("ln_mix_g", "ln_mix_b") if i % 2 == 0 else ("ln_mlp_g", "ln_mlp_b")
                else:
                    gb = ("ln_mix_g_2", "ln_mix_b_2") if i % 2 == 0 else ("ln_ffn_g_2", "ln_ffn_b_2")
                if i >= 1:
                    pool.wait_ge(s["src_ready"], ready(NORM_TURN[i - 1], 1))
                for w, name in enumerate(gb):
                    pool.dma_start(lnw[:, w, :], t[name][layer].partition_broadcast(P)).then_inc(s["ln_landed"], 16)

            load_ln(0)
            freq_a, freq_m = inverse_frequencies()
            for c, f in enumerate(freq_a + freq_m):
                last = g.memset(inv[:, c : c + 1], f)
            last.then_inc(s["inv_done"], 1)

            def note(ins):
                ins.then_inc(s["pool_step"], 1)
                n_step[0] += 1

            def rotate(v, n_heads, cos, sin, hd, tt, scratch, signal=None):
                c = cos[:, tt, :].unsqueeze(1).broadcast_to([P, n_heads, hd])
                sn = sin[:, tt, :].unsqueeze(1).broadcast_to([P, n_heads, hd])
                a, b, e, f = (scratch[:, q, 0 : n_heads * hd].rearrange("p (h d) -> p h d", h=n_heads) for q in range(4))
                t1, t2 = v[:, :, 0:hd], v[:, :, hd : 2 * hd]
                note(g.tensor_tensor(a, t1, c, ALU.mult))
                note(g.tensor_tensor(b, t2, sn, ALU.mult))
                note(g.tensor_tensor(e, t2, c, ALU.mult))
                step(g.tensor_tensor(f, t1, sn, ALU.mult))
                step(g.tensor_tensor(t1, a, b, ALU.subtract))
                last = g.tensor_tensor(t2, e, f, ALU.add)
                if signal is None:
                    step(last)
                else:
                    last.then_inc(s[signal], 1)
                    pool.wait_ge(s[signal], tt + 1)

            note(g.memset(ikT[:, :, :], 0.0))
            step(g.memset(kT[:, :, :, :], 0.0))
            pool.wait_ge(s["tables_done"], 1)
            pool.wait_ge(s["kvi_act"], 2)
            pool.wait_ge(s["kvi_dve"], 2)
            pool.wait_ge(s["small_out"], 2)
            for tt in range(TT):
                rotate(kvi[:, tt, 512:1024].rearrange("p (h d) -> p h d", d=A_HD), IDX_HEADS, cosA, sinA, ROT, tt, rot4)
                rotate(ikw[:, tt, 0:A_HD].unsqueeze(1), 1, cosA, sinA, ROT, tt, rot4)
                step(g.tensor_copy(ikdup[:, tt, :, :], ikw[:, tt, 0:A_HD].unsqueeze(1).broadcast_to([P, 2, A_HD])))
                g.tensor_scalar(ikw[:, tt, A_HD:A_SMALL], ikw[:, tt, A_HD:A_SMALL], float(IDX_HEADS**-0.5), None,
                                ALU.mult).then_inc(s["index_rotated"], 1)
            for tt in range(TT):
                rotate(kvi[:, tt, 0:256].rearrange("p (h d) -> p h d", d=A_HD), A_KV, cosA, sinA, ROT, tt, rot4)
                g.tensor_copy(kdup[:, tt, :, :, :], kvi[:, tt, 0:256].rearrange("p (h d) -> p h d", d=A_HD).unsqueeze(2)
                              .broadcast_to([P, A_KV, 2, A_HD])).then_inc(s["k_rotated"], 1)
            for b in range(TT):
                pool.wait_ge(s["index_added"], (2, 6)[b])
                g.affine_select(out=work[:, b, 0, :], in_=score[:, b, :], compare_op=ALU.is_ge, fill=NOT_CAUSAL,
                                base=b * P, pattern=[[-1, SEQ]], channel_multiplier=1).then_inc(s["score_masked"], 1)
            for tt in range(TT):
                pool.wait_ge(s["q_out"], 2 * tt + 2)
                rotate(qtok[:, tt, :].rearrange("p (h d) -> p h d", d=A_HD), A_HEADS, cosA, sinA, ROT, tt, rot4, "q_rotated")
            for b in range(TT):
                pool.wait_ge(s["chosen"], b + 1)
                g.affine_select(out=bias[:, b, :], in_=work[:, b, 1, :], compare_op=ALU.is_ge, fill=MASKED,
                                base=b * P, pattern=[[-1, SEQ]], channel_multiplier=1).then_inc(s["bias_done"], 1)

            for m in range(1, 8):
                lv = LEVELS[m]
                v = masks[:, m - 1, :].rearrange("p (b e c) -> p b e c", e=2, c=lv)
                step(g.memset(masks[:, m - 1, :], 0.0))
                step(g.memset(v[:, :, 1, :], 1.0))
                step(g.affine_select(out=v[:, :, 1, :], in_=v[:, :, 1, :], compare_op=ALU.is_ge, fill=0.0, base=0,
                                     pattern=[[-2 * lv, P // (2 * lv)], [0, lv]], channel_multiplier=1))
                step(g.affine_select(out=v[:, :, 1, :], in_=v[:, :, 1, :], compare_op=ALU.is_ge, fill=0.0, base=lv - 1,
                                     pattern=[[2 * lv, P // (2 * lv)], [0, lv]], channel_multiplier=-1))
            g.tensor_copy(masks[:, 7, :], ident[:, :]).then_inc(s["masks_done"], 1)
            pool.wait_ge(s["src_ready"], ready(T_DSA, 1))
            pool.dma_start(wa2, t["b_w_a2"][0]).then_inc(s["wa2_landed"], 16)
            g.memset(att_own[0], 0.0).then_inc(s["att_zeroed"], 1)
            load_ln(1)
            load_ln(2)
            for h in range(4):
                pool.dma_start(gn[:, 256 * h : 256 * h + 256], t["b_g_norm"][0].partition_broadcast(P)).then_inc(s["gn_landed"], 16)
            load_ln(3)
            pool.wait_ge(s["src_ready"], ready(T_GLA, 1))
            step(g.memset(causal[:, :, :], 0.0))
            for b in range(TT):
                ins = g.affine_select(out=causal[:, b, :], in_=causal[:, b, :], compare_op=ALU.is_ge, fill=MASKED,
                                      base=b * P, pattern=[[-1, SEQ]], channel_multiplier=1)
            ins.then_inc(s["causal_done"], 1)
            step(g.memset(krT[:, :, :], 0.0))
            pool.wait_ge(s["kr_out"], TT)
            for tt in range(TT):
                rotate(krtok[:, tt, :].unsqueeze(1), 1, cosM, sinM, M_HALF, tt, rot4)
                g.tensor_copy(krdup[:, tt, :, :], krtok[:, tt, :].unsqueeze(1).broadcast_to([P, 2, M_ROPE])).then_inc(s["kr_rotated"], 1)
            pool.wait_ge(s["qr_out"], 4)
            for tt in range(TT):
                rotate(qrtok[:, tt, :].rearrange("p (h d) -> p h d", d=M_ROPE), M_HEADS, cosM, sinM, M_HALF, tt, rot4, "qr_rotated")
            load_ln(4)
            pool.wait_ge(s["src_ready"], ready(T_MLA, 1))
            pool.dma_start(ptok, t["p_2"][0, 0].rearrange("(t p) d -> p t d", p=P)).then_inc(s["p_landed"], 16)
            load_ln(5)
            load_ln(6)
            pool.wait_ge(s["src_ready"], ready(T_X7, 1))
            pool.dma_start(gn, t["hgrn_out_norm_2"][0].partition_broadcast(P)).then_inc(s["gn_landed"], 16)
            note(g.memset(work[:, :, :, :], 0.0))
            g.memset(att_own[0], 0.0).then_inc(s["att_zeroed"], 1)
            pool.wait_ge(s["src_ready"], ready(T_HGRN, 1))
            pool.dma_start(ptok, t["p_2"][1, 0].rearrange("(t p) d -> p t d", p=P)).then_inc(s["p_landed"], 16)
            load_ln(7)

        @block.tensor
        def _(pe):
            mm = nc.tensor.matmul

            def three(o, a, b, start, stop):
                mm(o, a[0], b[0], start=start, stop=False)
                mm(o, a[1], b[0], start=False, stop=False)
                return mm(o, a[0], b[1], start=False, stop=stop)

            def weights(n, k, cols):
                slot = n % RING
                return [w[:, slot, 0 : k * cols].rearrange("p (k c) -> p k c", k=k) for w in (whi, wlo)]

            def take(n):
                pe.wait_ge(s["lo_done"], n + 1)

            def rows(n, k, cols, k0, total_k, outs, src=(xh, xl)):
                w = weights(n, k, cols)
                for kk in range(k):
                    for tt, cs, o in outs:
                        a = [v[:, k0 + kk, tt * P : (tt + 1) * P] for v in src]
                        last = three(o, a, [v[:, kk, cs] for v in w], k0 + kk == 0, k0 + kk == total_k - 1)
                return last

            def by_rows(n, k, cols, k0, total_k, outs, src=(xh, xl)):
                take(n)
                rows(n, k, cols, k0, total_k, outs, src).then_inc(s["w_done"], 1)

            def to_norm(n, k0, total_k, k_of):
                take(n)
                w = weights(n, 2, D)
                for tt in range(TT):
                    for kk in range(2):
                        for _, cs, o in wide(0)[2 * tt : 2 * tt + 2]:
                            last = three(o, k_of(kk, tt), [v[:, kk, cs] for v in w], k0 + kk == 0, k0 + kk == total_k - 1)
                    last.then_inc(s["acc_done" if tt == 0 else "w_done"], 1)

            def row_part(n, k, cols, k0, total_k, outs):
                return n, lambda tt: rows(n, k, cols, k0, total_k, [o for o in outs if o[0] == tt])


            def wide(base):
                return [(tt, slice(512 * c, 512 * c + 512), bank(base + 2 * tt + c)) for tt in range(TT) for c in range(2)]

            def square(n0, base, q0=0, q1=4):
                for q in range(q0, q1):
                    by_rows(n0 + q, 2, D, 2 * q, KD, wide(base))

            def last_two(n, signal):
                take(n + 1)
                for tt in range(TT):
                    for q in range(2):
                        last = rows(n + q, 2, D, 4 + 2 * q, KD, wide(0)[2 * tt : 2 * tt + 2])
                        if tt == 1 and q == 0:
                            last.then_inc(s["w_done"], 1)
                    last.then_inc(s[signal if tt == 0 else "w_done"], 1)

            def output_product(j, name):
                n0 = first[name]
                turn(j, y, [row_part(n0 + q, 2, D, 2 * q, KD, wide(0)) for q in range(2)])
                last_two(n0 + 2, "acc_done")

            def columns(w, o, turned=None):
                for f in range(2):
                    for kk in range(KD):
                        if turned is not None and f == 0 and kk == KD // 2:
                            pe.wait_ge(s["turn_lo"], turned)
                        last = three(o[:, 256 * f : 256 * f + 256], [v[:, kk, P * f : P * f + P] for v in w],
                                     [v[:, kk, :] for v in (xh, xl)], kk == 0, kk == KD - 1)
                return last

            def turn_to_columns(j, n, o):
                turn(j, x, [])
                take(n)
                pe.wait_ge(s["turn_lo"], 4 * j + 3)
                columns(weights(n, KD, FG), o, turned=4 * j + 4).then_inc(s["w_done"], 1)

            def turn(j, src, parts):
                for tt in range(TT):
                    if j == 0:
                        pe.wait_ge(s[f"x_landed{tt}"], 16)
                        pe.wait_ge(s["ident_done"], 1)
                    for hf in range(2):
                        if j > 0:
                            pe.wait_ge(s["src_ready"], ready(j, tt, hf))
                        for q in range(4):
                            last = nc.tensor.transpose(ps[:, 4 + 2 * tt + hf, P * q : P * q + P],
                                                       src[:, tt, P * (4 * hf + q) : P * (4 * hf + q) + P], ident[:, :])
                        last.then_inc(s["turned"], 1)
                    if parts:
                        pe.wait_ge(s["turn_lo"], 4 * j + 2 * tt + 2)
                    for n, products in parts:
                        if tt == 0:
                            take(n)
                        last = products(tt)
                        if tt == TT - 1:
                            last.then_inc(s["w_done"], 1)

            def mlp(layer):
                n0 = first[f"mlp{layer}"]
                turn_to_columns((T_X1, T_X3)[layer], n0, bank(4))

                def down(n, slot, start, stop):
                    w = weights(n, 2, D)
                    for f in range(2):
                        for tt, cs, o in wide(0):
                            a = [v[:, slot, 256 * f + P * tt : 256 * f + P * tt + P] for v in (hh, hl)]
                            last = three(o, a, [v[:, f, cs] for v in w], start and f == 0, stop and f == 1)
                    last.then_inc(s["w_done"], 1)

                def body(it, j, start):
                    n = n0 + 1 + 2 * j
                    up_ready, h_ready, down_ready = n + 1, hcount(layer, 0, j) + 1, n + 2
                    if it is not None:
                        up_ready = pe.snap(it * 6 + up_ready)
                        h_ready = pe.snap(it * 3 + h_ready)
                        down_ready = pe.snap(it * 6 + down_ready)
                    pe.wait_ge(s["lo_done"], up_ready)
                    columns(weights(n, KD, FG), bank(4 + (j + 1) % 3)).then_inc(s["w_done"], 1)
                    pe.wait_ge(s["h_lo"], h_ready)
                    pe.wait_ge(s["lo_done"], down_ready)
                    down(n + 1, j % 3, start, False)

                for j in range(3):
                    body(None, j, j == 0)
                with pe.Fori(1, (MLP_GROUPS - 1) // 3) as it:
                    for j in range(3):
                        body(it, j, False)
                n = n0 + 2 * MLP_GROUPS - 1
                slot = (MLP_GROUPS - 1) % 3
                pe.wait_ge(s["h_lo"], hcount(layer, 0, MLP_GROUPS - 1) + 1)
                to_norm(n, 1, 3, lambda f, tt: [v[:, slot, 256 * f + P * tt : 256 * f + P * tt + P] for v in (hh, hl)])

            def ffn(layer):
                n0 = first[f"ffn{layer}"]
                turn_to_columns((T_X5, T_X8)[layer], n0, bank(4))
                pe.wait_ge(s["p_landed"], 16 * (layer + 1))
                for tt in range(TT):
                    for q in range(2):
                        last = nc.tensor.transpose(ps[:, 0, 256 * q + P * tt : 256 * q + P * tt + P], ptok[:, tt, P * q : P * q + P], ident[:, :])
                last.then_inc(s["p_turned"], 1)
                take(n0 + 1)
                columns(weights(n0 + 1, KD, FG), bank(5)).then_inc(s["w_done"], 1)

                def down(n, slot, start, stop):
                    w = weights(n, 2, D)
                    for f in range(2):
                        for tt, cs, o in wide(0):
                            a = [v[:, slot, 256 * f + P * tt : 256 * f + P * tt + P] for v in (hh, hl)]
                            last = three(o, a, [v[:, f, cs] for v in w], start and f == 0, stop and f == 1)
                    last.then_inc(s["w_done"], 1)

                def body(it, j, start):
                    n = n0 + 2 + 3 * j
                    for w in range(2):
                        ready = n + w + 1
                        if it is not None:
                            ready = pe.snap(it * 6 + ready)
                        pe.wait_ge(s["lo_done"], ready)
                        columns(weights(n + w, KD, FG), bank(4 + 2 * ((j + 1) % 2) + w)).then_inc(s["w_done"], 1)
                    h_ready, down_ready = hcount(layer, 1, j) + 1, n + 3
                    if it is not None:
                        h_ready = pe.snap(it * 2 + h_ready)
                        down_ready = pe.snap(it * 6 + down_ready)
                    pe.wait_ge(s["h_lo"], h_ready)
                    pe.wait_ge(s["lo_done"], down_ready)
                    if start:
                        pe.wait_ge(s["p_lo"], layer + 1)
                    down(n + 2, j % 2, start, False)

                body(None, 0, True)
                body(None, 1, False)
                with pe.Fori(1, (FFN_GROUPS - 1) // 2) as it:
                    for j in range(2):
                        body(it, j, False)
                n = n0 + 3 * FFN_GROUPS - 1
                slot = (FFN_GROUPS - 1) % 2
                pe.wait_ge(s["h_lo"], hcount(layer, 1, FFN_GROUPS - 1) + 1)
                to_norm(n, 1, 3, lambda f, tt: [v[:, slot, 256 * f + P * tt : 256 * f + P * tt + P] for v in (hh, hl)])

            def attention(kind, units, score_mm, value, hd, before_second=None):
                n_units = len(units)
                base = kind * ATT_BASE

                def logits(u):
                    b, g = units[u]
                    if u >= 2:
                        pe.wait_ge(s["logit_read"], base + u - 1)
                    for h in range(4):
                        n = P * (b + 1)
                        o = ps[:, 2 * (u % 2), P * h : P * h + P] if b == 0 else ps[:, 2 * (u % 2) + h // 2, 256 * (h % 2) : 256 * (h % 2) + 256]
                        last = score_mm(o, b, 4 * g + h, n)
                    last.then_inc(s["logits"], 1)

                def rest(u):
                    b, g = units[u]
                    pe.wait_ge(s["exp_done"], base + u + 1)
                    nk = b + 1
                    for kt in range(nk):
                        for h in range(4):
                            src = logit[:, u % 2, P * nk * h + P * kt : P * nk * h + P * kt + P]
                            last = nc.tensor.transpose(ps[:, 4 + kt, P * h : P * h + P], src, ident[:, :])
                    last.then_inc(s["probs_turned"], 1)
                    if u + 2 < n_units:
                        logits(u + 2)
                    pe.wait_ge(s["probT_act"], base + u + 1)
                    pe.wait_ge(s["probT_dve"], base + u + 1)
                    if u == n_units // 2:
                        pe.wait_ge(s["src_ready"], ready((T_DSA, T_MLA)[kind], 0))
                    for h in range(4):
                        hd0 = (4 * g + h) * hd
                        o = ps[:, 6 + hd0 // 512, hd0 % 512 : hd0 % 512 + hd]
                        for kt in range(nk):
                            lhs = probT[:, u % 2, 512 * kt + P * h : 512 * kt + P * h + P]
                            last = mm(o, lhs, value(kt, 4 * g + h), start=(kt == 0), stop=(kt == nk - 1))
                    last.then_inc(s["att_pv"], 1)

                logits(0)
                logits(1)
                if before_second:
                    before_second()
                for u in range(n_units):
                    rest(u)

            def decay_levels(c, levels):
                for lv in levels:
                    b0 = 4 + 2 * (lv % 2)
                    if lv < 8:
                        pe.wait_ge(s["zed_done"], 8 * c + lv + 1)
                    if lv >= 2 or c > 0:
                        pe.wait_ge(s["level_read"], 9 * c + max(lv - 1, 0))
                    if lv == 0:
                        for h in range(4):
                            z = zed[0][:, 256 * h : 256 * h + 256]
                            last = mm(ps[:, 4, P * h : P * h + P], z[:, 0:P], z[:, P:SEQ], start=True, stop=True)
                    else:
                        for h in range(4):
                            for tt in range(TT):
                                sl = slice(256 * h + P * tt, 256 * h + P * tt + P)
                                if lv < 8:
                                    a = b = zed[lv % 2][:, sl]
                                else:
                                    a = k4[int(c == 2)][:, h, P * tt : P * tt + P]
                                    b = q4[int(c == 2)][:, h, P * tt : P * tt + P]
                                o = ps[:, b0 + h // 2, 256 * (h % 2) + P * tt : 256 * (h % 2) + P * tt + P]
                                last = mm(o, a, b, start=True, stop=True)
                    last.then_inc(s["level_done"], 1)

            def decay_values(sets, hd):
                pe.wait_ge(s["level_read"], 9 * sets[-1] + 9)
                for tt in range(TT):
                    for c in sets:
                        own, past = att_own[int(c == 2)], att_past[int(c == 2)]
                        for h in range(4):
                            o = decay_out(c, tt, h, hd)
                            hv = slice(vcol0(c) + hd * h, vcol0(c) + hd * h + hd)
                            if tt == 0:
                                last = mm(o, own[:, h, 0, :], vtok[:, 0, hv], start=True, stop=True)
                            else:
                                mm(o, past[:, h, :], vtok[:, 0, hv], start=True, stop=False)
                                last = mm(o, own[:, h, 1, :], vtok[:, 1, hv], start=False, stop=True)
                    last.then_inc(s["decay_pv"], 1)

            def ple(layer, j):
                n0 = first[f"ple{layer}"]
                parts = [v[:, P_SLOT, :].rearrange("p (k n) -> p k n", k=2) for v in (hh, hl)]
                by_rows(n0, 2, D, 0, 2, wide(4), src=parts)
                pe.wait_ge(s["side_out"], 4 * layer + 4)
                turn(j, x, [row_part(n0 + 1 + q, 2, D, 2 * q, KD, wide(0)) for q in range(2)])
                last_two(n0 + 3, "gate_done")

            turn(T_X0, x, [])
            pe.wait_ge(s["turn_lo"], 4)
            square(first["dsa_kvi"], 0, 0, 1)
            pe.wait_ge(s["vrow_landed"], 64)
            nc.tensor.transpose(ps[:, 4, 0:V_ROWS], vrow[:, :], ident[0:V_ROWS, 0:V_ROWS]).then_inc(s["vrow_turned"], 1)

            square(first["dsa_kvi"], 0, 1)
            pe.wait_ge(s["vcol_done"], 1)
            by_rows(first["dsa_small"], KD, A_SMALL, 0, KD,
                    [(tt, slice(0, A_SMALL), bank(4 + tt, A_SMALL)) for tt in range(TT)])
            pe.wait_ge(s["kvi_act"], 2)
            pe.wait_ge(s["kvi_dve"], 2)
            for q in range(2):
                by_rows(first["dsa_q"] + q, 2, D, 2 * q, KD, wide(0))
            for tt in range(TT):
                pe.wait_ge(s["index_rotated"], tt + 1)
                for q in range(4):
                    nc.tensor.transpose(ps[:, 6 + tt, P * q : P * q + P], kvi[:, tt, 512 + P * q : 512 + P * q + P], ident[:, :])
                last = nc.tensor.transpose(ps[:, 4 + tt, 0:P], ikdup[:, tt, :, :].rearrange("p e d -> p (e d)"), ident[:, :])
                last.then_inc(s["index_turned"], 1)
            pe.wait_ge(s["indexT_done"], 2 * TT)
            for u, (b, hs) in enumerate(INDEX_UNITS):
                if u >= 4:
                    pe.wait_ge(s["index_relu"], u - 3)
                n = P * (b + 1)
                for i, h in enumerate(hs):
                    last = mm(ps[:, 4 + u % 4, n * i : n * i + n], iqT[:, h // 2, b * P : b * P + P], ikT[:, h % 2, 0:n], start=True, stop=True)
                last.then_inc(s["index_scores"], 1)
            for q in range(2, 4):
                by_rows(first["dsa_q"] + q, 2, D, 2 * q, KD, wide(0))
            pe.wait_ge(s["index_relu"], len(INDEX_UNITS))
            for tt in range(TT):
                pe.wait_ge(s["k_rotated"], tt + 1)
                for g in range(A_KV):
                    last = nc.tensor.transpose(ps[:, 4 + tt, P * g : P * g + P], kdup[:, tt, g, :, :].rearrange("p e d -> p (e d)"), ident[:, :])
                last.then_inc(s["k_turned"], 1)
            def turn_queries(tt):
                pe.wait_ge(s["q_rotated"], tt + 1)
                for hf in range(2):
                    b = 6 + hf if tt == 0 else 4 + hf
                    if tt == 1:
                        pe.wait_ge(s["kT_done"], hf + 1)
                    for q in range(4):
                        last = nc.tensor.transpose(ps[:, b, P * q : P * q + P], qtok[:, tt, P * (4 * hf + q) : P * (4 * hf + q) + P], ident[:, :])
                    last.then_inc(s["q_turned"], 1)
                pe.wait_ge(s["qT_done"], 2 * tt + 2)

            turn_queries(0)

            def dsa_scores(o, b, h, n):
                return mm(o, qT[:, h // 2, b * P : b * P + P], kT[:, h // 4, h % 2, 0:n], start=True, stop=True)

            attention(0, ATT_UNITS[0], dsa_scores, lambda kt, h: kvi[:, kt, 256 + 64 * (h // 4) : 320 + 64 * (h // 4)], A_HD,
                      lambda: turn_queries(1))
            output_product(T_DSA, "dsa_o")
            mlp(0)

            turn(T_X2, x, [row_part(first["gla_low"], KD, B_RANK, 0, KD, [(tt, slice(0, B_RANK), bank(4 + tt, B_RANK)) for tt in range(TT)])])
            for q in range(4):
                n = first["gla_qk"] + q
                take(n)
                columns(weights(n, KD, FG), bank(q)).then_inc(s["w_done"], 1)
                if q == 0:
                    pe.wait_ge(s["low_out"], 1)
                    for tt in range(TT):
                        last = nc.tensor.transpose(ps[0:B_RANK, 4, P * tt : P * tt + P], alow[:, tt, :], ident[:, :])
                    last.then_inc(s["low_turned"], 1)
                    pe.wait_ge(s["lowT_done"], 1)
                    pe.wait_ge(s["wa2_landed"], 16)
                    for h in range(4):
                        last = mm(ps[:, 6 + h // 2, 256 * (h % 2) : 256 * (h % 2) + 256], wa2[:, P * h : P * h + P], alowT[:, :], start=True, stop=True)
                    last.then_inc(s["gates"], 1)
            pe.wait_ge(s["qk_out"], 4)
            for q in range(4):
                square(first["gla_v"], 0, q, q + 1)
                decay_levels(0, GLA_LEVELS[q])
            pe.wait_ge(s["v_out"], 4)
            for q in range(4):
                square(first["gla_r"], 0, q, q + 1)
                decay_levels(0, GLA_LEVELS[q + 4])
            decay_levels(0, [8])
            pe.wait_ge(s["r_out"], 4)
            decay_values([0], 256)
            output_product(T_GLA, "gla_o")
            mlp(1)

            turn(T_X4, x, [row_part(first["mla_down"] + q, 4, 512, 4 * q, KD, [(tt, slice(0, 512), bank(tt)) for tt in range(TT)]) for q in range(2)])
            by_rows(first["mla_down"] + 2, KD, M_ROPE, 0, KD, [(tt, slice(0, M_ROPE), bank(2 + tt, M_ROPE)) for tt in range(TT)])
            for tt in range(TT):
                pe.wait_ge(s["lat_done"], tt + 1)
                for q in range(4):
                    last = nc.tensor.transpose(ps[:, 4 + tt, P * q : P * q + P], latn[:, tt, P * q : P * q + P], ident[:, :])
                last.then_inc(s["lat_turned"], 1)
            for tt in range(TT):
                pe.wait_ge(s["kr_rotated"], tt + 1)
                last = nc.tensor.transpose(ps[:, 6, P * tt : P * tt + P], krdup[:, tt, :, :].rearrange("p e d -> p (e d)"), ident[:, :])
            last.then_inc(s["kr_turned"], 1)
            pe.wait_ge(s["latT_lo"], TT)
            lat_h, lat_l = xh, xl
            for c in range(2):
                n = first["mla_q"] + c
                take(n)
                w = [v.rearrange("p k (h d) -> p k h d", h=4) for v in weights(n, 2, 768)]
                if c == 1:
                    pe.wait_ge(s["qn_out"], 2)
                    pe.wait_ge(s["qr_out"], 2)
                for h in range(4):
                    for kk in range(2):
                        last = three(ps[:, h // 2, 256 * (h % 2) : 256 * (h % 2) + 256], [v[:, kk, h, 0:P] for v in w],
                                     (lat_h[:, kk, :], lat_l[:, kk, :]), kk == 0, kk == 1)
                for tt in range(TT):
                    for kk in range(2):
                        last = three(ps[:, 2 + tt, 0:256], (lat_h[:, kk, P * tt : P * tt + P], lat_l[:, kk, P * tt : P * tt + P]),
                                     [v[:, kk, :, P : P + M_ROPE] for v in w], kk == 0, kk == 1)
                last.then_inc(s["w_done"], 1)
            for c in range(2):
                n = first["mla_kv"] + c
                take(n)
                w = [v.rearrange("p k (h d) -> p k h d", h=4) for v in weights(n, 2, D)]
                pe.wait_ge(s["qn_out"], 4)
                pe.wait_ge(s["qr_out"], 4)
                if c == 1:
                    pe.wait_ge(s["kn_out"], 2)
                    pe.wait_ge(s["vM_out"], 2)
                for h in range(4):
                    for kk in range(2):
                        last = three(ps[:, h // 2, 256 * (h % 2) : 256 * (h % 2) + 256], [v[:, kk, h, 0:P] for v in w],
                                     (lat_h[:, 2 + kk, :], lat_l[:, 2 + kk, :]), kk == 0, kk == 1)
                for tt in range(TT):
                    for kk in range(2):
                        last = three(ps[:, 2 + tt, :], (lat_h[:, 2 + kk, P * tt : P * tt + P], lat_l[:, 2 + kk, P * tt : P * tt + P]),
                                     [v[:, kk, :, P:256] for v in w], kk == 0, kk == 1)
                last.then_inc(s["w_done"], 1)
            pe.wait_ge(s["latT_lo"], TT)
            for tt in range(TT):
                pe.wait_ge(s["qr_rotated"], tt + 1)
                for q in range(4):
                    last = nc.tensor.transpose(ps[:, 4 + tt, P * q : P * q + P], qrtok[:, tt, P * q : P * q + P], ident[:, :])
                last.then_inc(s["qr_turned"], 1)
            pe.wait_ge(s["qrT_done"], TT)
            pe.wait_ge(s["krT_done"], 1)
            pe.wait_ge(s["kn_out"], 4)
            pe.wait_ge(s["vM_out"], 4)

            def mla_scores(o, b, h, n):
                mm(o, qnT[:, h, b * P : b * P + P], knT[:, h, 0:n], start=True, stop=False)
                return mm(o, qrT[:, h // 2, b * P : b * P + P], krT[:, h % 2, 0:n], start=False, stop=True)

            attention(1, ATT_UNITS[1], mla_scores, lambda kt, h: vM[:, kt, P * h : P * h + P], P)
            output_product(T_MLA, "mla_o")
            ffn(0)
            ple(0, T_X6)

            turn_to_columns(T_X7, first["hgrn_f"], bank(0))
            for q in range(1, 4):
                n = first["hgrn_f"] + q
                take(n)
                columns(weights(n, KD, FG), bank(q)).then_inc(s["w_done"], 1)
            for q in range(4):
                n = first["hgrn_q"] + q
                take(n)
                columns(weights(n, KD, FG), bank(4 + q)).then_inc(s["w_done"], 1)
            pe.wait_ge(s["f_out"], 4)
            for q in range(4):
                square(first["hgrn_v"], 0, q, q + 1)
                for c in (1, 2):
                    decay_levels(c, HGRN_LEVELS[q][c])
            pe.wait_ge(s["v_out"], 8)
            for q in range(4):
                square(first["hgrn_gate"], 0, q, q + 1)
                for c in (1, 2):
                    decay_levels(c, HGRN_LEVELS[q + 4][c])
            pe.wait_ge(s["r_out"], 8)
            decay_values([1, 2], P)
            output_product(T_HGRN, "hgrn_o")
            ffn(1)
            ple(1, T_X9)

        @block.scalar
        def _(act):
            n_step = [0]
            n_hi = [0]
            a = nc.scalar

            def step(ins):
                ins.then_inc(s["act_step"], 1)
                n_step[0] += 1
                act.wait_ge(s["act_step"], n_step[0])

            def hi_part(n):
                slot, w = n % RING, width[n]
                act.wait_ge(s[f"raw_landed{slot}"], 16 * (n // RING + 1))
                if n >= RING:
                    act.wait_ge(s["w_done"], n - RING + 1)
                a.activation(whi[:, slot, 0:w], raw[:, slot, 0:w], ACT.Copy).then_inc(s["hi_done"], 1)

            def ahead(n):
                while n_hi[0] <= min(n + 2, N_CHUNKS - 1):
                    hi_part(n_hi[0])
                    n_hi[0] += 1

            def turned(j):
                for u in range(4):
                    tt, hf = u // 2, u % 2
                    act.wait_ge(s["turned"], 4 * j + u + 1)
                    a.activation(xh[:, 4 * hf : 4 * hf + 4, P * tt : P * tt + P],
                                 bank(4 + u).rearrange("p (k n) -> p k n", k=4), ACT.Copy).then_inc(s["turn_hi"], 1)

            def mlp(layer):
                n0 = first[f"mlp{layer}"]

                def hidden(b, slot):
                    r = buf[slot // 2][:, 512 * (slot % 2) : 512 * (slot % 2) + 512]
                    a.activation(r, bank(b), ACT.Relu).then_inc(s["h_act"], 1)

                def high(slot):
                    r = buf[slot // 2][:, 512 * (slot % 2) : 512 * (slot % 2) + 512]
                    a.activation(hh[:, slot, :], r, ACT.Square).then_inc(s["h_hi"], 1)

                ahead(n0)
                act.wait_ge(s["w_done"], n0 + 1)
                hidden(4, 0)
                act.wait_ge(s["h_act"], hcount(layer, 0, 0) + 1)
                high(0)
                base = n_hi[0]
                assert base == n0 + 3
                with act.Fori(0, (MLP_GROUPS - 1) // 3) as it:
                    for j in range(3):
                        nu = n0 + 1 + 2 * j
                        for w in range(2):
                            n = nu + 2 + w
                            slot = n % RING
                            landed = act.snap(it * 32 + 16 * (n // RING + 1))
                            done = act.snap(it * 6 + (n - RING + 1))
                            act.wait_ge(s[f"raw_landed{slot}"], landed)
                            act.wait_ge(s["w_done"], done)
                            a.activation(whi[:, slot, :], raw[:, slot, :], ACT.Copy).then_inc(s["hi_done"], 1)
                            if w == 0:
                                ready = act.snap(it * 6 + (nu + 1))
                                act.wait_ge(s["w_done"], ready)
                                hidden(4 + (j + 1) % 3, (j + 1) % 3)
                                own = act.snap(it * 3 + (hcount(layer, 0, j + 1) + 1))
                                act.wait_ge(s["h_act"], own)
                                high((j + 1) % 3)
                n_hi[0] = base + 2 * (MLP_GROUPS - 1)

            def ffn(layer):
                n0 = first[f"ffn{layer}"]
                sig = lambda slot: buf[1][:, 512 * slot : 512 * slot + 512]
                prod = lambda slot: buf[1][:, 1024 + 512 * slot : 1536 + 512 * slot]

                ahead(n0)
                act.wait_ge(s["w_done"], n0 + 1)
                a.activation(sig(0), bank(4), ACT.Silu).then_inc(s["h_act"], 1)
                act.wait_ge(s["p_turned"], layer + 1)
                a.activation(hh[:, P_SLOT, :], bank(0), ACT.Copy).then_inc(s["p_hi"], 1)
                ahead(n0 + 1)
                act.wait_ge(s["h_prod"], FFN_GROUPS * layer + 1)
                a.activation(hh[:, 0, :], prod(0), ACT.Copy).then_inc(s["h_hi"], 1)
                base = n_hi[0]
                assert base == n0 + 4
                with act.Fori(0, (FFN_GROUPS - 1) // 2) as it:
                    for j in range(2):
                        nu = n0 + 2 + 3 * j
                        sl = (j + 1) % 2
                        for w in range(3):
                            n = nu + 2 + w
                            slot = n % RING
                            landed = act.snap(it * 32 + 16 * (n // RING + 1))
                            done = act.snap(it * 6 + (n - RING + 1))
                            act.wait_ge(s[f"raw_landed{slot}"], landed)
                            act.wait_ge(s["w_done"], done)
                            a.activation(whi[:, slot, :], raw[:, slot, :], ACT.Copy).then_inc(s["hi_done"], 1)
                            if w == 0:
                                ready = act.snap(it * 6 + (nu + 1))
                                act.wait_ge(s["w_done"], ready)
                                a.activation(sig(sl), bank(4 + 2 * sl), ACT.Silu).then_inc(s["h_act"], 1)
                            if w == 1:
                                ready = act.snap(it * 2 + (FFN_GROUPS * layer + j + 2))
                                act.wait_ge(s["h_prod"], ready)
                                a.activation(hh[:, sl, :], prod(sl), ACT.Copy).then_inc(s["h_hi"], 1)
                n_hi[0] = base + 3 * (FFN_GROUPS - 1)

            def attention(kind, units):
                n_units = len(units)
                base = kind * ATT_BASE

                def exps(u):
                    b, g = units[u]
                    n = P * (b + 1)
                    act.wait_ge(s["negmax"], base + u + 1)
                    for h in range(4):
                        v = logit[:, u % 2, n * h : n * h + n]
                        last = a.activation(v, v, ACT.Exp, bias=negmax[:, u % 2, h : h + 1], accum_out=rowsum[:, b, 4 * g + h : 4 * g + h + 1])
                    last.then_inc(s["exp_done"], 1)

                def copies(u):
                    b, g = units[u]
                    act.wait_ge(s["probs_turned"], base + u + 1)
                    if b == 0:
                        a.activation(probT[:, u % 2, 0:256], ps[:, 4, 0:256], ACT.Copy).then_inc(s["probT_act"], 1)
                    else:
                        a.activation(probT[:, u % 2, 0:512], bank(4), ACT.Copy).then_inc(s["probT_act"], 1)

                exps(0)
                for u in range(n_units):
                    if u + 1 < n_units:
                        exps(u + 1)
                    copies(u)

            def reference_exps(c, lv):
                m = LEVELS[lv]
                G = g4[c - 1]
                act.wait_ge(s["summed"], c)
                if c == 2:
                    act.wait_ge(s["zed_done"], 8 * c - 1 + lv)
                for h in range(4):
                    for b in range(SEQ // (2 * m)):
                        c0 = 2 * m * b
                        e0 = SEQ * h + c0
                        r = (c0 + m) // 64 - 1
                        a.activation(expo[lv][:, e0 : e0 + m], G[:, h, c0 : c0 + m], ACT.Exp, scale=-1.0, bias=G[:, h, c0 + m - 1 : c0 + m])
                        last = a.activation(expo[lv][:, e0 + m : e0 + 2 * m], G[:, h, c0 + m : c0 + 2 * m], ACT.Exp,
                                            bias=negref[:, c - 1, h, r : r + 1])
                last.then_inc(s["expo_done"], 1)

            def decay_levels(c, levels, scale):
                for lv in levels:
                    if c > 0 and lv < 2:
                        reference_exps(c, lv)
                    elif lv < 8:
                        act.wait_ge(s["diff_done"], diffs(c, lv))
                        a.activation(expo[lv % 2], expo[lv % 2], ACT.Exp, scale=scale).then_inc(s["expo_done"], 1)

            def decay_squares(sets, hd):
                base = TT * (len(sets) - 1)
                for tt in range(TT):
                    act.wait_ge(s["decay_pv"], base + tt + 1)
                    if base + tt:
                        act.wait_ge(s["ss_done"], base + tt)
                    for m, c in enumerate(sets):
                        for h in range(4):
                            last = a.activation(rot4[:, h, P * m : P * m + hd], decay_out(c, tt, h, hd), ACT.Square,
                                                accum_out=ss[:, tt, 4 * m + h : 4 * m + h + 1])
                    last.then_inc(s["ss_done"], 1)

            def ple(layer, j):
                n0 = first[f"ple{layer}"]
                act.wait_ge(s["w_done"], n0 + 1)
                for u in range(4):
                    a.activation(side[:, u // 2, 512 * (u % 2) : 512 * (u % 2) + 512], bank(4 + u), ACT.Copy).then_inc(s["side_out"], 1)
                ahead(n0)
                turned(j)
                for q in range(4):
                    ahead(n0 + 1 + q)
                for u in range(4):
                    if u == 0:
                        act.wait_ge(s["gate_done"], layer + 1)
                    if u == 2:
                        act.wait_ge(s["w_done"], n0 + 5)
                    a.activation(y[:, u // 2, 512 * (u % 2) : 512 * (u % 2) + 512], bank(u), ACT.Sigmoid).then_inc(s["sig_done"], 1)

            turned(T_X0)
            ahead(1)
            for w, (sn, cs) in enumerate(((sinA, cosA), (sinM, cosM))):
                act.wait_ge(s["angle_done"], w + 1)
                a.activation(sn[:, :, :], cs[:, :, :], ACT.Sin)
                a.activation(cs[:, :, :], cs[:, :, :], ACT.Sin, scale=0.5).then_inc(s["sines_done"], 1)
            ahead(first["dsa_kvi"] + 1)
            act.wait_ge(s["lb_diff"], 1)
            a.activation(lbv[:, 1:3, :], lbv[:, 1:3, :], ACT.Exp).then_inc(s["lb_exp"], 1)
            act.wait_ge(s["lb_done"], 1)
            a.activation(lbv[:, 4:6, :], lbv[:, 4:6, :], ACT.Ln).then_inc(s["lb_ln"], 1)

            for q in range(4):
                ahead(first["dsa_kvi"] + q)
            act.wait_ge(s["w_done"], first["dsa_kvi"] + 4)
            for c in range(2):
                a.activation(kvi[:, 0, 512 * c : 512 * c + 512], bank(c), ACT.Copy).then_inc(s["kvi_act"], 1)
            ahead(first["dsa_small"])
            act.wait_ge(s["w_done"], first["dsa_small"] + 1)
            for tt in range(TT):
                a.activation(ikw[:, tt, :], bank(4 + tt, A_SMALL), ACT.Copy).then_inc(s["small_out"], 1)
            ahead(first["dsa_q"] + 1)
            for tt in range(TT):
                act.wait_ge(s["index_turned"], tt + 1)
                a.activation(iqT[:, :, P * tt : P * tt + P], bank(6 + tt).rearrange("p (k n) -> p k n", k=4), ACT.Copy).then_inc(s["indexT_done"], 1)
                for e in range(2):
                    r = slice(64 * e, 64 * e + 64)
                    last = a.activation(ikT[r, e, P * tt : P * tt + P], ps[r, 4 + tt, 0:P], ACT.Copy)
                last.then_inc(s["indexT_done"], 1)
            for u, (b, hs) in enumerate(INDEX_UNITS):
                act.wait_ge(s["index_scores"], u + 1)
                if u >= 4:
                    act.wait_ge(s["index_added"], u - 3)
                a.activation(relu_s[:, u % 4, :], bank(4 + u % 4), ACT.Relu, scale=float(A_HD**-0.5)).then_inc(s["index_relu"], 1)
            ahead(first["dsa_q"] + 2)
            ahead(first["dsa_q"] + 3)
            act.wait_ge(s["w_done"], first["dsa_q"] + 4)
            for u in range(4):
                a.activation(qtok[:, u // 2, 512 * (u % 2) : 512 * (u % 2) + 512], bank(u), ACT.Copy).then_inc(s["q_out"], 1)
            for tt in range(TT):
                act.wait_ge(s["k_turned"], tt + 1)
                for e in range(2):
                    r = slice(64 * e, 64 * e + 64)
                    last = a.activation(kT[r, :, e, P * tt : P * tt + P], ps[r, 4 + tt, :].rearrange("p (k n) -> p k n", k=4), ACT.Copy)
                last.then_inc(s["kT_done"], 1)
            for u in range(4):
                tt, hf = u // 2, u % 2
                act.wait_ge(s["q_turned"], u + 1)
                a.activation(qT[:, 4 * hf : 4 * hf + 4, P * tt : P * tt + P], bank((6 if tt == 0 else 4) + hf).rearrange("p (k n) -> p k n", k=4),
                             ACT.Copy).then_inc(s["qT_done"], 1)
            attention(0, ATT_UNITS[0])
            turned(T_DSA)
            for q in range(4):
                ahead(first["dsa_o"] + q)
            turned(T_X1)
            mlp(0)
            ahead(first["gla_low"] - 1)
            turned(T_X2)

            ahead(first["gla_low"])
            act.wait_ge(s["w_done"], first["gla_low"] + 1)
            a.activation(alow[:, :, :], ps[:, 4:6, 0:B_RANK], ACT.Copy).then_inc(s["low_out"], 1)
            act.wait_ge(s["low_turned"], 1)
            a.activation(alowT[:, :], ps[0:B_RANK, 4, 0:SEQ], ACT.Copy).then_inc(s["lowT_done"], 1)
            for q in range(4):
                n = first["gla_qk"] + q
                ahead(n)
                act.wait_ge(s["w_done"], n + 1)
                dst = (q4[0] if q < 2 else k4[0])[:, 2 * (q % 2) : 2 * (q % 2) + 2, :].rearrange("p h n -> p (h n)")
                a.activation(dst, bank(q), ACT.Copy, scale=float(P**-0.5) if q < 2 else 1.0).then_inc(s["qk_out"], 1)
                if q == 0:
                    act.wait_ge(s["gates"], 1)
                    for h in range(4):
                        last = a.activation(expo[0][:, 256 * h : 256 * h + 256], ps[:, 6 + h // 2, 256 * (h % 2) : 256 * (h % 2) + 256],
                                            ACT.Identity, bias=vcol[:, V_BA + h : V_BA + h + 1])
                    step(last)
                if q == 0:
                    step(a.activation(expo[1], expo[0], ACT.Abs))
                if q == 1:
                    step(a.activation(expo[1], expo[1], ACT.Exp, scale=-1.0))
                if q == 2:
                    a.activation(expo[1], expo[1], ACT.Ln, bias=1.0).then_inc(s["tail_done"], 1)
            for q in range(4):
                ahead(first["gla_v"] + q)
                decay_levels(0, GLA_LEVELS[q], 1.0 / 16.0)
            act.wait_ge(s["w_done"], first["gla_v"] + 4)
            for u in range(4):
                a.activation(vtok[:, u // 2, 512 * (u % 2) : 512 * (u % 2) + 512], bank(u), ACT.Copy).then_inc(s["v_out"], 1)
            for q in range(4):
                ahead(first["gla_r"] + q)
                decay_levels(0, GLA_LEVELS[q + 4], 1.0 / 16.0)
            act.wait_ge(s["w_done"], first["gla_r"] + 4)
            for u in range(4):
                a.activation(gate[:, u // 2, 512 * (u % 2) : 512 * (u % 2) + 512], bank(u), ACT.Silu).then_inc(s["r_out"], 1)
            decay_squares([0], 256)
            turned(T_GLA)
            for q in range(4):
                ahead(first["gla_o"] + q)
            turned(T_X3)
            mlp(1)
            ahead(first["mla_down"] - 1)
            turned(T_X4)

            for q in range(3):
                ahead(first["mla_down"] + q)
            act.wait_ge(s["w_done"], first["mla_down"] + 3)
            for tt in range(TT):
                for w in range(2):
                    last = a.activation(rot4[:, 2 * tt + w, :], ps[:, tt, 256 * w : 256 * w + 256], ACT.Square, accum_out=ss[:, tt, w : w + 1])
                last.then_inc(s["lat_squares"], 1)
                a.activation(krtok[:, tt, :], bank(2 + tt, M_ROPE), ACT.Copy).then_inc(s["kr_out"], 1)
            for tt in range(TT):
                act.wait_ge(s["latT_full"], tt + 1)
                a.activation(xh[:, 0:4, P * tt : P * tt + P], lat[:, tt, :].rearrange("p (k n) -> p k n", k=4), ACT.Copy).then_inc(s["latT_hi"], 1)
            act.wait_ge(s["kr_turned"], 1)
            for e in range(2):
                r = slice(64 * e, 64 * e + 64)
                last = a.activation(krT[r, e, :], ps[r, 6, 0:SEQ], ACT.Copy)
            last.then_inc(s["krT_done"], 1)
            for c in range(2):
                n = first["mla_q"] + c
                ahead(n)
                act.wait_ge(s["w_done"], n + 1)
                for u in range(2):
                    a.activation(qnT[:, 4 * c + 2 * u : 4 * c + 2 * u + 2, :].rearrange("p h n -> p (h n)"), bank(u), ACT.Copy).then_inc(s["qn_out"], 1)
            for c in range(2):
                n = first["mla_kv"] + c
                ahead(n)
                act.wait_ge(s["w_done"], n + 1)
                for u in range(2):
                    a.activation(knT[:, 4 * c + 2 * u : 4 * c + 2 * u + 2, :].rearrange("p h n -> p (h n)"), bank(u), ACT.Copy).then_inc(s["kn_out"], 1)
            for tt in range(TT):
                act.wait_ge(s["qr_turned"], tt + 1)
                a.activation(qrT[:, :, P * tt : P * tt + P], bank(4 + tt).rearrange("p (k n) -> p k n", k=4), ACT.Copy).then_inc(s["qrT_done"], 1)
            attention(1, ATT_UNITS[1])
            turned(T_MLA)
            for q in range(4):
                ahead(first["mla_o"] + q)
            turned(T_X5)
            ffn(0)
            ahead(first["ple0"] - 1)
            ple(0, T_X6)

            turned(T_X7)
            ahead(first["hgrn_f"] - 1)
            for q in range(4):
                n = first["hgrn_f"] + q
                ahead(n)
                act.wait_ge(s["w_done"], n + 1)
                w, cs = q // 2, slice(512 * (q % 2), 512 * (q % 2) + 512)
                a.activation(expo[w][:, cs], bank(q), ACT.Copy).then_inc(s["f_copied"], 1)
                a.activation(k4[w][:, 2 * (q % 2) : 2 * (q % 2) + 2, :].rearrange("p h n -> p (h n)"), bank(q), ACT.Sigmoid, scale=-1.0).then_inc(s["k_sig"], 1)
                a.activation(zed[w][:, cs], bank(q), ACT.Abs).then_inc(s["f_out"], 1)
            for q in range(4):
                n = first["hgrn_q"] + q
                ahead(n)
                for w in range(2):
                    if q == 0:
                        act.wait_ge(s["f_out"], 2 * w + 2)
                        a.activation(zed[w], zed[w], ACT.Exp, scale=-1.0).then_inc(s["tail_exp"], 1)
                    if q == 1:
                        act.wait_ge(s["tail_exp"], w + 1)
                        a.activation(zed[w], zed[w], ACT.Ln, bias=1.0).then_inc(s["tail_done"], 1)
                    if q == 2:
                        act.wait_ge(s["gap_done"], w + 1)
                        a.activation(zed[w], g4[w].rearrange("p h n -> p (h n)"), ACT.Abs).then_inc(s["gap_abs"], 1)
                if q == 2:
                    for w in range(2):
                        act.wait_ge(s["gap_abs"], w + 1)
                        a.activation(zed[w], zed[w], ACT.Exp, scale=-1.0).then_inc(s["tail_exp"], 1)
                if q == 3:
                    for w in range(2):
                        act.wait_ge(s["tail_exp"], w + 3)
                        a.activation(zed[w], zed[w], ACT.Ln, bias=1.0).then_inc(s["tail_done"], 1)
            act.wait_ge(s["w_done"], first["hgrn_q"] + 4)
            for q in range(4):
                a.activation(q4[q // 2][:, 2 * (q % 2) : 2 * (q % 2) + 2, :].rearrange("p h n -> p (h n)"), bank(4 + q), ACT.Silu).then_inc(s["qk_out"], 1)
            for q in range(4):
                ahead(first["hgrn_v"] + q)
                for c in (1, 2):
                    decay_levels(c, HGRN_LEVELS[q][c], 1.0)
            act.wait_ge(s["w_done"], first["hgrn_v"] + 4)
            for u in range(4):
                a.activation(vtok[:, u // 2, 512 * (u % 2) : 512 * (u % 2) + 512], bank(u), ACT.Copy).then_inc(s["v_out"], 1)
            for q in range(4):
                ahead(first["hgrn_gate"] + q)
                for c in (1, 2):
                    decay_levels(c, HGRN_LEVELS[q + 4][c], 1.0)
            act.wait_ge(s["w_done"], first["hgrn_gate"] + 4)
            for u in range(4):
                a.activation(gate[:, u // 2, 512 * (u % 2) : 512 * (u % 2) + 512], bank(u), ACT.Silu).then_inc(s["r_out"], 1)
            decay_squares([1, 2], P)
            turned(T_HGRN)
            for q in range(4):
                ahead(first["hgrn_o"] + q)
            turned(T_X8)
            ffn(1)
            ahead(first["ple1"] - 1)
            ple(1, T_X9)

        @block.vector
        def _(dve):
            n_step = [0]
            n_lo = [0]
            v = nc.vector

            def step(ins):
                ins.then_inc(s["dve_step"], 1)
                n_step[0] += 1
                dve.wait_ge(s["dve_step"], n_step[0])

            def lo_part(n):
                slot, w = n % RING, width[n]
                dve.wait_ge(s["hi_done"], n + 1)
                v.tensor_tensor(wlo[:, slot, 0:w], raw[:, slot, 0:w], whi[:, slot, 0:w].bitcast(F32), ALU.subtract).then_inc(s["lo_done"], 1)

            def ahead(n):
                while n_lo[0] <= min(n + 2, N_CHUNKS - 1):
                    lo_part(n_lo[0])
                    n_lo[0] += 1

            def turned(j, tt):
                for hf in range(2):
                    u = 2 * tt + hf
                    dve.wait_ge(s["turn_hi"], 4 * j + u + 1)
                    hi = xh[:, 4 * hf : 4 * hf + 4, P * tt : P * tt + P]
                    lo = xl[:, 4 * hf : 4 * hf + 4, P * tt : P * tt + P]
                    v.tensor_tensor(lo, bank(4 + u).rearrange("p (k n) -> p k n", k=4), hi.bitcast(F32), ALU.subtract).then_inc(s["turn_lo"], 1)

            def rsqrt(o, val, tmp):
                step(v.tensor_scalar(o.bitcast(I32), val.bitcast(I32), 1, None, ALU.logical_shift_right))
                v.tensor_scalar(val, val, 64.0, None, ALU.mult)
                step(v.tensor_scalar(o.bitcast(I32), o.bitcast(I32), -1.0, RSQRT_SEED_8, ALU.mult, ALU.add))
                for m in range(3):
                    step(v.tensor_tensor(tmp, o, o, ALU.mult))
                    step(v.tensor_tensor(tmp, tmp, val, ALU.mult))
                    if m < 2:
                        v.tensor_scalar(val, val, 0.25, None, ALU.mult)
                    step(v.scalar_tensor_tensor(o, tmp, -3.0, o, ALU.add, ALU.mult))

            def layer_norm(i, n_last, j):
                def sums(tt, q):
                    c = q % 2
                    cs = slice(512 * c, 512 * c + 512)
                    if q < 2:
                        v.scalar_tensor_tensor(y[:, tt, cs], x[:, tt, cs], ALPHA, bank(2 * tt + c), ALU.mult, ALU.add).then_inc(s["resid"], 1)
                    else:
                        dve.wait_ge(s["resid"], 4 * i + 2 * tt + c + 1)
                        v.bn_stats(stats[:, tt, c, :], y[:, tt, cs]).then_inc(s["stats_done"], 1)

                def root(tt, between):
                    c0 = 8 * tt
                    val, r, tmp = small[:, c0 : c0 + 4], small[:, c0 + 4 : c0 + 5], small[:, c0 + 5 : c0 + 6]

                    def link(k, ins):
                        ins.then_inc(s["dve_step"], 1)
                        n_step[0] += 1
                        own = n_step[0]
                        between(k)
                        dve.wait_ge(s["dve_step"], own)

                    dve.wait_ge(s["stats_done"], 4 * i + 2 * tt + 2)
                    step(v.bn_aggr(mv[:, tt, :], stats[:, tt, :, :].rearrange("p a b -> p (a b)")))
                    for c, factor in enumerate((64.0, 16.0, 4.0, 1.0)):
                        last = v.tensor_scalar(val[:, c : c + 1], mv[:, tt, 1:2], LN_EPS, factor, ALU.add, ALU.mult)
                    step(last)
                    link(0, v.tensor_scalar(r.bitcast(I32), val[:, 3:4].bitcast(I32), 1, None, ALU.logical_shift_right))
                    link(1, v.tensor_scalar(r.bitcast(I32), r.bitcast(I32), -1.0, RSQRT_SEED_8, ALU.mult, ALU.add))
                    for m in range(3):
                        link(2 + 2 * m, v.scalar_tensor_tensor(tmp, r, val[:, m : m + 1], r, ALU.mult, ALU.mult))
                        link(3 + 2 * m, v.scalar_tensor_tensor(r, tmp, -3.0, r, ALU.add, ALU.mult))

                def gain(tt, cs):
                    return v.scalar_tensor_tensor(y[:, tt, cs], y[:, tt, cs], mv[:, tt, 0:1], lnw[:, 0, cs], ALU.subtract, ALU.mult).then_inc(s["gained"], 1)

                def finish(tt, cs):
                    return v.scalar_tensor_tensor(x[:, tt, cs], y[:, tt, cs], small[:, 8 * tt + 4 : 8 * tt + 5], lnw[:, 1, cs], ALU.mult, ALU.add)

                def between_first(k):
                    if k == 0:
                        dve.wait_ge(s["w_done"], n_last + 1)
                    if k < 4:
                        sums(1, k)

                def between_second(k):
                    cs = slice(256 * (k % 4), 256 * (k % 4) + 256)
                    if k < 4:
                        gain(0, cs)
                    else:
                        dve.wait_ge(s["gained"], 6 * i + k - 3)
                        last = finish(0, cs)
                        if k % 2:
                            last.then_inc(s["src_ready"], 1)

                dve.wait_ge(s["acc_done"], i + 1)
                for q in range(4):
                    sums(0, q)
                if i % 2:
                    root(0, between_first)
                else:
                    root(0, lambda k: None)
                    for k in range(4):
                        between_first(k)
                dve.wait_ge(s["ln_landed"], 32 * (i + 1))
                root(1, between_second)
                for hf in range(2):
                    cs = slice(512 * hf, 512 * hf + 512)
                    gain(1, cs)
                    dve.wait_ge(s["gained"], 6 * i + 5 + hf)
                    finish(1, cs).then_inc(s["src_ready"], 1)
                    if hf == 0:
                        turned(j, 0)
                        if j in (T_X4, T_X6, T_X9):
                            ahead(n_last + (j != T_X4))
                turned(j, 1)
                ahead(n_last)

            def output_operand(j):
                for tt in range(TT):
                    turned(j, tt)

            def mlp(layer):
                n0 = first[f"mlp{layer}"]

                def full(slot):
                    r = buf[slot // 2][:, 512 * (slot % 2) : 512 * (slot % 2) + 512]
                    return v.tensor_tensor(buf[2][:, 512 * slot : 512 * slot + 512], r, r, ALU.mult).then_inc(s["h_full"], 1)

                def low(slot):
                    v.tensor_tensor(hl[:, slot, :], buf[2][:, 512 * slot : 512 * slot + 512], hh[:, slot, :].bitcast(F32), ALU.subtract).then_inc(s["h_lo"], 1)

                ahead(n0)
                dve.wait_ge(s["h_act"], hcount(layer, 0, 0) + 1)
                full(0)
                dve.wait_ge(s["h_hi"], hcount(layer, 0, 0) + 1)
                dve.wait_ge(s["h_full"], MLP_GROUPS * layer + 1)
                low(0)
                base = n_lo[0]
                with dve.Fori(0, (MLP_GROUPS - 1) // 3) as it:
                    for j in range(3):
                        nu = n0 + 1 + 2 * j
                        for w in range(2):
                            n = nu + 2 + w
                            slot = n % RING
                            ready = dve.snap(it * 6 + (n + 1))
                            dve.wait_ge(s["hi_done"], ready)
                            v.tensor_tensor(wlo[:, slot, :], raw[:, slot, :], whi[:, slot, :].bitcast(F32), ALU.subtract).then_inc(s["lo_done"], 1)
                            if w == 0:
                                sl = (j + 1) % 3
                                ready = dve.snap(it * 3 + (hcount(layer, 0, j + 1) + 1))
                                dve.wait_ge(s["h_act"], ready)
                                full(sl)
                                ready = dve.snap(it * 3 + (hcount(layer, 0, j + 1) + 1))
                                own = dve.snap(it * 3 + (MLP_GROUPS * layer + j + 2))
                                dve.wait_ge(s["h_hi"], ready)
                                dve.wait_ge(s["h_full"], own)
                                low(sl)
                n_lo[0] = base + 2 * (MLP_GROUPS - 1)

            def ffn(layer):
                n0 = first[f"ffn{layer}"]
                sig = lambda slot: buf[1][:, 512 * slot : 512 * slot + 512]
                prod = lambda slot: buf[1][:, 1024 + 512 * slot : 1536 + 512 * slot]

                ahead(n0)
                ahead(n0 + 1)
                dve.wait_ge(s["p_hi"], layer + 1)
                v.tensor_tensor(hl[:, P_SLOT, :], bank(0), hh[:, P_SLOT, :].bitcast(F32), ALU.subtract).then_inc(s["p_lo"], 1)
                dve.wait_ge(s["h_act"], hcount(layer, 1, 0) + 1)
                dve.wait_ge(s["w_done"], n0 + 2)
                v.tensor_tensor(prod(0), sig(0), bank(5), ALU.mult).then_inc(s["h_prod"], 1)
                dve.wait_ge(s["h_hi"], hcount(layer, 1, 0) + 1)
                v.tensor_tensor(hl[:, 0, :], prod(0), hh[:, 0, :].bitcast(F32), ALU.subtract).then_inc(s["h_lo"], 1)
                base = n_lo[0]
                with dve.Fori(0, (FFN_GROUPS - 1) // 2) as it:
                    for j in range(2):
                        nu = n0 + 2 + 3 * j
                        sl = (j + 1) % 2
                        for w in range(3):
                            n = nu + 2 + w
                            slot = n % RING
                            ready = dve.snap(it * 6 + (n + 1))
                            dve.wait_ge(s["hi_done"], ready)
                            v.tensor_tensor(wlo[:, slot, :], raw[:, slot, :], whi[:, slot, :].bitcast(F32), ALU.subtract).then_inc(s["lo_done"], 1)
                            if w == 1:
                                a_ready = dve.snap(it * 2 + (hcount(layer, 1, j + 1) + 1))
                                w_ready = dve.snap(it * 6 + (nu + 2))
                                dve.wait_ge(s["h_act"], a_ready)
                                dve.wait_ge(s["w_done"], w_ready)
                                v.tensor_tensor(prod(sl), sig(sl), bank(5 + 2 * sl), ALU.mult).then_inc(s["h_prod"], 1)
                                ready = dve.snap(it * 2 + (hcount(layer, 1, j + 1) + 1))
                                dve.wait_ge(s["h_hi"], ready)
                                v.tensor_tensor(hl[:, sl, :], prod(sl), hh[:, sl, :].bitcast(F32), ALU.subtract).then_inc(s["h_lo"], 1)
                n_lo[0] = base + 3 * (FFN_GROUPS - 1)

            def attention(kind, units, bias_of, scale, heads):
                n_units = len(units)
                base = kind * ATT_BASE
                hd = D // heads

                def prepare(u):
                    b, g = units[u]
                    n = P * (b + 1)
                    dve.wait_ge(s["logits"], base + u + 1)
                    if u >= 2:
                        dve.wait_ge(s["probs_turned"], base + u - 1)
                    src = banks(2 * (u % 2), 2)[:, 0 : 4 * n].rearrange("p (h n) -> p h n", h=4)
                    dst = logit[:, u % 2, 0 : 4 * n].rearrange("p (h n) -> p h n", h=4)
                    bb = bias_of(b)[:, 0:n].unsqueeze(1).broadcast_to([P, 4, n])
                    v.scalar_tensor_tensor(dst, src, scale, bb, ALU.mult, ALU.add).then_inc(s["logit_read"], 1)
                    dve.wait_ge(s["logit_read"], base + u + 1)
                    v.tensor_reduce(negmax[:, u % 2, :], dst, AX_X, ALU.max, negate=True).then_inc(s["negmax"], 1)

                def copies(u):
                    b, g = units[u]
                    if b == 0:
                        dve.wait_ge(s["probT_act"], base + u + 1)
                        v.tensor_copy(probT[:, u % 2, 256:512], ps[:, 4, 256:512]).then_inc(s["probT_dve"], 1)
                    else:
                        dve.wait_ge(s["probs_turned"], base + u + 1)
                        v.tensor_copy(probT[:, u % 2, 512:1024], bank(5)).then_inc(s["probT_dve"], 1)

                def output(b, j):
                    step(v.reciprocal(rinv[:, b, 0:heads], rowsum[:, b, 0:heads]))
                    dve.wait_ge(s["att_pv"], base + n_units // 2 * (b + 1))
                    v.tensor_tensor(y[:, b, :].rearrange("p (h d) -> p h d", h=heads), banks(6, 2).rearrange("p (h d) -> p h d", h=heads),
                                    rinv[:, b, 0:heads].unsqueeze(2).broadcast_to([P, heads, hd]), ALU.mult).then_inc(s["src_ready"], 2)

                prepare(0)
                prepare(1)
                for u in range(n_units):
                    copies(u)
                    if u + 2 < n_units:
                        prepare(u + 2)
                    if u == n_units // 2 - 1:
                        output(0, 0)
                output(1, 0)

            def blocks(ap, lv):
                return ap.rearrange("p (b e n) -> p b e n", e=2, n=LEVELS[lv])

            def diff(c, lv):
                m = LEVELS[lv]
                nb = 1024 // (2 * m)
                if lv >= 2:
                    dve.wait_ge(s["zed_done"], 8 * c + lv - 1)
                G = g4[int(c == 2)].rearrange("p h n -> p (h n)")
                gb, eb = blocks(G, lv), blocks(expo[lv % 2], lv)
                ref = gb[:, :, 0, m - 1 : m].broadcast_to([P, nb, m])
                v.tensor_tensor(eb[:, :, 0, :], ref, gb[:, :, 0, :], ALU.subtract)
                v.tensor_tensor(eb[:, :, 1, :], gb[:, :, 1, :], ref, ALU.subtract).then_inc(s["diff_done"], 1)

            def operand(c, lv):
                Q = q4[int(c == 2)].rearrange("p h n -> p (h n)")
                K = k4[int(c == 2)].rearrange("p h n -> p (h n)")
                dve.wait_ge(s["expo_done"], 8 * c + lv + 1)
                if lv >= 2:
                    dve.wait_ge(s["level_done"], 9 * c + lv - 1)
                elif c == 2:
                    dve.wait_ge(s["level_done"], 9 * c + lv - 2)
                eb, zb = blocks(expo[lv % 2], lv), blocks(zed[lv % 2], lv)
                v.tensor_tensor(zb[:, :, 0, :], blocks(K, lv)[:, :, 0, :], eb[:, :, 0, :], ALU.mult)
                v.tensor_tensor(zb[:, :, 1, :], blocks(Q, lv)[:, :, 1, :], eb[:, :, 1, :], ALU.mult).then_inc(s["zed_done"], 1)

            def pick(c, lv):
                own, past = att_own[int(c == 2)], att_past[int(c == 2)]
                dve.wait_ge(s["level_done"], 9 * c + lv + 1)
                if lv >= 2:
                    dve.wait_ge(s["level_read"], 9 * c + lv)
                if lv == 0:
                    v.tensor_copy(past, bank(4).rearrange("p (h n) -> p h n", h=4)).then_inc(s["level_read"], 1)
                    return
                b0 = 4 + 2 * (lv % 2)
                mk = masks[:, lv - 1, :].bitcast(I32).unsqueeze(1).broadcast_to([P, 2, P])
                for h in range(4):
                    src = ps[:, b0 + h // 2, 256 * (h % 2) : 256 * (h % 2) + 256].rearrange("p (t n) -> p t n", t=2)
                    last = v.copy_predicated(own[:, h, :, :], mk, src)
                last.then_inc(s["level_read"], 1)

            def decay_levels(c, levels):
                for lv in levels:
                    if lv < 8:
                        operand(c, lv)
                    if lv + 2 < 8:
                        diff(c, lv + 2)
                    if lv >= 1:
                        pick(c, lv - 1)
                    if lv == 8:
                        pick(c, 8)

            def decay_output(sets, hd, j):
                n = 4 * len(sets)
                for tt in range(TT):
                    c0 = 16 * tt
                    val, r, tmp = small[:, c0 : c0 + n], small[:, c0 + 8 : c0 + 8 + n], small[:, 32 + c0 : 32 + c0 + n]
                    dve.wait_ge(s["ss_done"], TT * (len(sets) - 1) + tt + 1)
                    step(v.tensor_scalar(val, ss[:, tt, 0:n], 1.0 / hd, RMS_EPS, ALU.mult, ALU.add))
                    rsqrt(r, val, tmp)
                    for m, c in enumerate(sets):
                        for h in range(4):
                            cs = slice(vcol0(c) + hd * h, vcol0(c) + hd * h + hd)
                            last = v.scalar_tensor_tensor(y[:, tt, cs], decay_out(c, tt, h, hd), r[:, 4 * m + h : 4 * m + h + 1], gate[:, tt, cs], ALU.mult, ALU.mult)
                    last.then_inc(s["src_ready"], 2)
                for tt in range(TT):
                    turned(j, tt)

            def gated(n_gate, n_landed):
                dve.wait_ge(s["r_out"], n_gate)
                dve.wait_ge(s["gn_landed"], n_landed)
                for tt in range(TT):
                    last = v.tensor_tensor(gate[:, tt, :], gate[:, tt, :], gn, ALU.mult)
                step(last)

            def ple(layer, j):
                n0 = first[f"ple{layer}"]
                for q in range(4):
                    ahead(n0 + 1 + q)
                dve.wait_ge(s["side_out"], 4 * layer + 4)
                for u in range(4):
                    tt, cs = u // 2, slice(512 * (u % 2), 512 * (u % 2) + 512)
                    dve.wait_ge(s["sig_done"], 4 * layer + u + 1)
                    step(v.tensor_tensor(y[:, tt, cs], y[:, tt, cs], side[:, tt, cs], ALU.mult))
                    last = v.tensor_tensor(x[:, tt, cs], x[:, tt, cs], y[:, tt, cs], ALU.add)
                    if layer == 0:
                        last.then_inc(s["src_ready"], 1)
                    elif u % 2:
                        last.then_inc(s["out_ready"], 1)

            for tt in range(TT):
                turned(T_X0, tt)
            ahead(0)
            dve.wait_ge(s["pos_landed"], 32)
            dve.wait_ge(s["inv_done"], 1)
            step(v.tensor_copy(posf[:, :, :], posi[:, :, :]))
            for w, (sn, cs, c0, n) in enumerate(((sinA, cosA, 0, ROT), (sinM, cosM, ROT, M_HALF))):
                for tt in range(TT):
                    last = v.tensor_scalar(cs[:, tt, :], inv[:, c0 : c0 + n], posf[:, w, tt : tt + 1], None, ALU.mult)
                step(last)
                step(v.tensor_scalar(sn[:, :, :], cs[:, :, :], 1.0 / TWO_PI, MAGIC, ALU.mult, ALU.add))
                step(v.tensor_scalar(sn[:, :, :], sn[:, :, :], -MAGIC, None, ALU.add))
                for part in (PI_A, PI_B, PI_C):
                    step(v.scalar_tensor_tensor(cs[:, :, :], sn[:, :, :], -part, cs[:, :, :], ALU.mult, ALU.add))
                v.tensor_scalar(cs[:, :, :], cs[:, :, :], PI_MAX, -PI_MAX, ALU.min, ALU.max).then_inc(s["angle_done"], 1)
            ahead(first["dsa_kvi"] + 1)
            for w, cs in enumerate((cosA, cosM)):
                dve.wait_ge(s["sines_done"], w + 1)
                step(v.tensor_tensor(cs[:, :, :], cs[:, :, :], cs[:, :, :], ALU.mult))
                last = v.tensor_scalar(cs[:, :, :], cs[:, :, :], -2.0, 1.0, ALU.mult, ALU.add)
            last.then_inc(s["tables_done"], 1)
            dve.wait_ge(s["vrow_turned"], 1)
            v.tensor_copy(vcol[:, :], ps[:, 4, 0:V_ROWS]).then_inc(s["vcol_done"], 1)
            dve.wait_ge(s["vcol_done"], 1)
            l0, l1 = vcol[:, V_LB : V_LB + 8], vcol[:, V_LB + 8 : V_LB + 16]
            mx, e0, e1, sm, c1, a1, ga, one = (lbv[:, i, :] for i in range(8))
            step(v.tensor_tensor(mx, l0, l1, ALU.max))
            v.tensor_tensor(e0, l0, mx, ALU.subtract)
            v.tensor_tensor(e1, l1, mx, ALU.subtract).then_inc(s["lb_diff"], 1)
            dve.wait_ge(s["lb_exp"], 1)
            step(v.tensor_tensor(sm, e0, e1, ALU.add))
            step(v.reciprocal(sm, sm))
            v.tensor_tensor(e0, e0, sm, ALU.mult)
            step(v.tensor_tensor(e1, e1, sm, ALU.mult))
            step(v.tensor_tensor(e1, e0, e1, ALU.add))
            step(v.tensor_tensor(e1, e1, e0, ALU.subtract))
            step(v.tensor_scalar(one, e1, -1.0, 1.0, ALU.mult, ALU.add))
            v.tensor_scalar(c1, one, LN_FLOOR, None, ALU.max)
            v.tensor_scalar(a1, e1, LN_FLOOR, None, ALU.max).then_inc(s["lb_done"], 1)
            dve.wait_ge(s["lb_ln"], 1)
            step(v.tensor_tensor(ga, c1, a1, ALU.subtract))

            for q in range(4):
                ahead(first["dsa_kvi"] + q)
            dve.wait_ge(s["w_done"], first["dsa_kvi"] + 4)
            for c in range(2):
                v.tensor_copy(kvi[:, 1, 512 * c : 512 * c + 512], bank(2 + c)).then_inc(s["kvi_dve"], 1)
            ahead(first["dsa_small"])
            ahead(first["dsa_q"] + 1)
            dve.wait_ge(s["index_rotated"], TT)
            for u, (b, hs) in enumerate(INDEX_UNITS):
                dve.wait_ge(s["index_relu"], u + 1)
                n = P * (b + 1)
                for i, h in enumerate(hs):
                    w = ikw[:, b, A_HD + h : A_HD + h + 1]
                    rs = relu_s[:, u % 4, n * i : n * i + n]
                    if h == 0:
                        if b == 0:
                            step(v.memset(score[:, 0, P:SEQ], 0.0))
                        ins = v.tensor_scalar(score[:, b, 0:n], rs, w, None, ALU.mult)
                    else:
                        ins = v.scalar_tensor_tensor(score[:, b, 0:n], rs, w, score[:, b, 0:n], ALU.mult, ALU.add)
                    if i == len(hs) - 1:
                        ins.then_inc(s["index_added"], 1)
                        dve.wait_ge(s["index_added"], u + 1)
                    else:
                        step(ins)
            dve.wait_ge(s["score_masked"], TT)
            for r in range(TOPK // 8):
                for b in range(TT):
                    ins = v.max(top8[:, b, :], work[:, b, r % 2, :])
                step(ins)
                for b in range(TT):
                    ins = v.match_replace(work[:, b, 1 - r % 2, :], top8[:, b, :], work[:, b, r % 2, :], TAKEN)
                step(ins)
            for b in range(TT):
                v.tensor_scalar(work[:, b, 1, :], work[:, b, 0, :], 1.05 * NOT_CAUSAL, MASKED, ALU.is_gt, ALU.mult).then_inc(s["chosen"], 1)
            ahead(first["dsa_q"] + 3)
            dve.wait_ge(s["bias_done"], TT)
            attention(0, ATT_UNITS[0], lambda b: bias[:, b, :], float(A_HD**-0.5), A_HEADS)
            output_operand(T_DSA)
            for q in range(3):
                ahead(first["dsa_o"] + q)
            layer_norm(0, first["dsa_o"] + 3, T_X1)
            mlp(0)
            layer_norm(1, first["gla_low"] - 1, T_X2)

            ahead(first["gla_low"])
            for q in range(4):
                ahead(first["gla_qk"] + q)
            dve.wait_ge(s["tail_done"], 1)
            step(v.scalar_tensor_tensor(expo[1], expo[0], 0.0, expo[1], ALU.min, ALU.subtract))
            step(v.memset(zed[0][:, 0:SEQ], 1.0))
            for h in range(4):
                last = v.tensor_tensor_scan(g4[0][:, h, :], zed[0][:, 0:SEQ], expo[1][:, 256 * h : 256 * h + 256], 0.0, ALU.mult, ALU.add)
            step(last)
            diff(0, 0)
            diff(0, 1)
            dve.wait_ge(s["masks_done"], 1)
            dve.wait_ge(s["att_zeroed"], 1)
            dve.wait_ge(s["qk_out"], 4)
            for q in range(4):
                ahead(first["gla_v"] + q)
                decay_levels(0, GLA_LEVELS[q])
            for q in range(4):
                ahead(first["gla_r"] + q)
                decay_levels(0, GLA_LEVELS[q + 4])
            decay_levels(0, [8])
            gated(4, 64)
            decay_output([0], 256, T_GLA)
            for q in range(3):
                ahead(first["gla_o"] + q)
            layer_norm(2, first["gla_o"] + 3, T_X3)
            mlp(1)
            layer_norm(3, first["mla_down"] - 1, T_X4)

            for q in range(3):
                ahead(first["mla_down"] + q)
            dve.wait_ge(s["lat_squares"], TT)
            step(v.tensor_scalar(small[:, 16:20].rearrange("p (t w) -> p t w", t=TT), ss[:, :, 0:2], 1.0 / 256.0, RMS_EPS, ALU.mult, ALU.add))
            rsqrt(small[:, 24:28], small[:, 16:20], small[:, 32:36])
            for tt in range(TT):
                for w in range(2):
                    last = v.tensor_scalar(latn[:, tt, 256 * w : 256 * w + 256], ps[:, tt, 256 * w : 256 * w + 256],
                                           small[:, 24 + 2 * tt + w : 25 + 2 * tt + w], None, ALU.mult)
                last.then_inc(s["lat_done"], 1)
            for tt in range(TT):
                dve.wait_ge(s["lat_turned"], tt + 1)
                v.tensor_tensor(lat[:, tt, :].rearrange("p (k n) -> p k n", k=4), bank(4 + tt).rearrange("p (k n) -> p k n", k=4),
                                vcol[:, V_QN : V_QN + 4].unsqueeze(2).broadcast_to([P, 4, P]), ALU.mult).then_inc(s["latT_full"], 1)
            for tt in range(TT):
                dve.wait_ge(s["latT_hi"], tt + 1)
                dve.wait_ge(s["latT_full"], tt + 1)
                v.tensor_tensor(xl[:, 0:4, P * tt : P * tt + P], lat[:, tt, :].rearrange("p (k n) -> p k n", k=4),
                                xh[:, 0:4, P * tt : P * tt + P].bitcast(F32), ALU.subtract).then_inc(s["latT_lo"], 1)
            for c in range(2):
                n = first["mla_q"] + c
                ahead(n)
                dve.wait_ge(s["w_done"], n + 1)
                for tt in range(TT):
                    v.tensor_copy(qrtok[:, tt, 256 * c : 256 * c + 256], ps[:, 2 + tt, 0:256]).then_inc(s["qr_out"], 1)
            for c in range(2):
                n = first["mla_kv"] + c
                ahead(n)
                dve.wait_ge(s["w_done"], n + 1)
                for tt in range(TT):
                    v.tensor_copy(vM[:, tt, 512 * c : 512 * c + 512], bank(2 + tt)).then_inc(s["vM_out"], 1)
            dve.wait_ge(s["causal_done"], 1)
            attention(1, ATT_UNITS[1], lambda b: causal[:, b, :], M_SCALE, M_HEADS)
            output_operand(T_MLA)
            for q in range(3):
                ahead(first["mla_o"] + q)
            layer_norm(4, first["mla_o"] + 3, T_X5)
            ffn(0)
            layer_norm(5, first["ple0"] - 1, T_X6)
            ple(0, T_X6)

            output_operand(T_X7)
            ahead(first["hgrn_f"] - 1)
            for q in range(4):
                ahead(first["hgrn_f"] + q)

            def per_head(col, w):
                return col[:, 4 * w : 4 * w + 4].unsqueeze(2).broadcast_to([P, 4, SEQ])

            heads4 = lambda ap: ap.rearrange("p (h n) -> p h n", h=4)
            ahead(first["hgrn_q"])
            ahead(first["hgrn_q"] + 1)
            for w in range(2):
                dve.wait_ge(s["tail_done"], 2 + w)
                step(v.scalar_tensor_tensor(zed[w], expo[w], 0.0, zed[w], ALU.min, ALU.subtract))
                v.tensor_tensor(g4[w], heads4(zed[w]), per_head(ga, w), ALU.add).then_inc(s["gap_done"], 1)
            dve.wait_ge(s["k_sig"], 4)
            ahead(first["hgrn_q"] + 2)
            for w in range(2):
                v.tensor_tensor(k4[w], k4[w], per_head(one, w), ALU.mult)
            ahead(first["hgrn_q"] + 3)
            step(v.memset(rot4[:, 0, :], 1.0))
            for w in range(2):
                dve.wait_ge(s["tail_done"], 4 + w)
                step(v.scalar_tensor_tensor(zed[w], g4[w].rearrange("p h n -> p (h n)"), 0.0, zed[w], ALU.max, ALU.add))
                step(v.tensor_tensor(heads4(zed[w]), heads4(zed[w]), per_head(a1, w), ALU.add))
                for h in range(4):
                    last = v.tensor_tensor_scan(g4[w][:, h, :], rot4[:, 0, :], zed[w][:, 256 * h : 256 * h + 256], 0.0, ALU.mult, ALU.add)
                step(last)
                v.tensor_scalar(negref[:, w, :, :], g4[w][:, :, 63:192:64], -1.0, None, ALU.mult).then_inc(s["summed"], 1)
            dve.wait_ge(s["att_zeroed"], 2)
            dve.wait_ge(s["qk_out"], 8)
            for q in range(4):
                ahead(first["hgrn_v"] + q)
                for c in (1, 2):
                    decay_levels(c, HGRN_LEVELS[q][c])
            for q in range(4):
                ahead(first["hgrn_gate"] + q)
                for c in (1, 2):
                    decay_levels(c, HGRN_LEVELS[q + 4][c])
            gated(8, 80)
            decay_output([1, 2], P, T_HGRN)
            for q in range(3):
                ahead(first["hgrn_o"] + q)
            layer_norm(6, first["hgrn_o"] + 3, T_X8)
            ffn(1)
            layer_norm(7, first["ple1"] - 1, T_X9)
            ple(1, T_X9)


INDEX_UNITS = [(0, [0, 1, 2, 3]), (0, [4, 5, 6, 7])] + [(1, [2 * i, 2 * i + 1]) for i in range(4)]
GLA_LEVELS = [[], [0], [1], [2], [3], [4], [5, 6], [7]]
HGRN_LEVELS = [{1: [], 2: []}, {1: [0], 2: []}, {1: [1, 2], 2: []}, {1: [3, 4], 2: []},
               {1: [5, 6], 2: []}, {1: [7, 8], 2: []}, {1: [], 2: [0, 1, 2]}, {1: [], 2: [3, 4, 5, 6, 7, 8]}]
ATT_UNITS = [[(b, g) for b in range(TT) for g in range(n // 4)] for n in (A_HEADS, M_HEADS)]
ATT_BASE = len(ATT_UNITS[0])


def hcount(layer, kind, group):
    return (MLP_GROUPS * layer if kind == 0 else 2 * MLP_GROUPS + FFN_GROUPS * layer) + group


def diffs(c, lv):
    return lv + 1 if c == 0 else 8 + 6 * (c - 1) + lv - 1


def ready(j, tt, hf=1):
    return 2 * TT * (j - 1) + 2 * tt + hf + 1


def vcol0(c):
    return 512 if c == 2 else 0


INS = ["x", "positions", "a_w_in", "a_w_o", "b_w_in", "b_w_a2", "b_b_a", "b_g_norm", "b_w_o", "ln_mix_g", "ln_mix_b",
       "mlp_w_up", "mlp_w_down", "ln_mlp_g", "ln_mlp_b", "p_2", "positions_2", "mla_w_dqkv_2", "mla_q_norm_2",
       "mla_kv_norm_2", "mla_w_uq_2", "mla_w_ukv_2", "mla_w_o_2", "hgrn_w_in_2", "hgrn_lb_logits_2",
       "hgrn_out_norm_2", "hgrn_w_o_2", "ffn_w_in_2", "ffn_w_down_2", "ln_mix_g_2", "ln_mix_b_2", "ln_ffn_g_2",
       "ln_ffn_b_2", "ple_w_proj_2", "ple_w_gate_2"]


def kernel(**inputs):
    import concourse.bacc as bacc
    from concourse.bass_utils import run_bass_kernel_spmd as run

    nc = bacc.Bacc("TRN2", target_bir_lowering=False, num_devices=1)
    arrays, t = {}, {}
    for name in INS:
        a = np.ascontiguousarray(inputs[name])
        arrays[f"in_{name}"] = a
        t[name] = nc.dram_tensor(f"in_{name}", a.shape, mybir.dt.from_np(a.dtype), kind="ExternalInput").ap()
    out = nc.dram_tensor("out", (1, SEQ, D), F32, kind="ExternalOutput").ap()
    build(nc, t, out)
    r = run(nc, [arrays], core_ids=[0])
    return r.results[0]["out"]
```
